# Optimizing a Trainium2 kernel written in Bass

```python
import math
import jax, jax.numpy as jnp
from jax import lax
import numpy as np

D_MODEL = 1024
BATCH = 1
SEQ = 256
DEPTH = 2

CHUNK = 64
D_MIX = D_MODEL
D_POOL = D_MIX // 2
POOL_WINDOWS = (2, 4, 8, 16)
N_POOL_GROUPS = len(POOL_WINDOWS)
POOL_GROUP = D_POOL // N_POOL_GROUPS
D_MLSTM = D_MIX - D_POOL
N_MLSTM_HEADS = 4
MLSTM_HEAD_DIM = D_MLSTM // N_MLSTM_HEADS
CONV_WIDTH = 4
D_IN = D_POOL + 4 * D_MLSTM + 2 * N_MLSTM_HEADS
D_FF_DENSE = ((8 * D_MODEL // 3 + 127) // 128) * 128
N_EXPERTS = 8
TOP_K = 2
D_FF_EXPERT = 7 * D_MODEL // 2
N_DENSE_LAYERS = (DEPTH + 1) // 2
N_MOE_LAYERS = DEPTH // 2
ALPHA = (2 * DEPTH) ** 0.25
BETA = (8 * DEPTH) ** -0.25
LN_EPS = 1e-5

kernel_name = "hybrid_pool_mlstm_moe_deepnorm"

def layer_norm(x, g, b):
    xf = x.astype(jnp.float32)
    mu = jnp.mean(xf, axis=-1, keepdims=True)
    xc = xf - mu
    var = jnp.mean(xc * xc, axis=-1, keepdims=True)
    return (xc * lax.rsqrt(var + LN_EPS) * g.astype(jnp.float32) + b.astype(jnp.float32)).astype(x.dtype)

def pool_mixer(u, w_maps, scale):
    bsz, s, _ = u.shape
    uf = u.astype(jnp.float32)
    P = jnp.concatenate([jnp.zeros_like(uf[:, :1]), jnp.cumsum(uf, axis=1)], axis=1)
    t = jnp.arange(s)
    outs = []
    for g, w in enumerate(POOL_WINDOWS):
        sl = slice(g * POOL_GROUP, (g + 1) * POOL_GROUP)
        Pg = P[:, :, sl]
        lead = jnp.pad(Pg[:, : s + 1 - w], ((0, 0), (w - 1, 0), (0, 0)))
        count = jnp.minimum(t + 1, w).astype(jnp.float32)[None, :, None]
        outs.append((Pg[:, 1:] - lead) / count - uf[:, :, sl])
    d = jnp.stack(outs, axis=2)
    y = jnp.einsum('bsgc,gcd->bsgd', d, w_maps.astype(jnp.float32)).reshape(bsz, s, D_POOL)
    return (y * scale.astype(jnp.float32)).astype(u.dtype)

def causal_conv_silu(u, w, b):
    K = w.shape[0]
    s = u.shape[1]
    up = jnp.pad(u, ((0, 0), (K - 1, 0), (0, 0)))
    y = up[:, 0:s] * w[0]
    for j in range(1, K):
        y = y + up[:, j:j + s] * w[j]
    return jax.nn.silu(y + b)

def mlstm_chunkwise(q, k, v, i_pre, f_pre):
    bsz, s, H, Dh = q.shape
    nc, L = s // CHUNK, CHUNK

    def chunks(a):
        return a.astype(jnp.float32).reshape(bsz, nc, L, H, Dh).transpose(0, 3, 1, 2, 4)

    def chunks_g(a):
        return a.astype(jnp.float32).reshape(bsz, nc, L, H).transpose(0, 3, 1, 2)

    qc = chunks(q)
    kc = chunks(k) * (Dh ** -0.5)
    vc = chunks(v)
    ig = chunks_g(i_pre)
    logf = jax.nn.log_sigmoid(chunks_g(f_pre))
    b = jnp.cumsum(logf, axis=-1)
    g = b[..., -1]

    a = g[..., None] - b + ig
    m_loc = jnp.max(a, axis=-1)
    wa = jnp.exp(a - m_loc[..., None])
    C_loc = jnp.einsum('bhclv,bhclk->bhcvk', wa[..., None] * vc, kc)
    n_loc = jnp.einsum('bhcl,bhclk->bhck', wa, kc)

    def step(carry, inp):
        C, n, m = carry
        g_c, m_l, C_l, n_l = inp
        m_new = jnp.maximum(g_c + m, m_l)
        s_old = jnp.exp(g_c + m - m_new)
        s_loc = jnp.exp(m_l - m_new)
        C_new = s_old[..., None, None] * C + s_loc[..., None, None] * C_l
        n_new = s_old[..., None] * n + s_loc[..., None] * n_l
        return (C_new, n_new, m_new), (C, n, m)

    init = (jnp.zeros((bsz, H, Dh, Dh), jnp.float32), jnp.zeros((bsz, H, Dh), jnp.float32),
            jnp.zeros((bsz, H), jnp.float32))
    xs = (jnp.moveaxis(g, 2, 0), jnp.moveaxis(m_loc, 2, 0), jnp.moveaxis(C_loc, 2, 0), jnp.moveaxis(n_loc, 2, 0))
    _, (C_prev, n_prev, m_prev) = lax.scan(step, init, xs)
    C_prev = jnp.moveaxis(C_prev, 0, 2)
    n_prev = jnp.moveaxis(n_prev, 0, 2)
    m_prev = jnp.moveaxis(m_prev, 0, 2)

    Dlog = b[..., :, None] - b[..., None, :] + ig[..., None, :]
    causal = jnp.tril(jnp.ones((L, L), dtype=bool))
    Dlog = jnp.where(causal, Dlog, -jnp.inf)
    inter = b + m_prev[..., None]
    m_t = jnp.maximum(jnp.max(Dlog, axis=-1), inter)
    W = jnp.exp(Dlog - m_t[..., None]) * jnp.einsum('bhctk,bhcsk->bhcts', qc, kc)
    s_inter = jnp.exp(inter - m_t)
    num = jnp.einsum('bhcts,bhcsv->bhctv', W, vc) + s_inter[..., None] * jnp.einsum('bhcvk,bhctk->bhctv', C_prev, qc)
    den = jnp.sum(W, axis=-1) + s_inter * jnp.einsum('bhck,bhctk->bhct', n_prev, qc)
    h = num / jnp.maximum(jnp.abs(den), jnp.exp(-m_t))[..., None]
    return h.transpose(0, 2, 3, 1, 4).reshape(bsz, s, H, Dh)

def hybrid_mixer(x, w_in, b_gates, conv_w, conv_b, pool_w, pool_scale, mlstm_g, w_out):
    bsz, s, _ = x.shape
    H, Dh = N_MLSTM_HEADS, MLSTM_HEAD_DIM
    z = x @ w_in
    o0 = D_POOL
    u_pool = z[..., :o0]
    qk = z[..., o0:o0 + 2 * D_MLSTM]
    v = z[..., o0 + 2 * D_MLSTM:o0 + 3 * D_MLSTM]
    o_pre = z[..., o0 + 3 * D_MLSTM:o0 + 4 * D_MLSTM]
    gates = z[..., o0 + 4 * D_MLSTM:] + b_gates

    y_pool = pool_mixer(u_pool, pool_w, pool_scale)

    qk = causal_conv_silu(qk, conv_w, conv_b)
    q = qk[..., :D_MLSTM].reshape(bsz, s, H, Dh)
    k = qk[..., D_MLSTM:].reshape(bsz, s, H, Dh)
    h = mlstm_chunkwise(q, k, v.reshape(bsz, s, H, Dh), gates[..., :H], gates[..., H:])
    mu = jnp.mean(h, axis=-1, keepdims=True)
    hc = h - mu
    h = hc * lax.rsqrt(jnp.mean(hc * hc, axis=-1, keepdims=True) + LN_EPS)
    h = h.reshape(bsz, s, D_MLSTM) * mlstm_g.astype(jnp.float32)
    y_m = (jax.nn.sigmoid(o_pre.astype(jnp.float32)) * h).astype(x.dtype)

    return jnp.concatenate([y_pool, y_m], axis=-1) @ w_out

def swiglu(x, wg, wu, wd):
    return (jax.nn.silu(x @ wg) * (x @ wu)) @ wd

def moe_swiglu(x, w_router, b_router, wg, wu, wd):
    logits = (x @ w_router).astype(jnp.float32) + b_router.astype(jnp.float32)
    top_v, top_i = lax.top_k(logits, TOP_K)
    top_w = jax.nn.softmax(top_v, axis=-1)
    combine = jnp.sum(jax.nn.one_hot(top_i, N_EXPERTS, dtype=jnp.float32) * top_w[..., None], axis=-2)
    combine = combine.astype(x.dtype)
    out = jnp.zeros_like(x)
    for e in range(N_EXPERTS):
        out = out + combine[..., e:e + 1] * swiglu(x, wg[e], wu[e], wd[e])
    return out

def setup_inputs(seed: int = 0) -> dict:
    key = jax.random.key(seed)
    ks = jax.random.split(key, 24)
    f32 = jnp.float32
    H = N_MLSTM_HEADS
    nrm = lambda k, shape, scale: jax.random.normal(k, shape, f32) * scale

    x = nrm(ks[0], (BATCH, SEQ, D_MODEL), 1.0)
    w_in = nrm(ks[1], (DEPTH, D_MODEL, D_IN), D_MODEL ** -0.5)
    gate_bias0 = jnp.concatenate([jnp.zeros((H,), f32), jnp.linspace(3.0, 6.0, H, dtype=f32)])
    b_gates = gate_bias0[None, :] + nrm(ks[2], (DEPTH, 2 * H), 0.1)
    conv_w = nrm(ks[3], (DEPTH, CONV_WIDTH, 2 * D_MLSTM), CONV_WIDTH ** -0.5)
    conv_b = nrm(ks[4], (DEPTH, 2 * D_MLSTM), 0.02)
    pool_w = nrm(ks[5], (DEPTH, N_POOL_GROUPS, POOL_GROUP, POOL_GROUP), POOL_GROUP ** -0.5)
    pool_scale = 1.0 + nrm(ks[6], (DEPTH, D_POOL), 0.1)
    mlstm_g = 1.0 + nrm(ks[7], (DEPTH, D_MLSTM), 0.1)
    w_out = nrm(ks[8], (DEPTH, D_MIX, D_MODEL), BETA * D_MIX ** -0.5)
    ln1_g = 1.0 + nrm(ks[9], (DEPTH, D_MODEL), 0.05)
    ln1_b = nrm(ks[10], (DEPTH, D_MODEL), 0.02)
    ln2_g = 1.0 + nrm(ks[11], (DEPTH, D_MODEL), 0.05)
    ln2_b = nrm(ks[12], (DEPTH, D_MODEL), 0.02)
    wg_dense = nrm(ks[13], (N_DENSE_LAYERS, D_MODEL, D_FF_DENSE), D_MODEL ** -0.5)
    wu_dense = nrm(ks[14], (N_DENSE_LAYERS, D_MODEL, D_FF_DENSE), D_MODEL ** -0.5)
    wd_dense = nrm(ks[15], (N_DENSE_LAYERS, D_FF_DENSE, D_MODEL), BETA * D_FF_DENSE ** -0.5)
    w_router = nrm(ks[16], (N_MOE_LAYERS, D_MODEL, N_EXPERTS), D_MODEL ** -0.5)
    b_router = nrm(ks[17], (N_MOE_LAYERS, N_EXPERTS), 0.01)
    wg_exp = nrm(ks[18], (N_MOE_LAYERS, N_EXPERTS, D_MODEL, D_FF_EXPERT), D_MODEL ** -0.5)
    wu_exp = nrm(ks[19], (N_MOE_LAYERS, N_EXPERTS, D_MODEL, D_FF_EXPERT), D_MODEL ** -0.5)
    wd_exp = nrm(ks[20], (N_MOE_LAYERS, N_EXPERTS, D_FF_EXPERT, D_MODEL), BETA * D_FF_EXPERT ** -0.5)
    return {"x": x, "w_in": w_in, "b_gates": b_gates, "conv_w": conv_w, "conv_b": conv_b,
            "pool_w": pool_w, "pool_scale": pool_scale, "mlstm_g": mlstm_g, "w_out": w_out,
            "ln1_g": ln1_g, "ln1_b": ln1_b, "ln2_g": ln2_g, "ln2_b": ln2_b,
            "wg_dense": wg_dense, "wu_dense": wu_dense, "wd_dense": wd_dense,
            "w_router": w_router, "b_router": b_router,
            "wg_exp": wg_exp, "wu_exp": wu_exp, "wd_exp": wd_exp}

def reference(x, w_in, b_gates, conv_w, conv_b, pool_w, pool_scale, mlstm_g, w_out,
              ln1_g, ln1_b, ln2_g, ln2_b, wg_dense, wu_dense, wd_dense,
              w_router, b_router, wg_exp, wu_exp, wd_exp):
    for l in range(DEPTH):
        mix = hybrid_mixer(x, w_in[l], b_gates[l], conv_w[l], conv_b[l], pool_w[l],
                           pool_scale[l], mlstm_g[l], w_out[l])
        h = layer_norm(ALPHA * x + mix, ln1_g[l], ln1_b[l])
        j = l // 2
        if l % 2 == 0:
            f = swiglu(h, wg_dense[j], wu_dense[j], wd_dense[j])
        else:
            f = moe_swiglu(h, w_router[j], b_router[j], wg_exp[j], wu_exp[j], wd_exp[j])
        x = layer_norm(ALPHA * h + f, ln2_g[l], ln2_b[l])
    return x


_drawn_inputs = setup_inputs


def setup_inputs(seed=0):
    import zlib

    import numpy as np

    out = dict(_drawn_inputs(seed))
    spreads = {}
    factors = {'conv_b': 8.0, 'b_router': 18.616}
    for name, (base, spread) in spreads.items():
        noise = np.random.default_rng([zlib.crc32(name.encode()), seed]).standard_normal(out[name].shape)
        drawn = base * np.exp(spread * noise) if base else spread * noise
        out[name] = __import__('jax').numpy.asarray(drawn.astype(out[name].dtype))
    for name, factor in factors.items():
        out[name] = (out[name] * factor).astype(out[name].dtype)
    return out
```

```python
from contextlib import ExitStack

import numpy as np

import concourse.bass as bass
from concourse import mybir

F32 = mybir.dt.float32
I32 = mybir.dt.int32
ALU = mybir.AluOpType
ACT = mybir.ActivationFunctionType
AX_X = mybir.AxisListType.X

P = 128
T = 256
TT = T // P
D = 1024
DK = D // P
HALF = 512
LAYERS = 2
HEADS = 4
DH = 128
GROUPS = 4
TAPS = 4
PAD = TAPS - 1
D_POOL = 512
D_MLSTM = 512
GATE_COL = D_POOL + 4 * D_MLSTM
F_DENSE = 2816
F_EXP = 3584
E = 8
TOP_K = 2
FBLK = 512
DENSE_BLOCKS = -(-F_DENSE // FBLK)
EXP_BLOCKS = F_EXP // FBLK
ALPHA = (2 * LAYERS) ** 0.25
EPS = 1e-5
QK_SCALE = DH ** -0.5

CAP = 104
MAX_OVER = (TOP_K * T) // (CAP + 1)
MAX_ITEMS = E + MAX_OVER

RING = 7
SLOT = DK * FBLK
MIXER_UNITS = 7
DENSE_UNITS = 3 * DENSE_BLOCKS
ITEM_UNITS = 3 * EXP_BLOCKS
MIXER_UNIT0 = [0, MIXER_UNITS + DENSE_UNITS]
DENSE_UNIT0 = MIXER_UNITS
MOE_UNIT0 = 2 * MIXER_UNITS + DENSE_UNITS
DENSE_CHUNKS = F_DENSE // P
MIXER_CHUNKS = 16
MIXER_CHUNK0 = [0, MIXER_CHUNKS + DENSE_CHUNKS]
DENSE_CHUNK0 = MIXER_CHUNKS
assert ITEM_UNITS % RING == 0 and MAX_OVER * (CAP + 1) <= TOP_K * T

C_ID, C_TRI, C_ONES = 0, 128, 256
C_IOTA = C_ONES + T
C_LT = C_IOTA + P
C_INV = C_LT + E * E
C_CE = C_INV + GROUPS * 16
C_CT = C_CE + 2 * E
C_SEL = C_CT + 2 * E
C_END = C_SEL + HEADS * P

R_LN = {(1, "g"): 0, (1, "b"): 16, (2, "g"): 32, (2, "b"): 48}
R_CONVB, R_POOLS, R_MG, R_CONVW = 64, 80, 88, 96


def unit_pos(kind, b, blocks):
    if kind == "d":
        return 3 * b + 4 if b < blocks - 1 else 3 * blocks - 1
    return (3 * b - 1 if b else 0) + (kind == "u")


def unit_order(blocks):
    units = [(k, b) for b in range(blocks) for k in "gud"]
    return sorted(units, key=lambda kb: unit_pos(*kb, blocks))


def dense_chunks(b):
    return min(4, DENSE_CHUNKS - 4 * b)


class Steps:

    def __init__(self, eng, sem, base=0):
        self.eng, self.sem, self.base, self.n = eng, sem, base, 0

    def add(self, ins):
        ins.then_inc(self.sem, 1)
        self.n += 1

    def wait(self):
        self.eng.wait_ge(self.sem, self.base + self.n)

    def then(self, ins):
        self.add(ins)
        self.wait()


def build(nc, x, w_in, b_gates, conv_w, conv_b, pool_w, pool_scale, mlstm_g, w_out, ln1_g, ln1_b, ln2_g, ln2_b,
          wg_dense, wu_dense, wd_dense, w_router, b_router, wg_exp, wu_exp, wd_exp, consts, out):
    with ExitStack() as ctx:
        def sb(name, shape, dt=F32):
            return ctx.enter_context(nc.sbuf_tensor(name, shape, dt))

        def sem(name):
            return ctx.enter_context(nc.semaphore(name))

        ring = sb("ring", [P, RING, SLOT])
        tokens = sb("tokens", [P, TT, D])
        work = sb("work", [P, TT, D])
        xT = sb("xT", [P, DK, T])
        ln_row = sb("ln_row", [P, 2, D])
        cst = sb("cst", [P, C_END])
        par_rows = sb("par_rows", [96, P])
        par_rows2 = sb("par_rows2", [64, P])
        par = sb("par", [P, 160])
        gate_w = sb("gate_w", [P, LAYERS, DK, 64])
        gate_raw = sb("gate_raw", [P, LAYERS, DK, 2 * HEADS])
        gate_b = sb("gate_b", [P, LAYERS])
        pool_ws = sb("pool_ws", [P, LAYERS, GROUPS, DH])
        rout_w = sb("rout_w", [P, DK, E])
        rout_b = sb("rout_b", [P, E])
        small = sb("small", [P, 2])
        stats = sb("stats", [P, TT, 2, 6])
        mv = sb("mv", [P, TT, 2])
        rstd = sb("rstd", [P, TT, 2])

        arena = sb("arena", [P, 11200])
        at = [0]

        def carve(shape, start=None):
            if start is not None:
                at[0] = start
            n = int(np.prod(shape))
            v = arena[:, at[0]:at[0] + n]
            at[0] += n
            assert at[0] <= 11200
            if len(shape) == 1:
                return v
            names = "abcd"[:len(shape)]
            return v.rearrange(f"p ({' '.join(names)}) -> p {' '.join(names)}",
                               **{k: s for k, s in zip(names, shape)})

        zqk = carve([8, PAD + T], 0)
        h_norm = arena[:, 0:TT * D_MLSTM].rearrange("p (t c) -> p t c", t=TT)
        ubuf = carve([GROUPS, 16 + T])
        ptmp = carve([2, 16 + T])
        v_sb = carve([TT, D_MLSTM])
        sigT = carve([HEADS, T])
        decay = carve([HEADS, T + P])
        rows = carve([5, T])
        conv_acc = carve([2, T])
        qkT = carve([8, T])
        yT = qkT
        r_i, r_f, r_l, r_negm, r_m = (rows[0:HEADS, n, :] for n in range(5))
        cols = sb("cols", [P, 2, TT, HEADS])
        guard = sb("guard", [P, TT, HEADS])
        rden = sb("rden", [P, TT, HEADS])
        hstats = sb("hstats", [P, TT, HEADS, 6])
        hmv = sb("hmv", [P, TT, HEADS, 2])
        hstd = sb("hstd", [P, TT, HEADS])
        hrstd = sb("hrstd", [P, TT, HEADS])
        dh = carve([2, 4, T], 0)
        dsg = carve([2, T])
        xg = carve([DK, CAP], 0)
        esg = carve([2, 4 * CAP])
        eh = carve([2, 4, CAP])
        yTs = carve([DK, CAP])
        y_sb = carve([D])
        scat = carve([T])
        pick = carve([TT, CAP])
        pickc = carve([TT, CAP])
        logit = carve([TT, E])
        gt = carve([TT, E, E])
        eq = carve([TT, E, E])
        rank = carve([TT, E])
        chosen = carve([TT, E])
        top = carve([TT])
        expo = carve([TT, E])
        esum = carve([TT])
        comb = carve([TT, E])
        posm = carve([TT, E])
        count = carve([E])
        flag = carve([2 * E])
        frank = carve([2 * E])
        fsel = carve([2 * E])
        ftmp = carve([2 * E])
        over_e = carve([MAX_OVER])
        over_t = carve([MAX_OVER])
        n_over_f = carve([1])
        item_tab = carve([MAX_ITEMS + 1, 4])
        item_cur = carve([4])
        itmp = carve([TT, E])
        over_int = sb("over_int", [P, MAX_OVER + 1], I32)

        bank = [ctx.enter_context(nc.psum_tensor(f"bank{n}", [P, HALF], F32)) for n in range(8)]

        ident = cst[:, C_ID:C_ID + P]
        tri = cst[:, C_TRI:C_TRI + P]
        ones = cst[:, C_ONES:C_ONES + P]
        ones_t = cst[0:HEADS, C_ONES:C_ONES + T]
        iota = cst[:, C_IOTA:C_IOTA + CAP]
        one_col = small[:, 0:1]
        eps_col = small[:, 1:2]

        landed = [sem(f"landed{n}") for n in range(RING)]
        x_in, consts_in, par_in, gatew_in, poolw_in, router_in, ln_in, out_done = map(sem, (
            "x_in", "consts_in", "par_in", "gatew_in", "poolw_in", "router_in", "ln_in", "out_done"))
        par_turned, turned, gates_mm, chunk_done, v_done, cols_mm, bcast_mm, score_mm, pooly_mm, pv_mm, ht_mm, \
            wo_done, down_done, logit_mm, pos_mm, unit_done, gather_mm, yt_mm, scat_mm, st_mm = map(sem, (
                "par_turned", "turned", "gates_mm", "chunk_done", "v_done", "cols_mm", "bcast_mm", "score_mm",
                "pooly_mm", "pv_mm", "ht_mm", "wo_done", "down_done", "logit_mm", "pos_mm", "unit_done",
                "gather_mm", "yt_mm", "scat_mm", "st_mm"))
        act_turn, gate_i, gate_e, gate_l, zqk_ready, qk_ready, u_ready, sig_ready, decay_ready, guard_ready, \
            hstd_ready, std_ready, dsilu, esilu, expo_ready, yts_ready, ysb_ready = map(sem, (
                "act_turn", "gate_i", "gate_e", "gate_l", "zqk_ready", "qk_ready", "u_ready", "sig_ready",
                "decay_ready", "guard_ready", "hstd_ready", "std_ready", "dsilu", "esilu", "expo_ready",
                "yts_ready", "ysb_ready"))
        par_ready, dve_turn, absf_ready, rows_ready, conv_ready, v_ready, cols_ready, arg_ready, w_ready, \
            ypool_ready, hvar_ready, h_ready, ym_ready, var_ready, xhat_ready, dh_ready, logit_ready, \
            chosen_ready, table_ready, eh_ready, xg_ready, scat_ready, acc_done, out_ready, steps, \
            build_steps = map(sem, (
                "par_ready", "dve_turn", "absf_ready", "rows_ready", "conv_ready", "v_ready", "cols_ready",
                "arg_ready", "w_ready", "ypool_ready", "hvar_ready", "h_ready", "ym_ready", "var_ready",
                "xhat_ready", "dh_ready", "logit_ready", "chosen_ready", "table_ready", "eh_ready", "xg_ready",
                "scat_ready", "acc_done", "out_ready", "steps", "build_steps"))
        small_ready, gatew_zero, gatew_ready, pool_steps, pool_ready, mask_ready, tokens_ready = map(sem, (
            "small_ready", "gatew_zero", "gatew_ready", "pool_steps", "pool_ready", "mask_ready", "tokens_ready"))

        x_d = x.rearrange("b (t p) d -> p (b t) d", p=P)
        out_d = out.rearrange("b (t p) d -> p (b t) d", p=P)

        def par_col(name, layer, k):
            if name in R_LN:
                c = R_LN[name] + DK * layer + k
            elif name == "conv_b":
                c = R_CONVB + 8 * layer + k
            elif name == "pool_scale":
                c = R_POOLS + 4 * layer + k
            elif name == "mlstm_g":
                c = R_MG + 4 * layer + k
            else:
                c = R_CONVW + (layer * TAPS + name[1]) * 8 + k
            return par[:, c:c + 1]

        SUM_BANKS = [(0, 1), (4, 5)]
        TURN_BANKS = [(2, 3), (6, 7)]
        NORM = {1: (1, 0), 2: (2, 0), 3: (1, 1), 4: (2, 1)}

        def rows_of(w, r0, n):
            return w[r0:r0 + n * P, :].rearrange("(k p) n -> p k n", p=P)

        def mixer_sources(l):
            def cols_of(c0):
                return w_in[l].rearrange("(k p) n -> p k n", p=P)[:, :, c0:c0 + FBLK]
            return [cols_of(D_POOL), cols_of(D_POOL + D_MLSTM), cols_of(D_POOL + 2 * D_MLSTM), cols_of(0),
                    cols_of(D_POOL + 3 * D_MLSTM), rows_of(w_out[l], 0, 4), rows_of(w_out[l], HALF, 4)]

        def dense_source(kind, b):
            n = dense_chunks(b)
            if kind == "d":
                return rows_of(wd_dense[0], b * FBLK, n)
            w = wg_dense if kind == "g" else wu_dense
            return w[0].rearrange("(k p) n -> p k n", p=P)[:, :, b * FBLK:b * FBLK + n * P]

        def expert_source(kind, b, e):
            if kind == "d":
                return wd_exp[0, e].rearrange("(j p) n -> p j n", p=P)[:, 4 * b:4 * b + 4, :]
            w = wg_exp if kind == "g" else wu_exp
            return w[0, e].rearrange("(k p) n -> p k n", p=P)[:, :, b * FBLK:(b + 1) * FBLK]

        def slot_cols(n, cols_):
            return ring[:, n % RING, :].rearrange("p (k n) -> p k n", n=cols_)

        block = ctx.enter_context(nc.Block())

        @block.sync
        def _(sp):
            def freed(n):
                for l in range(LAYERS):
                    u = n - MIXER_UNIT0[l]
                    if 0 <= u < MIXER_UNITS:
                        s, v = [(chunk_done, MIXER_CHUNK0[l] + 4), (chunk_done, MIXER_CHUNK0[l] + 8),
                                (v_done, TT * (l + 1)), (chunk_done, MIXER_CHUNK0[l] + 12),
                                (chunk_done, MIXER_CHUNK0[l] + 16), (wo_done, 3 * l + 1), (wo_done, 3 * l + 3)][u]
                        sp.wait_ge(s, v)
                        return
                kind, b = unit_order(DENSE_BLOCKS)[n - DENSE_UNIT0]
                if kind == "g":
                    sp.wait_ge(chunk_done, DENSE_CHUNK0 + 4 * b + 1)
                elif kind == "u":
                    sp.wait_ge(chunk_done, DENSE_CHUNK0 + 4 * b + dense_chunks(b))
                else:
                    sp.wait_ge(down_done, b + 1 if b < DENSE_BLOCKS - 1 else DENSE_BLOCKS + 1)

            def load(n, src):
                if n >= RING:
                    freed(n - RING)
                k, c = src.shape[1], src.shape[2]
                sp.dma_start(slot_cols(n, c)[:, 0:k, :], src).then_inc(landed[n % RING], 16)

            sp.dma_start(tokens[:, 0, :], x_d[:, 0, :]).then_inc(x_in, 16)
            sp.dma_start(tokens[:, 1, :], x_d[:, 1, :]).then_inc(x_in, 16)
            n = 0
            for src in mixer_sources(0):
                load(n, src)
                n += 1
            for kind, b in unit_order(DENSE_BLOCKS):
                load(n, dense_source(kind, b))
                n += 1
            for src in mixer_sources(1):
                load(n, src)
                n += 1

            def item_loads(i, e, first=False):
                for u, (kind, b) in enumerate(unit_order(EXP_BLOCKS)):
                    if first and u < RING:
                        freed(MOE_UNIT0 + u - RING)
                    else:
                        sp.wait_ge(unit_done, ITEM_UNITS * i + u - RING + 1)
                    m = MOE_UNIT0 + u
                    dst = slot_cols(m, D if kind == "d" else FBLK)
                    sp.dma_start(dst, expert_source(kind, b, e)).then_inc(landed[m % RING], 16)

            item_loads(0, 0, first=True)
            with sp.Fori(1, E) as i:
                item_loads(i, i)
            sp.wait_ge(table_ready, 1)
            n_over = sp.value_load(over_int[0:1, MAX_OVER:MAX_OVER + 1], min_val=0, max_val=MAX_OVER)
            with sp.Fori(0, MAX_OVER) as j:
                with sp.If(j < n_over):
                    e = sp.value_load(over_int[0:1, bass.ds(j, 1)], min_val=0, max_val=E - 1)
                    item_loads(j + E, e)
            for t in range(TT):
                sp.wait_ge(out_ready, t + 1)
                sp.dma_start(out_d[:, t, :], tokens[:, t, :]).then_inc(out_done, 16)
            sp.wait_ge(out_done, 16 * TT)

        @block.gpsimd
        def _(pool):
            g = nc.gpsimd
            g.memset(small[:, 0:1], 1.0).then_inc(small_ready, 1)
            g.memset(small[:, 1:2], EPS).then_inc(small_ready, 1)
            g.memset(gate_w[:], 0.0).then_inc(gatew_zero, 1)
            for l in range(LAYERS):
                pool.dma_start(gate_raw[:, l, :, :],
                               w_in[l, :, GATE_COL:GATE_COL + 2 * HEADS].rearrange("(k p) h -> p k h", p=P)
                               ).then_inc(gatew_in, 16)
                for r, c in ((0, 0), (32, HEADS)):
                    pool.dma_start(gate_b[r:r + HEADS, l:l + 1],
                                   b_gates[l, c:c + HEADS].rearrange("(h a) -> h a", a=1)).then_inc(gatew_in, 16)
            pool.wait_ge(gatew_in, 16 * 3 * LAYERS)
            pool.wait_ge(gatew_zero, 1)
            g.tensor_copy(gate_w[:, :, :, 0:HEADS].rearrange("p l k h -> p (l k) h"),
                          gate_raw[:, :, :, 0:HEADS].rearrange("p l k h -> p (l k) h")).then_inc(gatew_ready, 1)
            g.tensor_copy(gate_w[:, :, :, 32:32 + HEADS].rearrange("p l k h -> p (l k) h"),
                          gate_raw[:, :, :, HEADS:].rearrange("p l k h -> p (l k) h")).then_inc(gatew_ready, 1)

            def load_ln(s):
                norm, l = NORM[s]
                for n, w in enumerate(((ln1_g, ln1_b), (ln2_g, ln2_b))[norm - 1]):
                    pool.dma_start(ln_row[:, n, :], w[l:l + 1, :].partition_broadcast(P)
                                   .rearrange("p a d -> p (a d)")).then_inc(ln_in, 16)

            load_ln(1)
            pool.dma_start(pool_ws[:], pool_w.rearrange("l g c d -> c l g d")).then_inc(poolw_in, 16)
            pool.dma_start(rout_w[:], w_router[0].rearrange("(k p) e -> p k e", p=P)).then_inc(router_in, 16)
            pool.dma_start(rout_b[:], b_router[0:1, :].partition_broadcast(P)
                           .rearrange("p a e -> p (a e)")).then_inc(router_in, 16)

            st = Steps(pool, pool_steps)

            def pooling(l):
                if l:
                    pool.wait_ge(tokens_ready, TT * 2)
                    pool.wait_ge(chunk_done, MIXER_CHUNK0[l] + 1)
                st.then(g.memset(ptmp[:, :, 0:16], 0.0))
                for gr in range(GROUPS):
                    pool.wait_ge(u_ready, GROUPS * l + gr + 1)
                    st.then(g.memset(ubuf[:, gr, 0:16], 0.0))
                    u = ubuf[:, gr, :]
                    src = u
                    for step in range(gr + 1):
                        sh = 1 << step
                        dst = ptmp[:, step % 2, :]
                        st.then(g.tensor_tensor(dst[:, 16:], src[:, 16:], src[:, 16 - sh:16 + T - sh], ALU.add))
                        src = dst
                    st.add(g.tensor_tensor(src[:, 16:32], src[:, 16:32], cst[:, C_INV + 16 * gr:C_INV + 16 * gr + 16],
                                           ALU.mult))
                    st.then(g.tensor_scalar(src[:, 32:], src[:, 32:], 1.0 / (2 << gr), None, ALU.mult))
                    g.tensor_tensor(u[:, 16:], src[:, 16:], u[:, 16:], ALU.subtract).then_inc(pool_ready, 1)
                    pool.wait_ge(pool_ready, GROUPS * l + gr + 1)

            def masks(l):
                pool.wait_ge(decay_ready, HEADS * (l + 1))
                for c in (0, T):
                    blk = decay[:, :, c:c + P]
                    g.affine_select(out=blk, in_=blk, compare_op=ALU.is_ge, fill=0.0, base=0,
                                    pattern=[[0, HEADS], [1, P]], channel_multiplier=-1).then_inc(mask_ready, 1)

            def token_rows(s):
                pool.wait_ge(ln_in, 32 * s)
                for t in range(TT):
                    pool.wait_ge(xhat_ready, TT * (s - 1) + t + 1)
                    st.then(g.tensor_tensor(tokens[:, t, :], work[:, t, :], ln_row[:, 0, :], ALU.mult))
                    g.tensor_tensor(tokens[:, t, :], tokens[:, t, :], ln_row[:, 1, :], ALU.add) \
                        .then_inc(tokens_ready, 1)
                pool.wait_ge(tokens_ready, TT * s)
                load_ln(s + 1)

            pool.wait_ge(consts_in, 16)
            for l in range(LAYERS):
                masks(l)
                pooling(l)
                token_rows(2 * l + 1)
                if l + 1 < LAYERS:
                    token_rows(2 * l + 2)

        @block.scalar
        def _(act):
            a = nc.scalar
            act.dma_start(cst[:], consts).then_inc(consts_in, 16)
            for (norm, kind), w in (((1, "g"), ln1_g), ((1, "b"), ln1_b), ((2, "g"), ln2_g), ((2, "b"), ln2_b)):
                r = R_LN[(norm, kind)]
                act.dma_start(par_rows[r:r + 16, :], w.rearrange("l (k p) -> (l k) p", p=P)).then_inc(par_in, 16)
            for r, n, w in ((R_CONVB, 16, conv_b), (R_POOLS, 8, pool_scale), (R_MG, 8, mlstm_g)):
                act.dma_start(par_rows[r:r + n, :], w.rearrange("l (k p) -> (l k) p", p=P)).then_inc(par_in, 16)
            act.dma_start(par_rows2[:], conv_w.rearrange("l j (k p) -> (l j k) p", p=P)).then_inc(par_in, 16)

            def turn(s):
                for t in range(TT):
                    act.wait_ge(turned, 2 * (TT * s + t) + 1)
                    if s == 1 and t == 0:
                        act.wait_ge(par_ready, 2)
                    for k in range(DK // 2):
                        src = bank[TURN_BANKS[t][k // 4]][:, (k % 4) * P:(k % 4 + 1) * P]
                        dst = xT[:, k, t * P:(t + 1) * P]
                        if s == 0:
                            a.copy(dst, src).then_inc(act_turn, 1)
                        else:
                            norm, l = NORM[s]
                            a.activation(dst, src, ACT.Identity, bias=par_col((norm, "b"), l, k),
                                         scale=par_col((norm, "g"), l, k)).then_inc(act_turn, 1)

            def mixer(l):
                act.wait_ge(absf_ready, l + 1)
                a.activation(r_i, bank[6][0:HEADS, 0:T], ACT.Identity, bias=gate_b[0:HEADS, l:l + 1]) \
                    .then_inc(gate_i, 1)
                a.activation(r_l, r_l, ACT.Exp, scale=-1.0).then_inc(gate_e, 1)
                act.wait_ge(gate_e, l + 1)
                act.wait_ge(small_ready, 2)
                a.activation(r_l, r_l, ACT.Ln, bias=small[0:HEADS, 0:1]).then_inc(gate_l, 1)

                def silu(c):
                    act.wait_ge(conv_ready, 8 * l + c + 1)
                    a.activation(qkT[:, c, :], conv_acc[:, c % 2, :], ACT.Silu, bias=par_col("conv_b", l, c)) \
                        .then_inc(qk_ready, 1)

                for c in range(8):
                    act.wait_ge(chunk_done, MIXER_CHUNK0[l] + c + 1)
                    a.copy(zqk[:, c, PAD:], bank[c % 4][:, 0:T]).then_inc(zqk_ready, 1)
                    if c >= 1:
                        silu(c - 1)
                silu(7)
                for h in range(HEADS):
                    act.wait_ge(arg_ready, HEADS * l + h + 1)
                    a.activation(decay[:, h, :], decay[:, h, :], ACT.Exp).then_inc(decay_ready, 1)
                act.wait_ge(cols_ready, l + 1)
                a.activation(guard[:].rearrange("p t h -> p (t h)"), cols[:, 1].rearrange("p t h -> p (t h)"),
                             ACT.Exp, scale=-1.0).then_inc(guard_ready, 1)
                for c in range(GROUPS):
                    act.wait_ge(chunk_done, MIXER_CHUNK0[l] + 8 + c + 1)
                    a.copy(ubuf[:, c, 16:], bank[c][:, 0:T]).then_inc(u_ready, 1)
                for c in range(HEADS):
                    act.wait_ge(chunk_done, MIXER_CHUNK0[l] + 12 + c + 1)
                    a.activation(sigT[:, c, :], bank[(5, 6, 7, 4)[c]][:, 0:T], ACT.Sigmoid).then_inc(sig_ready, 1)
                for t in range(TT):
                    act.wait_ge(hvar_ready, TT * l + t + 1)
                    a.activation(hstd[:, t, :], hmv[:, t, :, 1], ACT.Sqrt, bias=eps_col).then_inc(hstd_ready, 1)

            def norm_std(s):
                for t in range(TT):
                    act.wait_ge(var_ready, TT * (s - 1) + t + 1)
                    a.activation(rstd[:, t, 0:1], mv[:, t, 1:2], ACT.Sqrt, bias=eps_col).then_inc(std_ready, 1)

            turn(0)
            for l in range(LAYERS):
                mixer(l)
                norm_std(2 * l + 1)
                turn(2 * l + 1)
                if l == 0:
                    for c in range(DENSE_CHUNKS):
                        act.wait_ge(chunk_done, DENSE_CHUNK0 + c + 1)
                        if c >= 2:
                            act.wait_ge(dh_ready, c - 1)
                        a.activation(dsg[:, c % 2, :], bank[(2, 3, 6, 7)[c % 4]][:, 0:T], ACT.Silu).then_inc(dsilu, 1)
                    norm_std(2)
                    turn(2)
            act.wait_ge(logit_ready, 1)
            for t in range(TT):
                a.activation(expo[:, t, :], logit[:, t, :], ACT.Exp, bias=top[:, t:t + 1]).then_inc(expo_ready, 1)

            def y_turn(i):
                for n in range(2):
                    act.wait_ge(yt_mm, 2 * i + n + 1)
                    a.copy(y_sb[0:CAP, n * HALF:(n + 1) * HALF], bank[4 + n][0:CAP, :]).then_inc(ysb_ready, 1)

            def item(i, first=False):
                for b in range(EXP_BLOCKS):
                    act.wait_ge(unit_done, ITEM_UNITS * i + unit_pos("g", b, EXP_BLOCKS) + 1)
                    a.activation(esg[:, b % 2, :], bank[(2, 6)[b % 2]][:, 0:4 * CAP], ACT.Silu).then_inc(esilu, 1)
                    if b == 0 and not first:
                        y_turn(i - 1)
                act.wait_ge(unit_done, ITEM_UNITS * (i + 1))
                for n in range(2):
                    a.copy(yTs[:, 4 * n:4 * n + 4, :].rearrange("p k c -> p (k c)"), bank[n][:, 0:4 * CAP]) \
                        .then_inc(yts_ready, 1)

            item(0, first=True)
            with act.Fori(1, E) as i:
                item(i)
            n_over = act.value_load(over_int[0:1, MAX_OVER:MAX_OVER + 1], min_val=0, max_val=MAX_OVER)
            with act.Fori(0, MAX_OVER) as j:
                with act.If(j < n_over):
                    item(j + E)
            y_turn(n_over + (E - 1))
            norm_std(4)

        @block.vector
        def _(dve):
            v = nc.vector
            st = Steps(dve, steps)

            for n, (r, c) in enumerate(((96, 0), (64, 96))):
                dve.wait_ge(par_turned, n + 1)
                v.tensor_copy(par[:, c:c + r], bank[n][:, 0:r]).then_inc(par_ready, 1)

            def turn(s):
                for t in range(TT):
                    dve.wait_ge(turned, 2 * (TT * s + t) + 2)
                    if s == 1 and t == 0:
                        dve.wait_ge(par_ready, 2)
                    for k in range(DK // 2, DK):
                        src = bank[TURN_BANKS[t][k // 4]][:, (k % 4) * P:(k % 4 + 1) * P]
                        dst = xT[:, k, t * P:(t + 1) * P]
                        if s == 0:
                            v.tensor_copy(dst, src).then_inc(dve_turn, 1)
                        else:
                            norm, l = NORM[s]
                            v.tensor_scalar(dst, src, par_col((norm, "g"), l, k), par_col((norm, "b"), l, k),
                                            ALU.mult, ALU.add).then_inc(dve_turn, 1)

            def mixer(l):
                dve.wait_ge(gates_mm, l + 1)
                dve.wait_ge(gatew_in, 16 * 3 * LAYERS)
                st.add(v.memset(zqk[:, :, 0:PAD], 0.0))
                st.then(v.tensor_scalar(r_f, bank[6][32:32 + HEADS, 0:T], gate_b[32:32 + HEADS, l:l + 1], None,
                                        ALU.add))
                v.scalar_tensor_tensor(out=r_l, in0=r_f, scalar=-1.0, in1=r_f, op0=ALU.mult, op1=ALU.max) \
                    .then_inc(absf_ready, 1)
                dve.wait_ge(gate_l, l + 1)
                st.then(v.scalar_tensor_tensor(out=r_f, in0=r_f, scalar=0.0, in1=r_l, op0=ALU.min,
                                               op1=ALU.subtract))
                st.then(v.tensor_tensor_scan(r_l, ones_t, r_f, 0.0, ALU.mult, ALU.add))
                dve.wait_ge(gate_i, l + 1)
                st.then(v.tensor_tensor(r_i, r_i, r_l, ALU.subtract))
                st.then(v.tensor_tensor_scan(r_m, ones_t, r_i, 0.0, ALU.mult, ALU.max))
                st.add(v.tensor_scalar(r_negm, r_m, -1.0, None, ALU.mult))
                st.wait()
                v.tensor_tensor(r_m, r_m, r_l, ALU.add).then_inc(rows_ready, 1)

                for c in range(8):
                    dve.wait_ge(zqk_ready, 8 * l + c + 1)
                    if c >= 2:
                        dve.wait_ge(qk_ready, 8 * l + c - 1)
                    acc = conv_acc[:, c % 2, :]
                    st.then(v.tensor_scalar(acc, zqk[:, c, 0:T], par_col(("conv_w", 0), l, c), None, ALU.mult))
                    for j in range(1, TAPS):
                        ins = v.scalar_tensor_tensor(out=acc, in0=zqk[:, c, j:j + T],
                                                     scalar=par_col(("conv_w", j), l, c), in1=acc,
                                                     op0=ALU.mult, op1=ALU.add)
                        if j < TAPS - 1:
                            st.then(ins)
                        else:
                            ins.then_inc(conv_ready, 1)
                for t in range(TT):
                    dve.wait_ge(v_done, TT * l + t + 1)
                    v.tensor_copy(v_sb[:, t, :], bank[4 + t][:, :]).then_inc(v_ready, 1)

                dve.wait_ge(cols_mm, l + 1)
                v.tensor_copy(cols[:].rearrange("p a t h -> p (a t h)"), bank[6][:, 0:4 * HEADS]) \
                    .then_inc(cols_ready, 1)
                dve.wait_ge(cols_ready, l + 1)
                for h in range(HEADS):
                    dve.wait_ge(bcast_mm, 2 * l + h // 2 + 1)
                    m = bank[(7, 4)[h // 2]][:, (h % 2) * T:(h % 2 + 1) * T]
                    st.add(v.tensor_scalar(decay[:, h, 0:T], m, cols[:, 0, 0, h:h + 1], 0.0, ALU.add, ALU.min))
                    v.tensor_scalar(decay[:, h, T:T + P], m[:, P:T], cols[:, 0, 1, h:h + 1], 0.0, ALU.add,
                                    ALU.min).then_inc(arg_ready, 1)
                dve.wait_ge(mask_ready, 2 * (l + 1))
                for h in range(HEADS):
                    dve.wait_ge(score_mm, HEADS * l + h + 1)
                    v.scalar_tensor_tensor(out=decay[:, h, :], in0=bank[h][:, 0:T + P], scalar=QK_SCALE,
                                           in1=decay[:, h, :], op0=ALU.mult, op1=ALU.mult).then_inc(w_ready, 1)
                for gr in range(GROUPS):
                    dve.wait_ge(pooly_mm, 2 * l + gr // 2 + 1)
                    v.tensor_scalar(yT[:, gr, :], bank[gr // 2][:, (gr % 2) * T:(gr % 2 + 1) * T],
                                    par_col("pool_scale", l, gr), None, ALU.mult).then_inc(ypool_ready, 1)
                dve.wait_ge(guard_ready, l + 1)
                for t in range(TT):
                    dve.wait_ge(pv_mm, TT * l + t + 1)
                    den = bank[6][:, t * HEADS:(t + 1) * HEADS]
                    st.then(v.tensor_tensor(rden[:, t, :], den, guard[:, t, :], ALU.max))
                    st.then(v.scalar_tensor_tensor(out=rden[:, t, :], in0=den, scalar=-1.0, in1=rden[:, t, :],
                                                   op0=ALU.mult, op1=ALU.max))
                    st.then(v.reciprocal(rden[:, t, :], rden[:, t, :]))
                    for h in range(HEADS):
                        st.add(v.tensor_scalar(h_norm[:, t, h * DH:(h + 1) * DH], bank[2 + t][:, h * DH:(h + 1) * DH],
                                               rden[:, t, h:h + 1], None, ALU.mult))
                    st.wait()
                    for h in range(HEADS):
                        st.add(v.bn_stats(hstats[:, t, h, :], h_norm[:, t, h * DH:(h + 1) * DH]))
                    st.wait()
                    for h in range(HEADS):
                        ins = v.bn_aggr(hmv[:, t, h, :], hstats[:, t, h, :])
                        if h < HEADS - 1:
                            st.add(ins)
                        else:
                            ins.then_inc(hvar_ready, 1)
                for t in range(TT):
                    dve.wait_ge(hstd_ready, TT * l + t + 1)
                    dve.wait_ge(hvar_ready, TT * l + t + 1)
                    st.then(v.reciprocal(hrstd[:, t, :], hstd[:, t, :]))
                    for h in range(HEADS):
                        v.tensor_scalar(h_norm[:, t, h * DH:(h + 1) * DH], h_norm[:, t, h * DH:(h + 1) * DH],
                                        hmv[:, t, h, 0:1], hrstd[:, t, h:h + 1], ALU.subtract, ALU.mult) \
                            .then_inc(h_ready, 1)
                dve.wait_ge(sig_ready, HEADS * (l + 1))
                for t in range(TT):
                    dve.wait_ge(ht_mm, TT * l + t + 1)
                    for h in range(HEADS):
                        v.scalar_tensor_tensor(out=yT[:, GROUPS + h, t * P:(t + 1) * P],
                                               in0=bank[(7, 6)[t]][:, h * P:(h + 1) * P],
                                               scalar=par_col("mlstm_g", l, h),
                                               in1=sigT[:, h, t * P:(t + 1) * P],
                                               op0=ALU.mult, op1=ALU.mult).then_inc(ym_ready, 1)

            def residual(s, t):
                if s > 1:
                    dve.wait_ge(tokens_ready, TT * (s - 1))
                for n in range(2):
                    st.add(v.scalar_tensor_tensor(out=work[:, t, n * HALF:(n + 1) * HALF],
                                                  in0=tokens[:, t, n * HALF:(n + 1) * HALF], scalar=ALPHA,
                                                  in1=bank[SUM_BANKS[t][n]][:, :], op0=ALU.mult, op1=ALU.add))
                st.wait()

            def normalise(s, t):
                for n in range(2):
                    st.add(v.bn_stats(stats[:, t, n, :], work[:, t, n * HALF:(n + 1) * HALF]))
                st.wait()
                v.bn_aggr(mv[:, t, :], stats[:, t].rearrange("p a b -> p (a b)")).then_inc(var_ready, 1)
                dve.wait_ge(std_ready, TT * (s - 1) + t + 1)
                dve.wait_ge(var_ready, TT * (s - 1) + t + 1)
                st.then(v.reciprocal(rstd[:, t, 1:2], rstd[:, t, 0:1]))
                v.tensor_scalar(work[:, t, :], work[:, t, :], mv[:, t, 0:1], rstd[:, t, 1:2],
                                ALU.subtract, ALU.mult).then_inc(xhat_ready, 1)

            turn(0)
            for l in range(LAYERS):
                mixer(l)
                for t in range(TT):
                    dve.wait_ge(wo_done, 3 * l + 2 + t)
                    residual(2 * l + 1, t)
                    normalise(2 * l + 1, t)
                turn(2 * l + 1)
                if l == 0:
                    for c in range(DENSE_CHUNKS):
                        dve.wait_ge(dsilu, c + 1)
                        v.tensor_tensor(dh[:, c // 4 % 2, c % 4, :], dsg[:, c % 2, :],
                                        bank[(2, 3, 6, 7)[c % 4]][:, T:2 * T], ALU.mult).then_inc(dh_ready, 1)
                    for t in range(TT):
                        dve.wait_ge(down_done, DENSE_BLOCKS + t)
                        residual(2, t)
                        normalise(2, t)
                    turn(2)

            dve.wait_ge(logit_mm, 1)
            dve.wait_ge(router_in, 32)
            for t in range(TT):
                st.add(v.tensor_tensor(logit[:, t, :], bank[4][:, t * E:(t + 1) * E], rout_b[:], ALU.add))
            st.wait()
            st.then(v.tensor_reduce(top, logit, AX_X, ALU.max))
            v.tensor_scalar(top, top, -1.0, None, ALU.mult).then_inc(logit_ready, 1)
            for t in range(TT):
                lj = logit[:, t, :].unsqueeze(1).to_broadcast([P, E, E])
                le = logit[:, t, :].unsqueeze(2).to_broadcast([P, E, E])
                st.add(v.tensor_tensor(gt[:, t], lj, le, ALU.is_gt))
                st.add(v.tensor_tensor(eq[:, t], lj, le, ALU.is_equal))
            st.wait()
            lt = cst[:, C_LT:C_LT + E * E].rearrange("p (e j) -> p e j", e=E)
            for t in range(TT):
                st.add(v.tensor_tensor(eq[:, t], eq[:, t], lt, ALU.mult))
            st.wait()
            st.then(v.tensor_tensor(gt.rearrange("p t e j -> p (t e j)"), gt.rearrange("p t e j -> p (t e j)"),
                                    eq.rearrange("p t e j -> p (t e j)"), ALU.add))
            st.then(v.tensor_reduce(rank.rearrange("p t e -> p (t e)"), gt.rearrange("p t e j -> p (t e) j"),
                                    AX_X, ALU.add))
            v.tensor_scalar(chosen.rearrange("p t e -> p (t e)"), rank.rearrange("p t e -> p (t e)"),
                            TOP_K - 0.5, None, ALU.is_lt).then_inc(chosen_ready, 1)
            dve.wait_ge(chosen_ready, 1)
            dve.wait_ge(expo_ready, 2)
            st.then(v.tensor_tensor(comb, expo, chosen, ALU.mult))
            st.then(v.tensor_reduce(esum, comb, AX_X, ALU.add))
            st.then(v.reciprocal(esum, esum))
            for t in range(TT):
                st.add(v.tensor_scalar(comb[:, t, :], comb[:, t, :], esum[:, t:t + 1], None, ALU.mult))
            dve.wait_ge(pos_mm, 1)
            st.add(v.tensor_copy(count, bank[4][:, 4 * E:5 * E]))
            st.then(v.scalar_tensor_tensor(out=posm.rearrange("p t e -> p (t e)"), in0=bank[4][:, 2 * E:4 * E],
                                           scalar=1.0, in1=chosen.rearrange("p t e -> p (t e)"),
                                           op0=ALU.add, op1=ALU.mult))
            st.then(v.tensor_scalar(posm, posm, -1.0, None, ALU.add))
            st.add(v.tensor_scalar(flag[:, 0:E], count, CAP + 0.5, None, ALU.is_gt))
            st.then(v.tensor_scalar(flag[:, E:], count, 2 * CAP + 0.5, None, ALU.is_gt))
            st.add(v.tensor_reduce(n_over_f, flag, AX_X, ALU.add))
            st.then(v.tensor_tensor_scan(frank, cst[:, C_ONES:C_ONES + 2 * E], flag, 0.0, ALU.mult, ALU.add))
            for j in range(MAX_OVER):
                st.then(v.scalar_tensor_tensor(out=fsel, in0=frank, scalar=float(j + 1), in1=flag,
                                               op0=ALU.is_equal, op1=ALU.mult))
                for col, o in ((C_CE, over_e), (C_CT, over_t)):
                    st.then(v.tensor_tensor(ftmp, fsel, cst[:, col:col + 2 * E], ALU.mult))
                    st.then(v.tensor_reduce(o[:, j:j + 1], ftmp, AX_X, ALU.add))
            st.add(v.tensor_copy(over_int[:, 0:MAX_OVER], over_e))
            v.tensor_copy(over_int[:, MAX_OVER:], n_over_f).then_inc(table_ready, 1)
            for t in range(TT):
                st.add(v.tensor_copy(item_tab[:, 0:E, t], posm[:, t, :]))
                st.add(v.tensor_copy(item_tab[:, 0:E, 2 + t], comb[:, t, :]))
            st.add(v.memset(item_tab[:, MAX_ITEMS, :], -1.0))
            st.wait()
            for j in range(MAX_OVER):
                st.then(v.tensor_scalar(fsel[:, 0:E], cst[:, C_CE:C_CE + E], over_e[:, j:j + 1], None, ALU.is_equal))
                for src, c in ((posm, 0), (comb, 2)):
                    for t in range(TT):
                        st.then(v.tensor_tensor(itmp[:, t, :], src[:, t, :], fsel[:, 0:E], ALU.mult))
                    st.then(v.tensor_reduce(item_tab[:, E + j, c:c + 2], itmp, AX_X, ALU.add))
                st.then(v.tensor_scalar(item_tab[:, E + j, 0:2], item_tab[:, E + j, 0:2], over_t[:, j:j + 1], None,
                                        ALU.subtract))
            dve.wait_ge(tokens_ready, TT * 3)
            st.then(v.tensor_scalar(work[:, :, :], tokens[:, :, :], ALPHA, None, ALU.mult))

            BUILD_STEPS = 5

            def build_pick(i):
                bs = Steps(dve, build_steps, BUILD_STEPS * i)
                bs.then(v.tensor_copy(item_cur.unsqueeze(1), item_tab[:, bass.ds(i, 1), :]))
                for t in range(TT):
                    bs.add(v.tensor_scalar(pick[:, t, :], iota, item_cur[:, t:t + 1], None, ALU.is_equal))
                    bs.add(v.tensor_scalar(pickc[:, t, :], iota, item_cur[:, t:t + 1], item_cur[:, 2 + t:3 + t],
                                           ALU.is_equal, ALU.mult))
                assert bs.n == BUILD_STEPS

            def gathered(i):
                for n in range(2):
                    dve.wait_ge(gather_mm, 2 * i + n + 1)
                    v.tensor_copy(xg[:, 4 * n:4 * n + 4, :].rearrange("p k c -> p (k c)"), bank[4 + n][:, 0:4 * CAP]) \
                        .then_inc(xg_ready, 1)

            def add_scattered(i, t):
                for n in range(2):
                    dve.wait_ge(scat_mm, 4 * i + 2 * t + n + 1)
                    w = work[:, t, n * HALF:(n + 1) * HALF]
                    v.tensor_tensor(w, w, bank[4 + n][:, :], ALU.add).then_inc(acc_done, 1)

            def item(i, first=False):
                for b in range(EXP_BLOCKS):
                    dve.wait_ge(esilu, EXP_BLOCKS * i + b + 1)
                    dve.wait_ge(unit_done, ITEM_UNITS * i + unit_pos("u", b, EXP_BLOCKS) + 1)
                    v.tensor_tensor(eh[:, b % 2].rearrange("p j c -> p (j c)"), esg[:, b % 2, :],
                                    bank[(3, 7)[b % 2]][:, 0:4 * CAP], ALU.mult).then_inc(eh_ready, 1)
                    if b in (1, 2) and not first:
                        add_scattered(i - 1, b - 1)
                    if b == 2:
                        dve.wait_ge(st_mm, i + 1)
                        v.tensor_copy(scat[0:CAP, :], bank[4][0:CAP, 0:T]).then_inc(scat_ready, 1)
                    if b == 3:
                        build_pick(i + 1)
                gathered(i + 1)

            build_pick(0)
            gathered(0)
            item(0, first=True)
            with dve.Fori(1, E) as i:
                item(i)
            n_over = dve.value_load(over_int[0:1, MAX_OVER:MAX_OVER + 1], min_val=0, max_val=MAX_OVER)
            with dve.Fori(0, MAX_OVER) as j:
                with dve.If(j < n_over):
                    item(j + E)
            for t in range(TT):
                add_scattered(n_over + (E - 1), t)
            dve.wait_ge(acc_done, 4 * (n_over + E))
            dve.wait_ge(ln_in, 32 * 4)
            for t in range(TT):
                normalise(4, t)
                dve.wait_ge(xhat_ready, TT * 3 + t + 1)
                st.then(v.tensor_tensor(work[:, t, :], work[:, t, :], ln_row[:, 0, :], ALU.mult))
                v.tensor_tensor(tokens[:, t, :], work[:, t, :], ln_row[:, 1, :], ALU.add).then_inc(out_ready, 1)

        @block.tensor
        def _(pe):
            mm = nc.tensor.matmul
            tr = nc.tensor.transpose

            def arrived(n):
                pe.wait_ge(landed[n % RING], 16 * (n // RING + 1))

            pe.wait_ge(consts_in, 16)
            pe.wait_ge(par_in, 16 * 8)
            tr(bank[0][:, 0:96], par_rows[:], ident[0:96, 0:96]).then_inc(par_turned, 1)
            tr(bank[1][:, 0:64], par_rows2[:], ident[0:64, 0:64]).then_inc(par_turned, 1)

            def turn(s):
                for t in range(TT):
                    if s == 0:
                        pe.wait_ge(x_in, 16 * TT)
                    else:
                        pe.wait_ge(xhat_ready, TT * (s - 1) + t + 1)
                    src = tokens if s == 0 else work
                    for k in range(DK):
                        last = tr(bank[TURN_BANKS[t][k // 4]][:, (k % 4) * P:(k % 4 + 1) * P],
                                  src[:, t, k * P:(k + 1) * P], ident)
                        if k % 4 == 3:
                            last.then_inc(turned, 1)
                pe.wait_ge(act_turn, TT * DK // 2 * (s + 1))
                pe.wait_ge(dve_turn, TT * DK // 2 * (s + 1))

            def mixer(l):
                u0 = MIXER_UNIT0[l]
                if l == 0:
                    pe.wait_ge(gatew_ready, 2)
                for k in range(DK):
                    last = mm(bank[6][0:64, 0:T], gate_w[:, l, k, :], xT[:, k, :], start=k == 0, stop=k == DK - 1)
                last.then_inc(gates_mm, 1)

                def chunk(unit, c, psum):
                    w = slot_cols(unit, FBLK)
                    for k in range(DK):
                        last = mm(psum, w[:, k, c * P:(c + 1) * P], xT[:, k, :], start=k == 0, stop=k == DK - 1)
                    last.then_inc(chunk_done, 1)

                if l == 0:
                    pe.wait_ge(par_ready, 2)
                for c in range(8):
                    if c % 4 == 0:
                        arrived(u0 + c // 4)
                    if c >= 4:
                        pe.wait_ge(zqk_ready, 8 * l + c - 3)
                    chunk(u0 + c // 4, c % 4, bank[c % 4][:, 0:T])
                arrived(u0 + 2)
                w = slot_cols(u0 + 2, FBLK)
                for t in range(TT):
                    for k in range(DK):
                        last = mm(bank[4 + t][:, :], xT[:, k, t * P:(t + 1) * P], w[:, k, :],
                                  start=k == 0, stop=k == DK - 1)
                    last.then_inc(v_done, 1)
                pe.wait_ge(rows_ready, l + 1)
                for n, r in enumerate((r_i, r_m)):
                    for t in range(TT):
                        c = (n * TT + t) * HEADS
                        last = tr(bank[6][:, c:c + HEADS], r[:, t * P:(t + 1) * P], ident[0:HEADS, 0:HEADS])
                last.then_inc(cols_mm, 1)
                for h in range(HEADS):
                    if h == 2:
                        pe.wait_ge(v_ready, TT * l + 1)
                    last = mm(bank[(7, 4)[h // 2]][:, (h % 2) * T:(h % 2 + 1) * T],
                              cst[0:HEADS, C_SEL + h * P:C_SEL + (h + 1) * P], r_negm, start=True, stop=True)
                    if h % 2:
                        last.then_inc(bcast_mm, 1)
                arrived(u0 + 3)
                pe.wait_ge(zqk_ready, 8 * (l + 1))
                for c in range(GROUPS):
                    chunk(u0 + 3, c, bank[c][:, 0:T])
                for h in range(HEADS):
                    if h == 0:
                        pe.wait_ge(qk_ready, 8 * (l + 1))
                    pe.wait_ge(u_ready, GROUPS * l + h + 1)
                    mm(bank[h][:, 0:T], qkT[:, HEADS + h, 0:P], qkT[:, h, :], start=True, stop=True)
                    mm(bank[h][:, T:T + P], qkT[:, HEADS + h, P:T], qkT[:, h, P:T], start=True, stop=True) \
                        .then_inc(score_mm, 1)
                arrived(u0 + 4)
                for c in range(HEADS):
                    if c == 0:
                        pe.wait_ge(v_ready, TT * (l + 1))
                    elif c == 1:
                        pe.wait_ge(cols_ready, l + 1)
                    elif c == 2:
                        pe.wait_ge(arg_ready, HEADS * (l + 1))
                    chunk(u0 + 4, c, bank[(5, 6, 7, 4)[c]][:, 0:T])
                pe.wait_ge(w_ready, HEADS * (l + 1))
                pe.wait_ge(v_ready, TT * (l + 1))
                pe.wait_ge(sig_ready, HEADS * l + 2)
                wts = [[(decay[:, h, 0:P], 0)] for h in range(HEADS)], \
                      [[(decay[:, h, P:T], 0), (decay[:, h, T:T + P], 1)] for h in range(HEADS)]
                for t in range(TT):
                    for h in range(HEADS):
                        for w, s in wts[t][h]:
                            mm(bank[6][:, t * HEADS + h:t * HEADS + h + 1], w, ones[:, 0:1],
                               start=s == 0, stop=s == t)
                for t in range(TT):
                    for h in range(HEADS):
                        for w, s in wts[t][h]:
                            last = mm(bank[2 + t][:, h * DH:(h + 1) * DH], w, v_sb[:, s, h * DH:(h + 1) * DH],
                                      start=s == 0, stop=s == t)
                    last.then_inc(pv_mm, 1)
                if l == 0:
                    pe.wait_ge(poolw_in, 16)
                for gr in range(GROUPS):
                    pe.wait_ge(pool_ready, GROUPS * l + gr + 1)
                    last = mm(bank[gr // 2][:, (gr % 2) * T:(gr % 2 + 1) * T], pool_ws[:, l, gr, :],
                              ubuf[:, gr, 16:], start=True, stop=True)
                    if gr % 2:
                        last.then_inc(pooly_mm, 1)

                def project(unit, k0, t, ks):
                    w = slot_cols(unit, D)
                    for n in range(2):
                        for k in ks:
                            last = mm(bank[SUM_BANKS[t][n]][:, :], yT[:, k0 + k, t * P:(t + 1) * P],
                                      w[:, k, n * HALF:(n + 1) * HALF], start=k0 + k == 0, stop=k0 + k == DK - 1)
                    return last

                pe.wait_ge(ypool_ready, GROUPS * (l + 1))
                pe.wait_ge(sig_ready, HEADS * (l + 1))
                arrived(u0 + 5)
                project(u0 + 5, 0, 0, range(4))
                project(u0 + 5, 0, 1, range(4)).then_inc(wo_done, 1)
                for t in range(TT):
                    pe.wait_ge(h_ready, HEADS * (TT * l + t + 1))
                    for h in range(HEADS):
                        last = tr(bank[(7, 6)[t]][:, h * P:(h + 1) * P], h_norm[:, t, h * DH:(h + 1) * DH], ident)
                    last.then_inc(ht_mm, 1)
                arrived(u0 + 6)
                for t in range(TT):
                    pe.wait_ge(ym_ready, HEADS * (TT * l + t + 1))
                    project(u0 + 6, 4, t, range(4)).then_inc(wo_done, 1)

            def dense():
                def gate_up(b):
                    for kind in "gu":
                        n = DENSE_UNIT0 + unit_pos(kind, b, DENSE_BLOCKS)
                        arrived(n)
                        w = slot_cols(n, dense_chunks(b) * P)
                        for j in range(dense_chunks(b)):
                            c = 4 * b + j
                            psum = bank[(2, 3, 6, 7)[c % 4]][:, (0 if kind == "g" else T):(T if kind == "g" else 2 * T)]
                            if kind == "g" and c >= 4:
                                pe.wait_ge(dh_ready, c - 3)
                            for k in range(DK):
                                last = mm(psum, w[:, k, j * P:(j + 1) * P], xT[:, k, :], start=k == 0,
                                          stop=k == DK - 1)
                            if kind == "u":
                                last.then_inc(chunk_done, 1)

                def down(b):
                    n = DENSE_UNIT0 + unit_pos("d", b, DENSE_BLOCKS)
                    arrived(n)
                    w = slot_cols(n, D)
                    final = b == DENSE_BLOCKS - 1
                    pe.wait_ge(dh_ready, 4 * b + dense_chunks(b))
                    for t in range(TT):
                        for half in range(2):
                            for j in range(dense_chunks(b)):
                                last = mm(bank[SUM_BANKS[t][half]][:, :], dh[:, b % 2, j, t * P:(t + 1) * P],
                                          w[:, j, half * HALF:(half + 1) * HALF],
                                          start=b == 0 and j == 0, stop=final and j == dense_chunks(b) - 1)
                        if final or t == TT - 1:
                            last.then_inc(down_done, 1)

                for b in range(DENSE_BLOCKS):
                    gate_up(b)
                    if b:
                        down(b - 1)
                down(DENSE_BLOCKS - 1)

            turn(0)
            mixer(0)
            turn(1)
            dense()
            turn(2)
            mixer(1)
            turn(3)

            pe.wait_ge(router_in, 32)
            for t in range(TT):
                for k in range(DK):
                    last = mm(bank[4][:, t * E:(t + 1) * E], xT[:, k, t * P:(t + 1) * P], rout_w[:, k, :],
                              start=k == 0, stop=k == DK - 1)
            last.then_inc(logit_mm, 1)
            pe.wait_ge(chosen_ready, 1)
            mm(bank[4][:, 2 * E:3 * E], tri, chosen[:, 0, :], start=True, stop=True)
            mm(bank[4][:, 3 * E:4 * E], ones, chosen[:, 0, :], start=True, stop=False)
            mm(bank[4][:, 3 * E:4 * E], tri, chosen[:, 1, :], start=False, stop=True)
            mm(bank[4][:, 4 * E:5 * E], ones, chosen[:, 0, :], start=True, stop=False)
            mm(bank[4][:, 4 * E:5 * E], ones, chosen[:, 1, :], start=False, stop=True).then_inc(pos_mm, 1)

            def gather(i):
                pe.wait_ge(build_steps, 5 * (i + 1))
                for k in range(DK):
                    for t in range(TT):
                        last = mm(bank[4 + k // 4][:, (k % 4) * CAP:(k % 4 + 1) * CAP],
                                  tokens[:, t, k * P:(k + 1) * P], pick[:, t, :], start=t == 0, stop=t == TT - 1)
                    if k % 4 == 3:
                        last.then_inc(gather_mm, 1)

            def y_turn(i):
                pe.wait_ge(yts_ready, 2 * (i + 1))
                for k in range(DK):
                    last = tr(bank[4 + k // 4][0:CAP, (k % 4) * P:(k % 4 + 1) * P], yTs[:, k, :], ident)
                    if k % 4 == 3:
                        last.then_inc(yt_mm, 1)

            def scatter(i, t):
                if t == 0:
                    pe.wait_ge(ysb_ready, 2 * (i + 1))
                    pe.wait_ge(scat_ready, i + 1)
                else:
                    pe.wait_ge(acc_done, 4 * i + 2)
                for n in range(2):
                    mm(bank[4 + n][:, :], scat[0:CAP, t * P:(t + 1) * P], y_sb[0:CAP, n * HALF:(n + 1) * HALF],
                       start=True, stop=True).then_inc(scat_mm, 1)

            def item(i, first=False):
                def landed_unit(u):
                    m = MOE_UNIT0 + u
                    pe.wait_ge(landed[m % RING], (ITEM_UNITS // RING * 16) * i + 16 * (m // RING + 1))

                def gate_up(b):
                    for kind in "gu":
                        u = unit_pos(kind, b, EXP_BLOCKS)
                        landed_unit(u)
                        w = slot_cols(MOE_UNIT0 + u, FBLK)
                        psum = bank[((2, 3), (6, 7))[b % 2][kind == "u"]]
                        for j in range(4):
                            for k in range(DK):
                                last = mm(psum[:, j * CAP:(j + 1) * CAP], w[:, k, j * P:(j + 1) * P], xg[:, k, :],
                                          start=k == 0, stop=k == DK - 1)
                        last.then_inc(unit_done, 1)

                def down(b):
                    u = unit_pos("d", b, EXP_BLOCKS)
                    landed_unit(u)
                    w = slot_cols(MOE_UNIT0 + u, D)
                    pe.wait_ge(eh_ready, EXP_BLOCKS * i + b + 1)
                    final = b == EXP_BLOCKS - 1
                    for k in range(DK):
                        for j in range(4):
                            last = mm(bank[k // 4][:, (k % 4) * CAP:(k % 4 + 1) * CAP], w[:, j, k * P:(k + 1) * P],
                                      eh[:, b % 2, j, :], start=b == 0 and j == 0 and k % 4 == 0,
                                      stop=final and j == 3 and k % 4 == 3, skip_group_check=True)
                    last.then_inc(unit_done, 1)

                pe.wait_ge(xg_ready, 2 * (i + 1))
                gate_up(0)
                if not first:
                    y_turn(i - 1)
                gate_up(1)
                if not first:
                    scatter(i - 1, 0)
                down(0)
                gate_up(2)
                if not first:
                    scatter(i - 1, 1)
                down(1)
                gate_up(3)
                if not first:
                    pe.wait_ge(acc_done, 4 * i)
                for t in range(TT):
                    last = tr(bank[4][0:CAP, t * P:(t + 1) * P], pickc[:, t, :], ident)
                last.then_inc(st_mm, 1)
                down(2)
                for b in range(4, EXP_BLOCKS):
                    gate_up(b)
                    down(b - 1)
                pe.wait_ge(scat_ready, i + 1)
                gather(i + 1)
                down(EXP_BLOCKS - 1)

            pe.wait_ge(tokens_ready, TT * 3)
            gather(0)
            item(0, first=True)
            with pe.Fori(1, E) as i:
                item(i)
            n_over = pe.value_load(over_int[0:1, MAX_OVER:MAX_OVER + 1], min_val=0, max_val=MAX_OVER)
            with pe.Fori(0, MAX_OVER) as j:
                with pe.If(j < n_over):
                    item(j + E)
            last_item = n_over + (E - 1)
            pe.wait_ge(xg_ready, 2 * (last_item + 2))
            y_turn(last_item)
            scatter(last_item, 0)
            scatter(last_item, 1)


def constant_table():
    c = np.zeros((P, C_END), np.float32)
    c[:, C_ID:C_ID + P] = np.eye(P)
    c[:, C_TRI:C_TRI + P] = np.triu(np.ones((P, P)), 1)
    c[:, C_ONES:C_ONES + T] = 1.0
    c[:, C_IOTA:C_IOTA + P] = np.arange(P)
    c[:, C_LT:C_LT + E * E] = np.tril(np.ones((E, E)), -1).reshape(-1)
    for g in range(GROUPS):
        c[:, C_INV + 16 * g:C_INV + 16 * g + 16] = 1.0 / np.minimum(np.arange(16) + 1, 2 << g)
    c[:, C_CE:C_CE + 2 * E] = np.tile(np.arange(E), 2)
    c[:, C_CT:C_CT + 2 * E] = np.repeat([CAP, 2 * CAP], E)
    for h in range(HEADS):
        c[h, C_SEL + h * P:C_SEL + (h + 1) * P] = 1.0
    return c


_INS = ["x", "w_in", "b_gates", "conv_w", "conv_b", "pool_w", "pool_scale", "mlstm_g", "w_out", "ln1_g", "ln1_b",
        "ln2_g", "ln2_b", "wg_dense", "wu_dense", "wd_dense", "w_router", "b_router", "wg_exp", "wu_exp", "wd_exp"]


def kernel(**inputs):
    import concourse.bacc as bacc
    from concourse.bass_utils import run_bass_kernel_spmd

    nc = bacc.Bacc("TRN2", target_bir_lowering=False, num_devices=1)
    arrays, args = {}, []
    for name in _INS:
        a = np.ascontiguousarray(inputs[name])
        arrays[f"in_{name}"] = a
        args.append(nc.dram_tensor(f"in_{name}", a.shape, mybir.dt.from_np(a.dtype), kind="ExternalInput").ap())
    c = constant_table()
    arrays["consts"] = c
    args.append(nc.dram_tensor("consts", c.shape, F32, kind="ExternalInput").ap())
    out = nc.dram_tensor("out", (1, T, D), F32, kind="ExternalOutput").ap()
    build(nc, *args, out)
    r = run_bass_kernel_spmd(nc, [arrays], core_ids=[0])
    return r.results[0]["out"]
```

```python
from contextlib import ExitStack

import numpy as np

import concourse.bass as bass
from concourse import mybir

F32 = mybir.dt.float32
F32R = mybir.dt.float32r
I32 = mybir.dt.int32
ALU = mybir.AluOpType
ACT = mybir.ActivationFunctionType
AX_X = mybir.AxisListType.X

P = 128
T = 256
TT = T // P
D = 1024
DK = D // P
HALF = 512
LAYERS = 2
HEADS = 4
DH = 128
GROUPS = 4
TAPS = 4
PAD = TAPS - 1
D_POOL = 512
D_MLSTM = 512
GATE_COL = D_POOL + 4 * D_MLSTM
F_DENSE = 2816
F_EXP = 3584
E = 8
TOP_K = 2
FBLK = 512
DENSE_BLOCKS = -(-F_DENSE // FBLK)
EXP_BLOCKS = F_EXP // FBLK
ALPHA = (2 * LAYERS) ** 0.25
EPS = 1e-5
QK_SCALE = DH ** -0.5

CAP = 104
MAX_OVER = (TOP_K * T) // (CAP + 1)
MAX_ITEMS = E + MAX_OVER

UNIT = 2048
RAW = 6
SPLIT = 3
AHEAD = SPLIT - 1
MIXER_KINDS = [(k, h) for k in "qkvpo" for h in range(2)] + [("w", h) for h in range(4)]
MIXER_UNITS = len(MIXER_KINDS)
DENSE_CHUNKS = F_DENSE // P
DENSE_LAST = DENSE_CHUNKS - 4 * (DENSE_BLOCKS - 1)
assert DENSE_LAST == 2
ITEM_UNITS = 6 * EXP_BLOCKS
assert ITEM_UNITS % RAW == 0 and ITEM_UNITS % SPLIT == 0 and MAX_OVER * (CAP + 1) <= TOP_K * T


def block_order(blocks):
    out = []
    for b in range(blocks):
        out += [("g", b), ("u", b)]
        if b:
            out.append(("d", b - 1))
    return out + [("d", blocks - 1)]


DENSE_ORDER = [(k, b, h) for k, b in block_order(DENSE_BLOCKS) for h in range(2 if b < DENSE_BLOCKS - 1 else 1)]
ITEM_ORDER = [(k, b, h) for k, b in block_order(EXP_BLOCKS) for h in range(2)]
DENSE_UNITS = len(DENSE_ORDER)
MIXER_UNIT0 = [0, MIXER_UNITS + DENSE_UNITS]
DENSE_UNIT0 = MIXER_UNITS
MOE_UNIT0 = 2 * MIXER_UNITS + DENSE_UNITS


def mixer_unit(l, kind, half):
    return MIXER_UNIT0[l] + MIXER_KINDS.index((kind, half))


def dense_unit(kind, b, half=0):
    return DENSE_UNIT0 + DENSE_ORDER.index((kind, b, half))


def dense_chunks(b):
    return min(4, DENSE_CHUNKS - 4 * b)


STEP_SILU = {ITEM_ORDER.index(("g", b, 1)): b for b in range(EXP_BLOCKS)}
STEP_MUL = {ITEM_ORDER.index(("u", b, 1)): b for b in range(EXP_BLOCKS)}
STEP_TURN = {ITEM_ORDER.index(("u", b, 1)) + (2 if b < EXP_BLOCKS - 1 else 1): b for b in range(EXP_BLOCKS)}
STEP_SCATTER = {7: 0, 9: 1, 11: 2, 13: 3}
STEP_SLOTS = 15
STEP_PICK = 20
STEP_GATHER = {ITEM_ORDER.index(("u", EXP_BLOCKS - 1, 1)): 0, ITEM_ORDER.index(("d", EXP_BLOCKS - 2, 1)): 1}

C_ID, C_TRI, C_ONES = 0, 128, 256
C_IOTA = C_ONES + T
C_LT = C_IOTA + P
C_INV = C_LT + E * E
C_CE = C_INV + GROUPS * 16
C_CT = C_CE + 2 * E
C_SEL = C_CT + 2 * E
C_END = C_SEL + HEADS * P

R_LN = {(1, "g"): 0, (1, "b"): 16, (2, "g"): 32, (2, "b"): 48}
R_CONVB, R_POOLS, R_MG, R_CONVW = 64, 80, 88, 96


class Steps:

    def __init__(self, eng, sem, base=0):
        self.eng, self.sem, self.base, self.n = eng, sem, base, 0

    def add(self, ins):
        ins.then_inc(self.sem, 1)
        self.n += 1

    def wait(self):
        self.eng.wait_ge(self.sem, self.base + self.n)

    def then(self, ins):
        self.add(ins)
        self.wait()


def build(nc, x, w_in, b_gates, conv_w, conv_b, pool_w, pool_scale, mlstm_g, w_out, ln1_g, ln1_b, ln2_g, ln2_b,
          wg_dense, wu_dense, wd_dense, w_router, b_router, wg_exp, wu_exp, wd_exp, consts, out):
    with ExitStack() as ctx:
        def sb(name, shape, dt=F32):
            return ctx.enter_context(nc.sbuf_tensor(name, shape, dt))

        def sem(name):
            return ctx.enter_context(nc.semaphore(name))

        raw = sb("raw", [P, RAW, UNIT])
        w_hi = sb("w_hi", [P, SPLIT, UNIT], F32R)
        w_lo = sb("w_lo", [P, SPLIT, UNIT], F32R)
        tokens = sb("tokens", [P, TT, D])
        work = sb("work", [P, TT, D])
        x_hi = sb("x_hi", [P, DK, T], F32R)
        x_lo = sb("x_lo", [P, DK, T], F32R)
        parts = sb("parts", [P, 2, 2048], F32R)
        ln_row = sb("ln_row", [P, 2, D])
        cst = sb("cst", [P, C_END])
        par_rows = sb("par_rows", [96, P])
        par_rows2 = sb("par_rows2", [64, P])
        par = sb("par", [P, 160])
        gate_w = sb("gate_w", [P, LAYERS, DK, 32 + HEADS])
        gate_raw = sb("gate_raw", [P, LAYERS, DK, 2 * HEADS])
        gate_b = sb("gate_b", [P, LAYERS])
        pool_ws = sb("pool_ws", [P, GROUPS, DH])
        rout_w = sb("rout_w", [P, DK, E])
        rout_b = sb("rout_b", [P, E])
        small = sb("small", [P, 2])
        stats = sb("stats", [P, TT, 2, 6])
        mv = sb("mv", [P, TT, 2])
        rstd = sb("rstd", [P, TT, 2])

        ARENA = 9600
        arena = sb("arena", [P, ARENA])
        at = [0]

        def shaped(v, shape):
            if len(shape) == 1:
                return v
            names = "abcd"[:len(shape)]
            return v.rearrange(f"p ({' '.join(names)}) -> p {' '.join(names)}",
                               **{k: s for k, s in zip(names, shape)})

        def carve(shape, start=None):
            if start is not None:
                at[0] = start
            n = int(np.prod(shape))
            v = arena[:, at[0]:at[0] + n]
            at[0] += n
            assert at[0] <= ARENA
            return shaped(v, shape)

        xf = carve([TT, DK, P], 0)
        zqk = carve([8, PAD + T], 0)
        decay = shaped(arena[:, 0:HEADS * (T + P)], [HEADS, T + P])
        h_norm = shaped(arena[:, at[0]:at[0] + TT * D_MLSTM], [TT, D_MLSTM])
        ubuf = carve([GROUPS, 16 + T])
        ptmp = carve([2, 16 + T])
        v_sb = carve([TT, D_MLSTM])
        sigT = carve([HEADS, T])
        rows = carve([5, T])
        conv_acc = carve([2, T])
        qkT = carve([8, T])
        yT = qkT
        r_i, r_f, r_l, r_negm, r_m = (rows[0:HEADS, n, :] for n in range(5))
        y_hi, y_lo = (shaped(parts[:, n, :], [8, T]) for n in range(2))
        cols = sb("cols", [P, 2, TT, HEADS])
        guard = sb("guard", [P, TT, HEADS])
        rden = sb("rden", [P, TT, HEADS])
        hstats = sb("hstats", [P, TT, HEADS, 6])
        hmv = sb("hmv", [P, TT, HEADS, 2])
        hstd = sb("hstd", [P, TT, HEADS])
        hrstd = sb("hrstd", [P, TT, HEADS])
        dsg = carve([2, T], 2048)
        dh = carve([2, T])
        dh_hi, dh_lo = (shaped(parts[:, n, :], [2, 4, T]) for n in range(2))
        esg = carve([2, FBLK], 2048)
        eh = carve([2, FBLK])
        XG = DK * CAP
        xg_hi, xg_lo = (shaped(parts[:, n, 0:XG], [DK, CAP]) for n in range(2))
        eh_hi, eh_lo = (shaped(parts[:, n, XG:XG + 8 * CAP], [2, 4, CAP]) for n in range(2))
        y_sb = carve([D])
        scat = carve([T])
        pick = carve([TT, CAP])
        pickc = carve([TT, CAP])
        logit = carve([TT, E])
        gt = carve([TT, E, E])
        eq = carve([TT, E, E])
        rank = carve([TT, E])
        chosen = carve([TT, E])
        top = carve([TT])
        expo = carve([TT, E])
        esum = carve([TT])
        comb = carve([TT, E])
        posm = carve([TT, E])
        count = carve([E])
        flag = carve([2 * E])
        frank = carve([2 * E])
        fsel = carve([2 * E])
        ftmp = carve([2 * E])
        over_e = carve([MAX_OVER])
        over_t = carve([MAX_OVER])
        n_over_f = carve([1])
        item_tab = carve([MAX_ITEMS + 1, 4])
        item_cur = carve([4])
        itmp = carve([TT, E])
        over_int = sb("over_int", [P, MAX_OVER + 1], I32)

        bank = [ctx.enter_context(nc.psum_tensor(f"bank{n}", [P, HALF], F32)) for n in range(8)]

        ident = cst[:, C_ID:C_ID + P]
        tri = cst[:, C_TRI:C_TRI + P]
        ones = cst[:, C_ONES:C_ONES + P]
        ones_t = cst[0:HEADS, C_ONES:C_ONES + T]
        iota = cst[:, C_IOTA:C_IOTA + CAP]
        one_col = small[:, 0:1]
        eps_col = small[:, 1:2]

        landed = [sem(f"landed{n}") for n in range(RAW)]
        x_in, consts_in, par_in, gatew_in, gateb_in, poolw_in, router_in, ln_in, out_done = map(sem, (
            "x_in", "consts_in", "par_in", "gatew_in", "gateb_in", "poolw_in", "router_in", "ln_in", "out_done"))
        hi_ready, lo_ready = map(sem, ("hi_ready", "lo_ready"))
        unit_done, chunk_done, par_turned, turned, gates_mm, cols_mm, bcast_mm, score_mm, pooly_mm, pv_mm, ht_mm, \
            logit_mm, pos_mm, gather_mm, eturn_mm, scat_mm, st_mm = map(sem, (
                "unit_done", "chunk_done", "par_turned", "turned", "gates_mm", "cols_mm", "bcast_mm", "score_mm",
                "pooly_mm", "pv_mm", "ht_mm", "logit_mm", "pos_mm", "gather_mm", "eturn_mm", "scat_mm", "st_mm"))
        xf_act, xhi_ready, gate_i, gate_e, gate_l, zqk_ready, qk_ready, u_ready, sig_ready, decay_ready, \
            guard_ready, hstd_ready, yhi_ready, std_ready, dsilu, dhi_ready, esilu, ehi_ready, xghi_ready, \
            expo_ready, ysb_ready = map(sem, (
                "xf_act", "xhi_ready", "gate_i", "gate_e", "gate_l", "zqk_ready", "qk_ready", "u_ready",
                "sig_ready", "decay_ready", "guard_ready", "hstd_ready", "yhi_ready", "std_ready", "dsilu",
                "dhi_ready", "esilu", "ehi_ready", "xghi_ready", "expo_ready", "ysb_ready"))
        par_ready, xf_dve, xlo_ready, absf_ready, rows_ready, conv_ready, v_ready, cols_ready, arg_ready, w_ready, \
            ypool_ready, rden_ready, hvar_ready, h_ready, ym_ready, ylo_ready, var_ready, xhat_ready, dh_ready, \
            dlo_ready, logit_ready, chosen_ready, table_ready, eh_ready, elo_ready, xglo_ready, scat_ready, \
            acc_done, out_ready, steps, build_steps = map(sem, (
                "par_ready", "xf_dve", "xlo_ready", "absf_ready", "rows_ready", "conv_ready", "v_ready",
                "cols_ready", "arg_ready", "w_ready", "ypool_ready", "rden_ready", "hvar_ready", "h_ready",
                "ym_ready", "ylo_ready", "var_ready", "xhat_ready", "dh_ready", "dlo_ready", "logit_ready",
                "chosen_ready", "table_ready", "eh_ready", "elo_ready", "xglo_ready", "scat_ready", "acc_done",
                "out_ready", "steps", "build_steps"))
        small_ready, gatew_zero, gatew_ready, pool_steps, pool_ready, mask_ready, tokens_ready = map(sem, (
            "small_ready", "gatew_zero", "gatew_ready", "pool_steps", "pool_ready", "mask_ready", "tokens_ready"))

        x_d = x.rearrange("b (t p) d -> p (b t) d", p=P)
        out_d = out.rearrange("b (t p) d -> p (b t) d", p=P)

        def par_col(name, layer, k):
            if name in R_LN:
                c = R_LN[name] + DK * layer + k
            elif name == "conv_b":
                c = R_CONVB + 8 * layer + k
            elif name == "pool_scale":
                c = R_POOLS + 4 * layer + k
            elif name == "mlstm_g":
                c = R_MG + 4 * layer + k
            else:
                c = R_CONVW + (layer * TAPS + name[1]) * 8 + k
            return par[:, c:c + 1]

        SUM_BANKS = [(0, 1), (4, 5)]
        TURN_BANKS = [(2, 3), (6, 7)]
        NORM = {1: (1, 0), 2: (2, 0), 3: (1, 1), 4: (2, 1)}

        SCORE_BANKS = (5, 6, 7, 4)
        PV_BANKS = (7, 6)

        def rows_of(w, r0, n):
            return w[r0:r0 + n * P, :].rearrange("(k p) n -> p k n", p=P)

        def mixer_source(l, kind, half):
            if kind == "w":
                return rows_of(w_out[l], 2 * P * half, 2)
            c0 = {"p": 0, "q": D_POOL, "k": D_POOL + D_MLSTM, "v": D_POOL + 2 * D_MLSTM,
                  "o": D_POOL + 3 * D_MLSTM}[kind]
            return rows_of(w_in[l], 4 * P * half, 4)[:, :, c0:c0 + FBLK]

        def dense_source(kind, b, half):
            if kind == "d":
                return rows_of(wd_dense[0], b * FBLK + 2 * P * half, 2)
            w = wg_dense if kind == "g" else wu_dense
            if b == DENSE_BLOCKS - 1:
                return rows_of(w[0], 0, DK)[:, :, b * FBLK:]
            return rows_of(w[0], 4 * P * half, 4)[:, :, b * FBLK:(b + 1) * FBLK]

        def expert_source(kind, b, half, e):
            w = {"g": wg_exp, "u": wu_exp, "d": wd_exp}[kind][0, e].rearrange("(k p) n -> p k n", p=P)
            if kind == "d":
                return w[:, 4 * b + 2 * half:4 * b + 2 * half + 2, :]
            return w[:, 4 * half:4 * half + 4, b * FBLK:(b + 1) * FBLK]

        def parts_of(n, width):
            return tuple(w[:, n % SPLIT, :].rearrange("p (k n) -> p k n", n=width) for w in (w_hi, w_lo))

        def chunk_event(l, kind, c):
            if c == (TT if kind == "v" else 4) - 1:
                return unit_done, mixer_unit(l, kind, 1) + 1
            before = {"q": 0, "k": 3, "v": 6, "p": 7, "o": 10}[kind]
            return chunk_done, CHUNKS0[l] + before + c + 1

        def dense_event(c):
            b = c // 4
            if c % 4 == dense_chunks(b) - 1:
                return unit_done, dense_unit("u", b, 1 if b < DENSE_BLOCKS - 1 else 0) + 1
            return chunk_done, DENSE_CHUNKS0 + 3 * b + c % 4 + 1

        CHUNKS_MIXER = 3 + 3 + 1 + 3 + 3 + 1
        CHUNKS_DENSE = 3 * (DENSE_BLOCKS - 1) + (DENSE_LAST - 1) + 1
        CHUNKS0 = [0, CHUNKS_MIXER + CHUNKS_DENSE]
        DENSE_CHUNKS0 = CHUNKS_MIXER

        def sum_event(s, t):
            if s == 2:
                return ((chunk_done, CHUNKS_MIXER + CHUNKS_DENSE) if t == 0 else
                        (unit_done, DENSE_UNIT0 + DENSE_UNITS))
            l = (s - 1) // 2
            return (chunk_done, CHUNKS0[l] + CHUNKS_MIXER) if t == 0 else (unit_done, mixer_unit(l, "w", 3) + 1)

        block = ctx.enter_context(nc.Block())

        @block.sync
        def _(sp):
            def load(n, src, i=0):
                k, c = src.shape[1], src.shape[2]
                if n >= RAW:
                    sp.wait_ge(lo_ready, i * ITEM_UNITS + (n - RAW + 1))
                dst = raw[:, n % RAW, :].rearrange("p (k n) -> p k n", n=c)[:, 0:k, :]
                sp.dma_start(dst, src).then_inc(landed[n % RAW], 16)

            for t in range(TT):
                sp.dma_start(tokens[:, t, :], x_d[:, t, :]).then_inc(x_in, 16)
            for l in range(LAYERS):
                sp.dma_start(gate_raw[:, l, :, :],
                             w_in[l, :, GATE_COL:GATE_COL + 2 * HEADS].rearrange("(k p) h -> p k h", p=P)
                             ).then_inc(gatew_in, 16)
            sp.wait_ge(consts_in, 16)
            sp.wait_ge(gateb_in, 16 * 2 * LAYERS)
            for kind, half in MIXER_KINDS:
                load(mixer_unit(0, kind, half), mixer_source(0, kind, half))
            for n, (kind, b, half) in enumerate(DENSE_ORDER):
                load(DENSE_UNIT0 + n, dense_source(kind, b, half))
            for kind, half in MIXER_KINDS:
                load(mixer_unit(1, kind, half), mixer_source(1, kind, half))

            def item_loads(i, e, units=ITEM_UNITS):
                for u, (kind, b, half) in enumerate(ITEM_ORDER[:units]):
                    load(MOE_UNIT0 + u, expert_source(kind, b, half, e), i)

            with sp.Fori(0, E) as i:
                item_loads(i, i)
            sp.wait_ge(table_ready, 1)
            n_over = sp.value_load(over_int[0:1, MAX_OVER:MAX_OVER + 1], min_val=0, max_val=MAX_OVER)
            with sp.Fori(0, MAX_OVER) as j:
                with sp.If(j < n_over):
                    e = sp.value_load(over_int[0:1, bass.ds(j, 1)], min_val=0, max_val=E - 1)
                    item_loads(j + E, e)
            item_loads(n_over + E, 0, AHEAD)
            for t in range(TT):
                sp.wait_ge(out_ready, t + 1)
                sp.dma_start(out_d[:, t, :], tokens[:, t, :]).then_inc(out_done, 16)
            sp.wait_ge(out_done, 16 * TT)

        @block.gpsimd
        def _(pool):
            g = nc.gpsimd
            g.memset(small[:, 0:1], 1.0).then_inc(small_ready, 1)
            g.memset(small[:, 1:2], EPS).then_inc(small_ready, 1)
            g.memset(gate_w[:], 0.0).then_inc(gatew_zero, 1)
            for l in range(LAYERS):
                for r, c in ((0, 0), (32, HEADS)):
                    pool.dma_start(gate_b[r:r + HEADS, l:l + 1],
                                   b_gates[l, c:c + HEADS].rearrange("(h a) -> h a", a=1)).then_inc(gateb_in, 16)
            pool.wait_ge(gatew_in, 16 * LAYERS)
            pool.wait_ge(gatew_zero, 1)
            g.tensor_copy(gate_w[:, :, :, 0:HEADS].rearrange("p l k h -> p (l k) h"),
                          gate_raw[:, :, :, 0:HEADS].rearrange("p l k h -> p (l k) h")).then_inc(gatew_ready, 1)
            g.tensor_copy(gate_w[:, :, :, 32:32 + HEADS].rearrange("p l k h -> p (l k) h"),
                          gate_raw[:, :, :, HEADS:].rearrange("p l k h -> p (l k) h")).then_inc(gatew_ready, 1)

            def load_ln(s):
                norm, l = NORM[s]
                for n, w in enumerate(((ln1_g, ln1_b), (ln2_g, ln2_b))[norm - 1]):
                    pool.dma_start(ln_row[:, n, :], w[l:l + 1, :].partition_broadcast(P)
                                   .rearrange("p a d -> p (a d)")).then_inc(ln_in, 16)

            load_ln(1)
            pool.dma_start(pool_ws[:], pool_w[0].rearrange("g c d -> c g d")).then_inc(poolw_in, 16)
            pool.dma_start(rout_w[:], w_router[0].rearrange("(k p) e -> p k e", p=P)).then_inc(router_in, 16)
            pool.dma_start(rout_b[:], b_router[0:1, :].partition_broadcast(P)
                           .rearrange("p a e -> p (a e)")).then_inc(router_in, 16)

            st = Steps(pool, pool_steps)

            def pooling(l):
                st.then(g.memset(ptmp[:, :, 0:16], 0.0))
                for gr in range(GROUPS):
                    pool.wait_ge(u_ready, GROUPS * l + gr + 1)
                    st.then(g.memset(ubuf[:, gr, 0:16], 0.0))
                    u = ubuf[:, gr, :]
                    src = u
                    if gr:
                        st.wait()
                    for step in range(gr + 1):
                        sh = 1 << step
                        dst = ptmp[:, step % 2, :]
                        st.then(g.tensor_tensor(dst[:, 16:], src[:, 16:], src[:, 16 - sh:16 + T - sh], ALU.add))
                        src = dst
                    st.add(g.tensor_tensor(src[:, 16:32], src[:, 16:32], cst[:, C_INV + 16 * gr:C_INV + 16 * gr + 16],
                                           ALU.mult))
                    st.then(g.tensor_scalar(src[:, 32:], src[:, 32:], 1.0 / (2 << gr), None, ALU.mult))
                    g.tensor_tensor(u[:, 16:], src[:, 16:], u[:, 16:], ALU.subtract).then_inc(pool_ready, 1)
                    pool.wait_ge(pool_ready, GROUPS * l + gr + 1)

            def masks(l):
                pool.wait_ge(decay_ready, HEADS * (l + 1))
                for c in (0, T):
                    blk = decay[:, :, c:c + P]
                    g.affine_select(out=blk, in_=blk, compare_op=ALU.is_ge, fill=0.0, base=0,
                                    pattern=[[0, HEADS], [1, P]], channel_multiplier=-1).then_inc(mask_ready, 1)

            def token_rows(s):
                pool.wait_ge(ln_in, 32 * s)
                for t in range(TT):
                    pool.wait_ge(xhat_ready, TT * (s - 1) + t + 1)
                    st.then(g.tensor_tensor(tokens[:, t, :], work[:, t, :], ln_row[:, 0, :], ALU.mult))
                    g.tensor_tensor(tokens[:, t, :], tokens[:, t, :], ln_row[:, 1, :], ALU.add) \
                        .then_inc(tokens_ready, 1)
                pool.wait_ge(tokens_ready, TT * s)
                load_ln(s + 1)

            pool.wait_ge(consts_in, 16)
            for l in range(LAYERS):
                masks(l)
                pooling(l)
                token_rows(2 * l + 1)
                if l + 1 < LAYERS:
                    pool.wait_ge(pooly_mm, 2)
                    pool.dma_start(pool_ws[:], pool_w[1].rearrange("g c d -> c g d")).then_inc(poolw_in, 16)
                    token_rows(2 * l + 2)

        @block.scalar
        def _(act):
            a = nc.scalar
            act.dma_start(cst[:], consts).then_inc(consts_in, 16)
            for (norm, kind), w in (((1, "g"), ln1_g), ((1, "b"), ln1_b), ((2, "g"), ln2_g), ((2, "b"), ln2_b)):
                r = R_LN[(norm, kind)]
                act.dma_start(par_rows[r:r + 16, :], w.rearrange("l (k p) -> (l k) p", p=P)).then_inc(par_in, 16)
            for r, n, w in ((R_CONVB, 16, conv_b), (R_POOLS, 8, pool_scale), (R_MG, 8, mlstm_g)):
                act.dma_start(par_rows[r:r + n, :], w.rearrange("l (k p) -> (l k) p", p=P)).then_inc(par_in, 16)
            act.dma_start(par_rows2[:], conv_w.rearrange("l j (k p) -> (l j k) p", p=P)).then_inc(par_in, 16)

            at_unit = [0]

            def round_hi(n, i=0):
                act.wait_ge(landed[n % RAW], i * (16 * ITEM_UNITS // RAW) + 16 * (n // RAW + 1))
                if n >= SPLIT:
                    act.wait_ge(unit_done, i * ITEM_UNITS + (n - SPLIT + 1))
                a.copy(w_hi[:, n % SPLIT, :], raw[:, n % RAW, :]).then_inc(hi_ready, 1)

            def ahead():
                round_hi(at_unit[0])
                at_unit[0] += 1

            def turn(s):
                for t in range(TT):
                    act.wait_ge(turned, 2 * (TT * s + t) + 1)
                    if s == 1 and t == 0:
                        act.wait_ge(par_ready, 2)
                    for k in range(DK // 2):
                        src = bank[TURN_BANKS[t][0]][:, k * P:(k + 1) * P]
                        if s == 0:
                            a.copy(xf[:, t, k, :], src).then_inc(xf_act, 1)
                        else:
                            norm, l = NORM[s]
                            a.activation(xf[:, t, k, :], src, ACT.Identity, bias=par_col((norm, "b"), l, k),
                                         scale=par_col((norm, "g"), l, k)).then_inc(xf_act, 1)
                    for n in range(2):
                        if n == 0:
                            act.wait_ge(xf_act, 4 * (TT * s + t + 1))
                        else:
                            act.wait_ge(xf_dve, 4 * (TT * s + t + 1))
                        a.copy(x_hi[:, 4 * n:4 * n + 4, t * P:(t + 1) * P], xf[:, t, 4 * n:4 * n + 4, :]) \
                            .then_inc(xhi_ready, 1)

            def mixer(l):
                ahead()
                act.wait_ge(absf_ready, l + 1)
                a.activation(r_i, bank[6][0:HEADS, 0:T], ACT.Identity, bias=gate_b[0:HEADS, l:l + 1]) \
                    .then_inc(gate_i, 1)
                a.activation(r_l, r_l, ACT.Exp, scale=-1.0).then_inc(gate_e, 1)
                act.wait_ge(gate_e, l + 1)
                if l == 0:
                    act.wait_ge(small_ready, 2)
                a.activation(r_l, r_l, ACT.Ln, bias=small[0:HEADS, 0:1]).then_inc(gate_l, 1)
                ahead()

                def copies(kind, c0):
                    for c in range(4):
                        act.wait_ge(*chunk_event(l, kind, c))
                        a.copy(zqk[:, c0 + c, PAD:], bank[c][:, 0:T]).then_inc(zqk_ready, 1)

                def silu(c):
                    act.wait_ge(conv_ready, 8 * l + c + 1)
                    a.activation(qkT[:, c, :], conv_acc[:, c % 2, :], ACT.Silu, bias=par_col("conv_b", l, c)) \
                        .then_inc(qk_ready, 1)

                copies("q", 0)
                ahead()
                silu(0)
                silu(1)
                ahead()
                silu(2)
                silu(3)
                copies("k", 4)
                ahead()
                silu(4)
                silu(5)
                ahead()
                silu(6)
                silu(7)
                ahead()
                for h in range(HEADS):
                    act.wait_ge(arg_ready, HEADS * l + h + 1)
                    a.activation(decay[:, h, :], decay[:, h, :], ACT.Exp).then_inc(decay_ready, 1)
                act.wait_ge(cols_ready, l + 1)
                a.activation(guard[:].rearrange("p t h -> p (t h)"), cols[:, 1].rearrange("p t h -> p (t h)"),
                             ACT.Exp, scale=-1.0).then_inc(guard_ready, 1)
                ahead()
                for c in range(GROUPS):
                    act.wait_ge(*chunk_event(l, "p", c))
                    a.copy(ubuf[:, c, 16:], bank[c][:, 0:T]).then_inc(u_ready, 1)
                ahead()
                ahead()
                for c in range(HEADS):
                    act.wait_ge(*chunk_event(l, "o", c))
                    a.activation(sigT[:, c, :], bank[c][:, 0:T], ACT.Sigmoid).then_inc(sig_ready, 1)
                ahead()
                act.wait_ge(ypool_ready, l + 1)
                a.copy(y_hi[:, 0:GROUPS, :], yT[:, 0:GROUPS, :]).then_inc(yhi_ready, 1)
                for t in range(TT):
                    act.wait_ge(hvar_ready, TT * l + t + 1)
                    a.activation(hstd[:, t, :], hmv[:, t, :, 1], ACT.Sqrt, bias=eps_col).then_inc(hstd_ready, 1)
                ahead()
                act.wait_ge(ym_ready, 2 * HEADS * (l + 1))
                a.copy(y_hi[:, GROUPS:, :], yT[:, GROUPS:, :]).then_inc(yhi_ready, 1)
                ahead()
                ahead()

            def norm_std(s):
                for t in range(TT):
                    act.wait_ge(var_ready, TT * (s - 1) + t + 1)
                    a.activation(rstd[:, t, 0:1], mv[:, t, 1:2], ACT.Sqrt, bias=eps_col).then_inc(std_ready, 1)

            def dense():
                def silu(c):
                    act.wait_ge(*dense_event(c))
                    if c >= 2:
                        act.wait_ge(dh_ready, c - 1)
                    a.activation(dsg[:, c % 2, :], bank[(2, 3, 6, 7)[c % 4]][:, 0:T], ACT.Silu).then_inc(dsilu, 1)

                def hidden_hi(c):
                    act.wait_ge(dh_ready, c + 1)
                    if c % 4 == 0 and c >= 8:
                        act.wait_ge(unit_done, dense_unit("d", c // 4 - 2, 1) + 1)
                    a.copy(dh_hi[:, c // 4 % 2, c % 4, :], dh[:, c % 2, :]).then_inc(dhi_ready, 1)

                for kind, b, half in DENSE_ORDER:
                    ahead()
                    if kind == "u" and half == (1 if b < DENSE_BLOCKS - 1 else 0):
                        c0, n = 4 * b, dense_chunks(b)
                        silu(c0)
                        for c in range(c0 + 1, c0 + n):
                            silu(c)
                            hidden_hi(c - 1)
                        hidden_hi(c0 + n - 1)

            for _ in range(AHEAD):
                ahead()
            turn(0)
            for l in range(LAYERS):
                mixer(l)
                norm_std(2 * l + 1)
                turn(2 * l + 1)
                if l == 0:
                    dense()
                    norm_std(2)
                    turn(2)
            act.wait_ge(logit_ready, 1)
            for t in range(TT):
                a.activation(expo[:, t, :], logit[:, t, :], ACT.Exp, bias=top[:, t:t + 1]).then_inc(expo_ready, 1)

            def gathered_hi(i, n):
                act.wait_ge(gather_mm, 2 * i + n + 1)
                a.copy(xg_hi[:, 4 * n:4 * n + 4, :].rearrange("p k c -> p (k c)"), bank[4][:, 0:4 * CAP]) \
                    .then_inc(xghi_ready, 1)

            def item(i):
                for u in range(ITEM_UNITS):
                    round_hi(MOE_UNIT0 + u + AHEAD, i)
                    if u in STEP_SILU:
                        b = STEP_SILU[u]
                        act.wait_ge(unit_done, i * ITEM_UNITS + (MOE_UNIT0 + u + 1))
                        a.activation(esg[0:CAP, b % 2, :], bank[(2, 6)[b % 2]][0:CAP, :], ACT.Silu) \
                            .then_inc(esilu, 1)
                    if u in STEP_TURN:
                        b = STEP_TURN[u]
                        act.wait_ge(eturn_mm, i * EXP_BLOCKS + (b + 1))
                        a.copy(eh_hi[:, b % 2].rearrange("p j c -> p (j c)"), bank[5][:, 0:4 * CAP]) \
                            .then_inc(ehi_ready, 1)
                    if u in STEP_GATHER:
                        gathered_hi(i + 1, STEP_GATHER[u])
                act.wait_ge(unit_done, i * ITEM_UNITS + (MOE_UNIT0 + ITEM_UNITS))
                for n in range(2):
                    a.copy(y_sb[0:CAP, n * HALF:(n + 1) * HALF], bank[n][0:CAP, :]).then_inc(ysb_ready, 1)

            gathered_hi(0, 0)
            gathered_hi(0, 1)
            with act.Fori(0, E) as i:
                item(i)
            n_over = act.value_load(over_int[0:1, MAX_OVER:MAX_OVER + 1], min_val=0, max_val=MAX_OVER)
            with act.Fori(0, MAX_OVER) as j:
                with act.If(j < n_over):
                    item(j + E)
            norm_std(4)

        @block.vector
        def _(dve):
            v = nc.vector
            st = Steps(dve, steps)

            at_unit = [0]

            def subtract_lo(n, i=0):
                dve.wait_ge(hi_ready, i * ITEM_UNITS + (n + 1))
                v.tensor_tensor(w_lo[:, n % SPLIT, :], raw[:, n % RAW, :], w_hi[:, n % SPLIT, :].bitcast(F32),
                                ALU.subtract).then_inc(lo_ready, 1)

            def ahead():
                subtract_lo(at_unit[0])
                at_unit[0] += 1

            def turn(s):
                for t in range(TT):
                    dve.wait_ge(turned, 2 * (TT * s + t) + 2)
                    if s == 1 and t == 0:
                        dve.wait_ge(par_ready, 2)
                    for k in range(DK // 2, DK):
                        src = bank[TURN_BANKS[t][1]][:, (k - 4) * P:(k - 3) * P]
                        if s == 0:
                            v.tensor_copy(xf[:, t, k, :], src).then_inc(xf_dve, 1)
                        else:
                            norm, l = NORM[s]
                            v.tensor_scalar(xf[:, t, k, :], src, par_col((norm, "g"), l, k),
                                            par_col((norm, "b"), l, k), ALU.mult, ALU.add).then_inc(xf_dve, 1)
                for t in range(TT):
                    for n in range(2):
                        dve.wait_ge(xhi_ready, 2 * (TT * s + t) + n + 1)
                        at_x = (slice(None), slice(4 * n, 4 * n + 4), slice(t * P, (t + 1) * P))
                        v.tensor_tensor(x_lo[at_x], xf[:, t, 4 * n:4 * n + 4, :], x_hi[at_x].bitcast(F32),
                                        ALU.subtract).then_inc(xlo_ready, 1)

            def mixer(l):
                ahead()
                dve.wait_ge(gates_mm, l + 1)
                dve.wait_ge(gateb_in, 16 * 2 * LAYERS)
                dve.wait_ge(xlo_ready, 2 * TT * (2 * l + 1))
                st.add(v.memset(zqk[:, :, 0:PAD], 0.0))
                st.then(v.tensor_scalar(r_f, bank[6][32:32 + HEADS, 0:T], gate_b[32:32 + HEADS, l:l + 1], None,
                                        ALU.add))
                v.scalar_tensor_tensor(out=r_l, in0=r_f, scalar=-1.0, in1=r_f, op0=ALU.mult, op1=ALU.max) \
                    .then_inc(absf_ready, 1)
                dve.wait_ge(gate_l, l + 1)
                st.then(v.scalar_tensor_tensor(out=r_f, in0=r_f, scalar=0.0, in1=r_l, op0=ALU.min,
                                               op1=ALU.subtract))
                st.then(v.tensor_tensor_scan(r_l, ones_t, r_f, 0.0, ALU.mult, ALU.add))
                dve.wait_ge(gate_i, l + 1)
                st.then(v.tensor_tensor(r_i, r_i, r_l, ALU.subtract))
                st.then(v.tensor_tensor_scan(r_m, ones_t, r_i, 0.0, ALU.mult, ALU.max))
                st.add(v.tensor_scalar(r_negm, r_m, -1.0, None, ALU.mult))
                st.wait()
                v.tensor_tensor(r_m, r_m, r_l, ALU.add).then_inc(rows_ready, 1)

                if l == 0:
                    for n, (r, c) in enumerate(((96, 0), (64, 96))):
                        dve.wait_ge(par_turned, n + 1)
                        v.tensor_copy(par[:, c:c + r], bank[(4, 5)[n]][:, 0:r]).then_inc(par_ready, 1)
                    dve.wait_ge(par_ready, 2)
                ahead()

                def conv(c):
                    dve.wait_ge(zqk_ready, 8 * l + c + 1)
                    if c >= 2:
                        dve.wait_ge(qk_ready, 8 * l + c - 1)
                    acc = conv_acc[:, c % 2, :]
                    st.then(v.tensor_scalar(acc, zqk[:, c, 0:T], par_col(("conv_w", 0), l, c), None, ALU.mult))
                    for j in range(1, TAPS):
                        ins = v.scalar_tensor_tensor(out=acc, in0=zqk[:, c, j:j + T],
                                                     scalar=par_col(("conv_w", j), l, c), in1=acc,
                                                     op0=ALU.mult, op1=ALU.add)
                        if j < TAPS - 1:
                            st.then(ins)
                        else:
                            ins.then_inc(conv_ready, 1)

                conv(0)
                conv(1)
                ahead()
                conv(2)
                conv(3)
                ahead()
                conv(4)
                conv(5)
                ahead()
                conv(6)
                conv(7)
                ahead()
                for t in range(TT):
                    dve.wait_ge(*chunk_event(l, "v", t))
                    v.tensor_copy(v_sb[:, t, :], bank[4 + t][:, :]).then_inc(v_ready, 1)
                dve.wait_ge(cols_mm, l + 1)
                v.tensor_copy(cols[:].rearrange("p a t h -> p (a t h)"), bank[6][:, 0:4 * HEADS]) \
                    .then_inc(cols_ready, 1)
                dve.wait_ge(cols_ready, l + 1)
                ahead()
                dve.wait_ge(conv_ready, 8 * (l + 1))
                for h in range(HEADS):
                    dve.wait_ge(bcast_mm, 2 * l + h // 2 + 1)
                    m = bank[(7, 4)[h // 2]][:, (h % 2) * T:(h % 2 + 1) * T]
                    st.add(v.tensor_scalar(decay[:, h, 0:T], m, cols[:, 0, 0, h:h + 1], 0.0, ALU.add, ALU.min))
                    v.tensor_scalar(decay[:, h, T:T + P], m[:, P:T], cols[:, 0, 1, h:h + 1], 0.0, ALU.add,
                                    ALU.min).then_inc(arg_ready, 1)
                ahead()
                ahead()
                dve.wait_ge(mask_ready, 2 * (l + 1))
                for h in range(HEADS):
                    dve.wait_ge(score_mm, HEADS * l + h + 1)
                    v.scalar_tensor_tensor(out=decay[:, h, :], in0=bank[SCORE_BANKS[h]][:, 0:T + P],
                                           scalar=QK_SCALE, in1=decay[:, h, :], op0=ALU.mult, op1=ALU.mult) \
                        .then_inc(w_ready, 1)
                ahead()
                for gr in range(GROUPS):
                    dve.wait_ge(pooly_mm, 2 * l + gr // 2 + 1)
                    ins = v.tensor_scalar(yT[:, gr, :], bank[2 + gr // 2][:, (gr % 2) * T:(gr % 2 + 1) * T],
                                          par_col("pool_scale", l, gr), None, ALU.mult)
                    if gr < GROUPS - 1:
                        st.add(ins)
                    else:
                        ins.then_inc(ypool_ready, 1)
                dve.wait_ge(guard_ready, l + 1)
                dve.wait_ge(pv_mm, TT * l + 1)
                den = bank[4][:, 0:TT * HEADS]
                rd, gd = (w[:].rearrange("p t h -> p (t h)") for w in (rden, guard))
                st.then(v.tensor_tensor(rd, den, gd, ALU.max))
                v.scalar_tensor_tensor(out=rd, in0=den, scalar=-1.0, in1=rd, op0=ALU.mult, op1=ALU.max) \
                    .then_inc(rden_ready, 1)
                dve.wait_ge(rden_ready, l + 1)
                st.then(v.reciprocal(rd, rd))
                dve.wait_ge(yhi_ready, 2 * l + 1)
                v.tensor_tensor(y_lo[:, 0:GROUPS, :], yT[:, 0:GROUPS, :], y_hi[:, 0:GROUPS, :].bitcast(F32),
                                ALU.subtract).then_inc(ylo_ready, 1)
                for t in range(TT):
                    dve.wait_ge(pv_mm, TT * l + t + 1)
                    for h in range(HEADS):
                        st.add(v.tensor_scalar(h_norm[:, t, h * DH:(h + 1) * DH],
                                               bank[PV_BANKS[t]][:, h * DH:(h + 1) * DH],
                                               rden[:, t, h:h + 1], None, ALU.mult))
                    st.wait()
                    for h in range(HEADS):
                        st.add(v.bn_stats(hstats[:, t, h, :], h_norm[:, t, h * DH:(h + 1) * DH]))
                    st.wait()
                    for h in range(HEADS):
                        ins = v.bn_aggr(hmv[:, t, h, :], hstats[:, t, h, :])
                        if h < HEADS - 1:
                            st.add(ins)
                        else:
                            ins.then_inc(hvar_ready, 1)
                ahead()
                for t in range(TT):
                    dve.wait_ge(hstd_ready, TT * l + t + 1)
                    dve.wait_ge(hvar_ready, TT * l + t + 1)
                    st.then(v.reciprocal(hrstd[:, t, :], hstd[:, t, :]))
                    for h in range(HEADS):
                        v.tensor_scalar(h_norm[:, t, h * DH:(h + 1) * DH], h_norm[:, t, h * DH:(h + 1) * DH],
                                        hmv[:, t, h, 0:1], hrstd[:, t, h:h + 1], ALU.subtract, ALU.mult) \
                            .then_inc(h_ready, 1)
                dve.wait_ge(sig_ready, HEADS * (l + 1))
                for t in range(TT):
                    dve.wait_ge(ht_mm, TT * l + t + 1)
                    for h in range(HEADS):
                        v.scalar_tensor_tensor(out=yT[:, GROUPS + h, t * P:(t + 1) * P],
                                               in0=bank[PV_BANKS[t]][:, h * P:(h + 1) * P],
                                               scalar=par_col("mlstm_g", l, h),
                                               in1=sigT[:, h, t * P:(t + 1) * P],
                                               op0=ALU.mult, op1=ALU.mult).then_inc(ym_ready, 1)
                ahead()
                dve.wait_ge(yhi_ready, 2 * l + 2)
                v.tensor_tensor(y_lo[:, GROUPS:, :], yT[:, GROUPS:, :], y_hi[:, GROUPS:, :].bitcast(F32),
                                ALU.subtract).then_inc(ylo_ready, 1)
                ahead()
                ahead()

            def residual(s, t):
                if s > 1:
                    dve.wait_ge(tokens_ready, TT * (s - 1))
                for n in range(2):
                    st.add(v.scalar_tensor_tensor(out=work[:, t, n * HALF:(n + 1) * HALF],
                                                  in0=tokens[:, t, n * HALF:(n + 1) * HALF], scalar=ALPHA,
                                                  in1=bank[SUM_BANKS[t][n]][:, :], op0=ALU.mult, op1=ALU.add))
                st.wait()

            def normalise(s, t):
                for n in range(2):
                    st.add(v.bn_stats(stats[:, t, n, :], work[:, t, n * HALF:(n + 1) * HALF]))
                st.wait()
                v.bn_aggr(mv[:, t, :], stats[:, t].rearrange("p a b -> p (a b)")).then_inc(var_ready, 1)
                dve.wait_ge(std_ready, TT * (s - 1) + t + 1)
                dve.wait_ge(var_ready, TT * (s - 1) + t + 1)
                st.then(v.reciprocal(rstd[:, t, 1:2], rstd[:, t, 0:1]))
                v.tensor_scalar(work[:, t, :], work[:, t, :], mv[:, t, 0:1], rstd[:, t, 1:2],
                                ALU.subtract, ALU.mult).then_inc(xhat_ready, 1)

            def dense():
                def mul(c):
                    dve.wait_ge(dsilu, c + 1)
                    if c >= 2:
                        dve.wait_ge(dlo_ready, c - 1)
                    v.tensor_tensor(dh[:, c % 2, :], dsg[:, c % 2, :], bank[(2, 3, 6, 7)[c % 4]][:, T:2 * T],
                                    ALU.mult).then_inc(dh_ready, 1)

                def hidden_lo(c):
                    dve.wait_ge(dhi_ready, c + 1)
                    v.tensor_tensor(dh_lo[:, c // 4 % 2, c % 4, :], dh[:, c % 2, :],
                                    dh_hi[:, c // 4 % 2, c % 4, :].bitcast(F32), ALU.subtract).then_inc(dlo_ready, 1)

                for kind, b, half in DENSE_ORDER:
                    ahead()
                    if kind == "u" and half == (1 if b < DENSE_BLOCKS - 1 else 0):
                        c0, n = 4 * b, dense_chunks(b)
                        mul(c0)
                        for c in range(c0 + 1, c0 + n):
                            mul(c)
                            hidden_lo(c - 1)
                        hidden_lo(c0 + n - 1)

            def norm(s):
                for t in range(TT):
                    dve.wait_ge(*sum_event(s, t))
                    residual(s, t)
                    normalise(s, t)
                turn(s)

            for _ in range(AHEAD):
                ahead()
            turn(0)
            for l in range(LAYERS):
                mixer(l)
                norm(2 * l + 1)
                if l == 0:
                    dense()
                    norm(2)

            dve.wait_ge(logit_mm, 1)
            dve.wait_ge(router_in, 32)
            for t in range(TT):
                st.add(v.tensor_tensor(logit[:, t, :], bank[4][:, t * E:(t + 1) * E], rout_b[:], ALU.add))
            st.wait()
            st.then(v.tensor_reduce(top, logit, AX_X, ALU.max))
            v.tensor_scalar(top, top, -1.0, None, ALU.mult).then_inc(logit_ready, 1)
            for t in range(TT):
                lj = logit[:, t, :].unsqueeze(1).to_broadcast([P, E, E])
                le = logit[:, t, :].unsqueeze(2).to_broadcast([P, E, E])
                st.add(v.tensor_tensor(gt[:, t], lj, le, ALU.is_gt))
                st.add(v.tensor_tensor(eq[:, t], lj, le, ALU.is_equal))
            st.wait()
            lt = cst[:, C_LT:C_LT + E * E].rearrange("p (e j) -> p e j", e=E)
            for t in range(TT):
                st.add(v.tensor_tensor(eq[:, t], eq[:, t], lt, ALU.mult))
            st.wait()
            st.then(v.tensor_tensor(gt.rearrange("p t e j -> p (t e j)"), gt.rearrange("p t e j -> p (t e j)"),
                                    eq.rearrange("p t e j -> p (t e j)"), ALU.add))
            st.then(v.tensor_reduce(rank.rearrange("p t e -> p (t e)"), gt.rearrange("p t e j -> p (t e) j"),
                                    AX_X, ALU.add))
            v.tensor_scalar(chosen.rearrange("p t e -> p (t e)"), rank.rearrange("p t e -> p (t e)"),
                            TOP_K - 0.5, None, ALU.is_lt).then_inc(chosen_ready, 1)
            dve.wait_ge(chosen_ready, 1)
            dve.wait_ge(expo_ready, 2)
            st.then(v.tensor_tensor(comb, expo, chosen, ALU.mult))
            st.then(v.tensor_reduce(esum, comb, AX_X, ALU.add))
            st.then(v.reciprocal(esum, esum))
            for t in range(TT):
                st.add(v.tensor_scalar(comb[:, t, :], comb[:, t, :], esum[:, t:t + 1], None, ALU.mult))
            dve.wait_ge(pos_mm, 1)
            st.add(v.tensor_copy(count, bank[4][:, 4 * E:5 * E]))
            st.then(v.scalar_tensor_tensor(out=posm.rearrange("p t e -> p (t e)"), in0=bank[4][:, 2 * E:4 * E],
                                           scalar=1.0, in1=chosen.rearrange("p t e -> p (t e)"),
                                           op0=ALU.add, op1=ALU.mult))
            st.then(v.tensor_scalar(posm, posm, -1.0, None, ALU.add))
            st.add(v.tensor_scalar(flag[:, 0:E], count, CAP + 0.5, None, ALU.is_gt))
            st.then(v.tensor_scalar(flag[:, E:], count, 2 * CAP + 0.5, None, ALU.is_gt))
            st.add(v.tensor_reduce(n_over_f, flag, AX_X, ALU.add))
            st.then(v.tensor_tensor_scan(frank, cst[:, C_ONES:C_ONES + 2 * E], flag, 0.0, ALU.mult, ALU.add))
            for j in range(MAX_OVER):
                st.then(v.scalar_tensor_tensor(out=fsel, in0=frank, scalar=float(j + 1), in1=flag,
                                               op0=ALU.is_equal, op1=ALU.mult))
                for col, o in ((C_CE, over_e), (C_CT, over_t)):
                    st.then(v.tensor_tensor(ftmp, fsel, cst[:, col:col + 2 * E], ALU.mult))
                    st.then(v.tensor_reduce(o[:, j:j + 1], ftmp, AX_X, ALU.add))
            st.add(v.tensor_copy(over_int[:, 0:MAX_OVER], over_e))
            v.tensor_copy(over_int[:, MAX_OVER:], n_over_f).then_inc(table_ready, 1)
            for t in range(TT):
                st.add(v.tensor_copy(item_tab[:, 0:E, t], posm[:, t, :]))
                st.add(v.tensor_copy(item_tab[:, 0:E, 2 + t], comb[:, t, :]))
            st.add(v.memset(item_tab[:, MAX_ITEMS, :], -1.0))
            st.wait()
            for j in range(MAX_OVER):
                st.then(v.tensor_scalar(fsel[:, 0:E], cst[:, C_CE:C_CE + E], over_e[:, j:j + 1], None, ALU.is_equal))
                for src, c in ((posm, 0), (comb, 2)):
                    for t in range(TT):
                        st.then(v.tensor_tensor(itmp[:, t, :], src[:, t, :], fsel[:, 0:E], ALU.mult))
                    st.then(v.tensor_reduce(item_tab[:, E + j, c:c + 2], itmp, AX_X, ALU.add))
                st.then(v.tensor_scalar(item_tab[:, E + j, 0:2], item_tab[:, E + j, 0:2], over_t[:, j:j + 1], None,
                                        ALU.subtract))
            dve.wait_ge(tokens_ready, TT * 3)
            st.then(v.tensor_scalar(work[:, :, :], tokens[:, :, :], ALPHA, None, ALU.mult))

            BUILD_STEPS = 5

            def build_pick(i):
                bs = Steps(dve, build_steps, BUILD_STEPS * i)
                bs.then(v.tensor_copy(item_cur.unsqueeze(1), item_tab[:, bass.ds(i, 1), :]))
                for t in range(TT):
                    bs.add(v.tensor_scalar(pick[:, t, :], iota, item_cur[:, t:t + 1], None, ALU.is_equal))
                    bs.add(v.tensor_scalar(pickc[:, t, :], iota, item_cur[:, t:t + 1], item_cur[:, 2 + t:3 + t],
                                           ALU.is_equal, ALU.mult))
                assert bs.n == BUILD_STEPS

            def gathered_lo(i, n):
                dve.wait_ge(xghi_ready, 2 * i + n + 1)
                at_x = (slice(None), slice(4 * n, 4 * n + 4))
                v.tensor_tensor(xg_lo[at_x].rearrange("p k c -> p (k c)"), bank[4][:, 0:4 * CAP],
                                xg_hi[at_x].rearrange("p k c -> p (k c)").bitcast(F32),
                                ALU.subtract).then_inc(xglo_ready, 1)

            def add_scattered(i, q):
                t, n = divmod(q, 2)
                dve.wait_ge(scat_mm, 4 * i + q + 1)
                w = work[:, t, n * HALF:(n + 1) * HALF]
                v.tensor_tensor(w, w, bank[4][:, :], ALU.add).then_inc(acc_done, 1)

            def item(i, first=False):
                for u in range(ITEM_UNITS):
                    subtract_lo(MOE_UNIT0 + u + AHEAD, i)
                    if u in STEP_MUL:
                        b = STEP_MUL[u]
                        dve.wait_ge(esilu, i * EXP_BLOCKS + (b + 1))
                        dve.wait_ge(unit_done, i * ITEM_UNITS + (MOE_UNIT0 + u + 1))
                        v.tensor_tensor(eh[0:CAP, b % 2, :], esg[0:CAP, b % 2, :], bank[(3, 7)[b % 2]][0:CAP, :],
                                        ALU.mult).then_inc(eh_ready, 1)
                    if u in STEP_TURN:
                        b = STEP_TURN[u]
                        dve.wait_ge(ehi_ready, i * EXP_BLOCKS + (b + 1))
                        v.tensor_tensor(eh_lo[:, b % 2].rearrange("p j c -> p (j c)"), bank[5][:, 0:4 * CAP],
                                        eh_hi[:, b % 2].rearrange("p j c -> p (j c)").bitcast(F32),
                                        ALU.subtract).then_inc(elo_ready, 1)
                    if u in STEP_SCATTER and not first:
                        add_scattered(i - 1, STEP_SCATTER[u])
                    if u == STEP_SLOTS:
                        dve.wait_ge(st_mm, i + 1)
                        v.tensor_copy(scat[0:CAP, :], bank[4][0:CAP, 0:T]).then_inc(scat_ready, 1)
                    if u == STEP_PICK:
                        build_pick(i + 1)
                    if u in STEP_GATHER:
                        gathered_lo(i + 1, STEP_GATHER[u])

            build_pick(0)
            gathered_lo(0, 0)
            gathered_lo(0, 1)
            item(0, first=True)
            with dve.Fori(1, E) as i:
                item(i)
            n_over = dve.value_load(over_int[0:1, MAX_OVER:MAX_OVER + 1], min_val=0, max_val=MAX_OVER)
            with dve.Fori(0, MAX_OVER) as j:
                with dve.If(j < n_over):
                    item(j + E)
            for q in range(4):
                add_scattered(n_over + (E - 1), q)
            dve.wait_ge(acc_done, 4 * (n_over + E))
            dve.wait_ge(ln_in, 32 * 4)
            for t in range(TT):
                normalise(4, t)
                dve.wait_ge(xhat_ready, TT * 3 + t + 1)
                st.then(v.tensor_tensor(work[:, t, :], work[:, t, :], ln_row[:, 0, :], ALU.mult))
                v.tensor_tensor(tokens[:, t, :], work[:, t, :], ln_row[:, 1, :], ALU.add).then_inc(out_ready, 1)

        @block.tensor
        def _(pe):
            mm = nc.tensor.matmul
            tr = nc.tensor.transpose

            def arrived(n, i=0):
                pe.wait_ge(lo_ready, i * ITEM_UNITS + (n + 1))

            def product(psum, left, right, first, last):
                mm(psum, left[0], right[0], start=first, stop=False)
                mm(psum, left[0], right[1], start=False, stop=False)
                return mm(psum, left[1], right[0], start=False, stop=last)

            def turn(s):
                for t in range(TT):
                    if s == 0:
                        pe.wait_ge(x_in, 16 * TT)
                    else:
                        pe.wait_ge(xhat_ready, TT * (s - 1) + t + 1)
                    src = tokens if s == 0 else work
                    for k in range(DK):
                        last = tr(bank[TURN_BANKS[t][k // 4]][:, (k % 4) * P:(k % 4 + 1) * P],
                                  src[:, t, k * P:(k + 1) * P], ident)
                        if k % 4 == 3:
                            last.then_inc(turned, 1)

            def x_parts(k, c=slice(None)):
                return x_hi[:, k, c], x_lo[:, k, c]

            def mixer(l):
                if l == 0:
                    pe.wait_ge(gatew_ready, 2)
                pe.wait_ge(xf_act, 4 * TT * (2 * l + 1))
                pe.wait_ge(xf_dve, 4 * TT * (2 * l + 1))
                for t in range(TT):
                    for k in range(DK):
                        last = mm(bank[6][0:32 + HEADS, t * P:(t + 1) * P], gate_w[:, l, k, :], xf[:, t, k, :],
                                  start=k == 0, stop=k == DK - 1)
                last.then_inc(gates_mm, 1)
                if l == 0:
                    pe.wait_ge(par_in, 16 * 8)
                    tr(bank[4][:, 0:96], par_rows[:], ident[0:96, 0:96]).then_inc(par_turned, 1)
                    tr(bank[5][:, 0:64], par_rows2[:], ident[0:64, 0:64]).then_inc(par_turned, 1)
                pe.wait_ge(xlo_ready, 2 * TT * (2 * l + 1))

                def chunks(kind, half, free=None):
                    arrived(mixer_unit(l, kind, half))
                    hi, lo = parts_of(mixer_unit(l, kind, half), FBLK)
                    for c in range(4):
                        if half == 0 and free is not None:
                            pe.wait_ge(*free(c))
                        for kk in range(4):
                            w = (slice(None), kk, slice(c * P, (c + 1) * P))
                            last = product(bank[c][:, 0:T], (hi[w], lo[w]), x_parts(4 * half + kk),
                                           half == 0 and kk == 0, half == 1 and kk == 3)
                        if c == 3:
                            last.then_inc(unit_done, 1)
                        elif half == 1:
                            last.then_inc(chunk_done, 1)

                chunks("q", 0)
                chunks("q", 1)
                chunks("k", 0, lambda c: (zqk_ready, 8 * l + c + 1))
                chunks("k", 1)
                if l == 0:
                    pe.wait_ge(par_ready, 2)
                for half in range(2):
                    n = mixer_unit(l, "v", half)
                    arrived(n)
                    w = parts_of(n, FBLK)
                    for t in range(TT):
                        for kk in range(4):
                            last = product(bank[4 + t][:, :], x_parts(4 * half + kk, slice(t * P, (t + 1) * P)),
                                           (w[0][:, kk, :], w[1][:, kk, :]), half == 0 and kk == 0,
                                           half == 1 and kk == 3)
                        if t == TT - 1:
                            last.then_inc(unit_done, 1)
                        elif half == 1:
                            last.then_inc(chunk_done, 1)
                pe.wait_ge(rows_ready, l + 1)
                for n, r in enumerate((r_i, r_m)):
                    for t in range(TT):
                        c = (n * TT + t) * HEADS
                        last = tr(bank[6][:, c:c + HEADS], r[:, t * P:(t + 1) * P], ident[0:HEADS, 0:HEADS])
                last.then_inc(cols_mm, 1)
                for h in range(HEADS):
                    if h == 2:
                        pe.wait_ge(v_ready, TT * l + 1)
                    last = mm(bank[(7, 4)[h // 2]][:, (h % 2) * T:(h % 2 + 1) * T],
                              cst[0:HEADS, C_SEL + h * P:C_SEL + (h + 1) * P], r_negm, start=True, stop=True)
                    if h % 2:
                        last.then_inc(bcast_mm, 1)
                chunks("p", 0, lambda c: (zqk_ready, 8 * l + 4 + c + 1))
                chunks("p", 1)
                pe.wait_ge(qk_ready, 8 * (l + 1))
                pe.wait_ge(v_ready, TT * (l + 1))
                pe.wait_ge(cols_ready, l + 1)
                pe.wait_ge(arg_ready, HEADS * (l + 1))
                for h, n in enumerate(SCORE_BANKS):
                    mm(bank[n][:, 0:T], qkT[:, HEADS + h, 0:P], qkT[:, h, :], start=True, stop=True)
                    mm(bank[n][:, T:T + P], qkT[:, HEADS + h, P:T], qkT[:, h, P:T], start=True, stop=True) \
                        .then_inc(score_mm, 1)
                chunks("o", 0, lambda c: (u_ready, GROUPS * l + c + 1))
                pe.wait_ge(w_ready, HEADS * (l + 1))
                wts = [[(decay[:, h, 0:P], 0)] for h in range(HEADS)], \
                      [[(decay[:, h, P:T], 0), (decay[:, h, T:T + P], 1)] for h in range(HEADS)]
                for t in range(TT):
                    for h in range(HEADS):
                        for w, s in wts[t][h]:
                            mm(bank[4][:, t * HEADS + h:t * HEADS + h + 1], w, ones[:, 0:1],
                               start=s == 0, stop=s == t)
                for t in range(TT):
                    for h in range(HEADS):
                        for w, s in wts[t][h]:
                            last = mm(bank[PV_BANKS[t]][:, h * DH:(h + 1) * DH], w, v_sb[:, s, h * DH:(h + 1) * DH],
                                      start=s == 0, stop=s == t)
                    last.then_inc(pv_mm, 1)
                chunks("o", 1)
                pe.wait_ge(poolw_in, 16 * (l + 1))
                pe.wait_ge(sig_ready, HEADS * (l + 1))
                for gr in range(GROUPS):
                    pe.wait_ge(pool_ready, GROUPS * l + gr + 1)
                    last = mm(bank[2 + gr // 2][:, (gr % 2) * T:(gr % 2 + 1) * T], pool_ws[:, gr, :],
                              ubuf[:, gr, 16:], start=True, stop=True)
                    if gr % 2:
                        last.then_inc(pooly_mm, 1)

                def project(q):
                    n = mixer_unit(l, "w", q)
                    arrived(n)
                    w = parts_of(n, D)
                    for t in range(TT):
                        for half in range(2):
                            for kk in range(2):
                                y = (slice(None), 2 * q + kk, slice(t * P, (t + 1) * P))
                                r = (slice(None), kk, slice(half * HALF, (half + 1) * HALF))
                                last = product(bank[SUM_BANKS[t][half]][:, :], (y_hi[y], y_lo[y]),
                                               (w[0][r], w[1][r]), q == 0 and kk == 0, q == 3 and kk == 1)
                        if t == TT - 1:
                            last.then_inc(unit_done, 1)
                        elif q == 3:
                            last.then_inc(chunk_done, 1)

                pe.wait_ge(ylo_ready, 2 * l + 1)
                pe.wait_ge(rden_ready, l + 1)
                project(0)
                for t in range(TT):
                    pe.wait_ge(h_ready, HEADS * (TT * l + t + 1))
                    for h in range(HEADS):
                        last = tr(bank[PV_BANKS[t]][:, h * P:(h + 1) * P], h_norm[:, t, h * DH:(h + 1) * DH], ident)
                    last.then_inc(ht_mm, 1)
                project(1)
                pe.wait_ge(ylo_ready, 2 * l + 2)
                project(2)
                project(3)

            def dense():
                pe.wait_ge(xlo_ready, 2 * TT * 2)

                def gate_up(b):
                    n = dense_chunks(b)
                    whole = b == DENSE_BLOCKS - 1
                    for kind in "gu":
                        cols_ = slice(0, T) if kind == "g" else slice(T, 2 * T)
                        for half in range(1 if whole else 2):
                            unit = dense_unit(kind, b, half)
                            arrived(unit)
                            hi, lo = parts_of(unit, n * P)
                            ks = range(DK) if whole else range(4 * half, 4 * half + 4)
                            for j in range(n):
                                c = 4 * b + j
                                if kind == "g" and half == 0 and c >= 4:
                                    pe.wait_ge(dh_ready, c - 3)
                                for kk, k in enumerate(ks):
                                    w = (slice(None), kk, slice(j * P, (j + 1) * P))
                                    last = product(bank[(2, 3, 6, 7)[c % 4]][:, cols_], (hi[w], lo[w]), x_parts(k),
                                                   k == 0, k == DK - 1)
                                if j == n - 1:
                                    last.then_inc(unit_done, 1)
                                elif kind == "u" and (whole or half == 1):
                                    last.then_inc(chunk_done, 1)

                def down(b):
                    final = b == DENSE_BLOCKS - 1
                    pe.wait_ge(dlo_ready, 4 * b + dense_chunks(b))
                    for half in range(1 if final else 2):
                        unit = dense_unit("d", b, half)
                        arrived(unit)
                        w = parts_of(unit, D)
                        for t in range(TT):
                            for n in range(2):
                                for jj in range(2):
                                    j = 2 * half + jj
                                    y = (slice(None), b % 2, j, slice(t * P, (t + 1) * P))
                                    r = (slice(None), jj, slice(n * HALF, (n + 1) * HALF))
                                    last = product(bank[SUM_BANKS[t][n]][:, :], (dh_hi[y], dh_lo[y]),
                                                   (w[0][r], w[1][r]), b == 0 and j == 0, final and jj == 1)
                            if t == TT - 1:
                                last.then_inc(unit_done, 1)
                            elif final:
                                last.then_inc(chunk_done, 1)

                for b in range(DENSE_BLOCKS):
                    gate_up(b)
                    if b:
                        down(b - 1)
                down(DENSE_BLOCKS - 1)

            pe.wait_ge(consts_in, 16)
            turn(0)
            mixer(0)
            turn(1)
            dense()
            turn(2)
            mixer(1)
            turn(3)

            pe.wait_ge(router_in, 32)
            pe.wait_ge(xf_act, 4 * TT * 4)
            pe.wait_ge(xf_dve, 4 * TT * 4)
            for t in range(TT):
                for k in range(DK):
                    last = mm(bank[4][:, t * E:(t + 1) * E], xf[:, t, k, :], rout_w[:, k, :],
                              start=k == 0, stop=k == DK - 1)
            last.then_inc(logit_mm, 1)
            pe.wait_ge(chosen_ready, 1)
            mm(bank[4][:, 2 * E:3 * E], tri, chosen[:, 0, :], start=True, stop=True)
            mm(bank[4][:, 3 * E:4 * E], ones, chosen[:, 0, :], start=True, stop=False)
            mm(bank[4][:, 3 * E:4 * E], tri, chosen[:, 1, :], start=False, stop=True)
            mm(bank[4][:, 4 * E:5 * E], ones, chosen[:, 0, :], start=True, stop=False)
            mm(bank[4][:, 4 * E:5 * E], ones, chosen[:, 1, :], start=False, stop=True).then_inc(pos_mm, 1)

            def gather(i, n):
                if n == 0:
                    pe.wait_ge(build_steps, 5 * (i + 1))
                else:
                    pe.wait_ge(xglo_ready, 2 * i + 1)
                for k in range(4 * n, 4 * n + 4):
                    for t in range(TT):
                        last = mm(bank[4][:, (k % 4) * CAP:(k % 4 + 1) * CAP],
                                  tokens[:, t, k * P:(k + 1) * P], pick[:, t, :], start=t == 0, stop=t == TT - 1)
                last.then_inc(gather_mm, 1)

            def scatter(i, q):
                t, n = divmod(q, 2)
                if q == 0:
                    pe.wait_ge(ysb_ready, 2 * i + 2)
                    pe.wait_ge(scat_ready, i + 1)
                else:
                    pe.wait_ge(acc_done, 4 * i + q)
                mm(bank[4][:, :], scat[0:CAP, t * P:(t + 1) * P], y_sb[0:CAP, n * HALF:(n + 1) * HALF],
                   start=True, stop=True).then_inc(scat_mm, 1)

            def item(i, first=False):
                pe.wait_ge(xglo_ready, 2 * i + 2)
                for u, (kind, b, half) in enumerate(ITEM_ORDER):
                    n = MOE_UNIT0 + u
                    arrived(n, i)
                    w = parts_of(n, D if kind == "d" else FBLK)
                    if kind == "d":
                        if half == 0:
                            pe.wait_ge(elo_ready, i * EXP_BLOCKS + (b + 1))
                        if b == 0 and half == 0 and not first:
                            pe.wait_ge(ysb_ready, 2 * i)
                        for hw in range(2):
                            for jj in range(2):
                                j = 2 * half + jj
                                r = (slice(None), jj, slice(hw * HALF, (hw + 1) * HALF))
                                last = product(bank[hw][0:CAP, :], (eh_hi[:, b % 2, j, :], eh_lo[:, b % 2, j, :]),
                                               (w[0][r], w[1][r]), b == 0 and j == 0,
                                               b == EXP_BLOCKS - 1 and j == 3)
                    else:
                        psum = bank[((2, 3), (6, 7))[b % 2][kind == "u"]][0:CAP, :]
                        for kk in range(4):
                            k = 4 * half + kk
                            last = product(psum, (xg_hi[:, k, :], xg_lo[:, k, :]), (w[0][:, kk, :], w[1][:, kk, :]),
                                           k == 0, k == DK - 1)
                    last.then_inc(unit_done, 1)
                    if u in STEP_TURN:
                        tb = STEP_TURN[u]
                        pe.wait_ge(eh_ready, i * EXP_BLOCKS + (tb + 1))
                        for j in range(4):
                            last = tr(bank[5][:, j * CAP:(j + 1) * CAP], eh[0:CAP, tb % 2, j * P:(j + 1) * P],
                                      ident[0:CAP, 0:CAP])
                        last.then_inc(eturn_mm, 1)
                    if u in STEP_SCATTER and not first:
                        scatter(i - 1, STEP_SCATTER[u])
                    if u == STEP_SLOTS:
                        if not first:
                            pe.wait_ge(acc_done, 4 * i)
                        for t in range(TT):
                            last = tr(bank[4][0:CAP, t * P:(t + 1) * P], pickc[:, t, :], ident)
                        last.then_inc(st_mm, 1)
                    if u in STEP_GATHER:
                        if STEP_GATHER[u] == 0:
                            pe.wait_ge(scat_ready, i + 1)
                        gather(i + 1, STEP_GATHER[u])

            pe.wait_ge(tokens_ready, TT * 3)
            gather(0, 0)
            gather(0, 1)
            item(0, first=True)
            with pe.Fori(1, E) as i:
                item(i)
            n_over = pe.value_load(over_int[0:1, MAX_OVER:MAX_OVER + 1], min_val=0, max_val=MAX_OVER)
            with pe.Fori(0, MAX_OVER) as j:
                with pe.If(j < n_over):
                    item(j + E)
            last_item = n_over + (E - 1)
            pe.wait_ge(xglo_ready, 2 * last_item + 4)
            for q in range(4):
                scatter(last_item, q)


def constant_table():
    c = np.zeros((P, C_END), np.float32)
    c[:, C_ID:C_ID + P] = np.eye(P)
    c[:, C_TRI:C_TRI + P] = np.triu(np.ones((P, P)), 1)
    c[:, C_ONES:C_ONES + T] = 1.0
    c[:, C_IOTA:C_IOTA + P] = np.arange(P)
    c[:, C_LT:C_LT + E * E] = np.tril(np.ones((E, E)), -1).reshape(-1)
    for g in range(GROUPS):
        c[:, C_INV + 16 * g:C_INV + 16 * g + 16] = 1.0 / np.minimum(np.arange(16) + 1, 2 << g)
    c[:, C_CE:C_CE + 2 * E] = np.tile(np.arange(E), 2)
    c[:, C_CT:C_CT + 2 * E] = np.repeat([CAP, 2 * CAP], E)
    for h in range(HEADS):
        c[h, C_SEL + h * P:C_SEL + (h + 1) * P] = 1.0
    return c


_INS = ["x", "w_in", "b_gates", "conv_w", "conv_b", "pool_w", "pool_scale", "mlstm_g", "w_out", "ln1_g", "ln1_b",
        "ln2_g", "ln2_b", "wg_dense", "wu_dense", "wd_dense", "w_router", "b_router", "wg_exp", "wu_exp", "wd_exp"]


def kernel(**inputs):
    import concourse.bacc as bacc
    from concourse.bass_utils import run_bass_kernel_spmd

    nc = bacc.Bacc("TRN2", target_bir_lowering=False, num_devices=1)
    arrays, args = {}, []
    for name in _INS:
        a = np.ascontiguousarray(inputs[name])
        arrays[f"in_{name}"] = a
        args.append(nc.dram_tensor(f"in_{name}", a.shape, mybir.dt.from_np(a.dtype), kind="ExternalInput").ap())
    c = constant_table()
    arrays["consts"] = c
    args.append(nc.dram_tensor("consts", c.shape, F32, kind="ExternalInput").ap())
    out = nc.dram_tensor("out", (1, T, D), F32, kind="ExternalOutput").ap()
    build(nc, *args, out)
    r = run_bass_kernel_spmd(nc, [arrays], core_ids=[0])
    return r.results[0]["out"]
```

```python
from contextlib import ExitStack

import numpy as np

import concourse.bass as bass
from concourse import mybir

F32 = mybir.dt.float32
F32R = mybir.dt.float32r
I32 = mybir.dt.int32
ALU = mybir.AluOpType
ACT = mybir.ActivationFunctionType
AX_X = mybir.AxisListType.X

P = 128
T = 256
TT = T // P
D = 1024
DK = D // P
HALF = 512
LAYERS = 2
HEADS = 4
DH = 128
GROUPS = 4
TAPS = 4
PAD = TAPS - 1
D_POOL = 512
D_MLSTM = 512
GATE_COL = D_POOL + 4 * D_MLSTM
F_DENSE = 2816
F_EXP = 3584
E = 8
TOP_K = 2
FBLK = 512
DENSE_BLOCKS = -(-F_DENSE // FBLK)
EXP_BLOCKS = F_EXP // FBLK
ALPHA = (2 * LAYERS) ** 0.25
EPS = 1e-5
QK_SCALE = DH ** -0.5

CAP = 104
MAX_OVER = (TOP_K * T) // (CAP + 1)
MAX_ITEMS = E + MAX_OVER

UNIT = 2048
RAW = 7
RING = RAW + 2
SPLIT = 3
AHEAD = SPLIT - 1
MIXER_KINDS = [(k, h) for k in "qkvpo" for h in range(2)] + [("w", h) for h in range(4)]
MIXER_UNITS = len(MIXER_KINDS)
DENSE_CHUNKS = F_DENSE // P
DENSE_LAST = DENSE_CHUNKS - 4 * (DENSE_BLOCKS - 1)
assert DENSE_LAST == 2
ITEM_UNITS = 6 * EXP_BLOCKS
assert ITEM_UNITS % SPLIT == 0 and MAX_OVER * (CAP + 1) <= TOP_K * T


def block_order(blocks):
    out = []
    for b in range(blocks):
        out += [("g", b), ("u", b)]
        if b:
            out.append(("d", b - 1))
    return out + [("d", blocks - 1)]


DENSE_ORDER = [(k, b, h) for k, b in block_order(DENSE_BLOCKS) for h in range(2 if b < DENSE_BLOCKS - 1 else 1)]
ITEM_ORDER = [(k, b, h) for k, b in block_order(EXP_BLOCKS) for h in range(2)]
DENSE_UNITS = len(DENSE_ORDER)
MIXER_UNIT0 = [0, MIXER_UNITS + DENSE_UNITS]
DENSE_UNIT0 = MIXER_UNITS
MOE_UNIT0 = 2 * MIXER_UNITS + DENSE_UNITS


def mixer_unit(l, kind, half):
    return MIXER_UNIT0[l] + MIXER_KINDS.index((kind, half))


def dense_unit(kind, b, half=0):
    return DENSE_UNIT0 + DENSE_ORDER.index((kind, b, half))


def dense_chunks(b):
    return min(4, DENSE_CHUNKS - 4 * b)


STEP_SILU = {ITEM_ORDER.index(("g", b, 1)): b for b in range(EXP_BLOCKS)}
STEP_MUL = {ITEM_ORDER.index(("u", b, 1)): b for b in range(EXP_BLOCKS)}
STEP_TURN = {ITEM_ORDER.index(("u", b, 1)) + (2 if b < EXP_BLOCKS - 1 else 1): b for b in range(EXP_BLOCKS)}
STEP_SCATTER = {7: 0, 9: 1, 11: 2, 13: 3}
STEP_SLOTS = 15
STEP_TABLES, STEP_SUMS = 4, 9
STEP_PICK = 20
STEP_GATHER = {ITEM_ORDER.index(("d", EXP_BLOCKS - 3, 1)): 0,
               ITEM_ORDER.index(("g", EXP_BLOCKS - 1, 0)): 1}
STEP_TAKE = {ITEM_ORDER.index(("u", EXP_BLOCKS - 1, 1)): 0,
             ITEM_ORDER.index(("d", EXP_BLOCKS - 2, 0)): 1}

C_ID, C_TRI, C_ONES = 0, 128, 256
C_IOTA = C_ONES + T
C_LT = C_IOTA + P
C_INV = C_LT + E * E
C_CE = C_INV + GROUPS * 16
C_CT = C_CE + 2 * E
C_SEL = C_CT + 2 * E
C_END = C_SEL + HEADS * P

R_LN = {(1, "g"): 0, (1, "b"): 16, (2, "g"): 32, (2, "b"): 48}
R_CONVB, R_POOLS, R_MG, R_CONVW = 64, 80, 88, 96


class Steps:

    def __init__(self, eng, sem, base=0):
        self.eng, self.sem, self.base, self.n = eng, sem, base, 0

    def add(self, ins):
        ins.then_inc(self.sem, 1)
        self.n += 1

    def wait(self):
        self.eng.wait_ge(self.sem, self.base + self.n)

    def then(self, ins):
        self.add(ins)
        self.wait()


def build(nc, x, w_in, b_gates, conv_w, conv_b, pool_w, pool_scale, mlstm_g, w_out, ln1_g, ln1_b, ln2_g, ln2_b,
          wg_dense, wu_dense, wd_dense, w_router, b_router, wg_exp, wu_exp, wd_exp, consts, out):
    with ExitStack() as ctx:
        def sb(name, shape, dt=F32):
            return ctx.enter_context(nc.sbuf_tensor(name, shape, dt))

        def sem(name):
            return ctx.enter_context(nc.semaphore(name))

        raw = sb("raw", [P, RAW, UNIT])
        w_hi = sb("w_hi", [P, SPLIT, UNIT], F32R)
        w_lo = sb("w_lo", [P, SPLIT, UNIT], F32R)
        tokens = sb("tokens", [P, TT, D])
        work = sb("work", [P, TT, D])
        x_hi = sb("x_hi", [P, DK, T], F32R)
        x_lo = sb("x_lo", [P, DK, T], F32R)
        parts = sb("parts", [P, 2, 2048], F32R)
        ln_row = sb("ln_row", [P, 2, D])
        cst = sb("cst", [P, C_END])
        par = sb("par", [P, 160])
        gate_w = sb("gate_w", [P, LAYERS, DK, 32 + HEADS])
        gate_raw = sb("gate_raw", [P, LAYERS, DK, 2 * HEADS])
        gate_b = sb("gate_b", [P, LAYERS])
        pool_ws = sb("pool_ws", [P, GROUPS, DH])
        rout_w = sb("rout_w", [P, DK, E])
        rout_b = sb("rout_b", [P, E])
        small = sb("small", [P, 2])
        stats = sb("stats", [P, TT, 2, 6])
        mv = sb("mv", [P, TT, 2])
        rstd = sb("rstd", [P, TT, 2])

        ARENA = 9080
        arena = sb("arena", [P, ARENA])
        at = [0]

        def shaped(v, shape):
            if len(shape) == 1:
                return v
            names = "abcd"[:len(shape)]
            return v.rearrange(f"p ({' '.join(names)}) -> p {' '.join(names)}",
                               **{k: s for k, s in zip(names, shape)})

        def carve(shape, start=None):
            if start is not None:
                at[0] = start
            n = int(np.prod(shape))
            v = arena[:, at[0]:at[0] + n]
            at[0] += n
            assert at[0] <= ARENA
            return shaped(v, shape)

        xf = carve([TT, DK, P], 0)
        zqk = carve([8, PAD + T], 0)
        decay = shaped(arena[:, 0:HEADS * (T + P)], [HEADS, T + P])
        ubuf = carve([GROUPS, 16 + T])
        h_norm = [arena[:, at[0] - GROUPS * (16 + T):][:, 0:D_MLSTM],
                  arena[:, HEADS * (T + P):HEADS * (T + P) + D_MLSTM]]
        POOL_CONVS = (3, 6)
        DVE_CONVS = tuple(c for c in range(8) if c not in POOL_CONVS)
        acc_pool, prod_pool = ubuf[:, 0:2, 16:], ubuf[:, 2, 16:]
        ptmp = carve([2, 16 + T])
        conv_acc = shaped(arena[:, at[0] - 2 * (16 + T):at[0] - 2 * 16], [2, T])
        v_sb = carve([TT, D_MLSTM])
        par_rows, par_rows2 = v_sb[0:96, 0, 0:P], v_sb[0:64, 1, 0:P]
        sigT = carve([HEADS, T])
        rows = carve([5, T])
        qkT = carve([8, T])
        yT = qkT
        r_i, r_f, r_l, r_negm, r_m = (rows[0:HEADS, n, :] for n in range(5))
        y_hi, y_lo = (shaped(parts[:, n, :], [8, T]) for n in range(2))
        cols = sb("cols", [P, 2, TT, HEADS])
        guard = sb("guard", [P, TT, HEADS])
        rden = sb("rden", [P, TT, HEADS])
        hstats = sb("hstats", [P, TT, HEADS, 6])
        hmv = sb("hmv", [P, TT, HEADS, 2])
        hstd = sb("hstd", [P, TT, HEADS])
        hrstd = sb("hrstd", [P, TT, HEADS])
        dsg = carve([2, T], 2048)
        dh = carve([2, T])
        dh_hi, dh_lo = (shaped(parts[:, n, :], [2, 4, T]) for n in range(2))
        esg = carve([2, FBLK], 2048)
        eh = carve([2, FBLK])
        XG = DK * CAP
        xg_hi, xg_lo = (shaped(parts[:, n, 0:XG], [DK, CAP]) for n in range(2))
        eh_hi, eh_lo = (shaped(parts[:, n, XG:XG + 8 * CAP], [2, 4, CAP]) for n in range(2))
        y_sb = carve([D])
        scat = carve([T])
        pick = carve([TT, CAP])
        pickc = carve([TT, CAP])
        logit = carve([TT, E])
        gt = carve([TT, E, E])
        eq = carve([TT, E, E])
        rank = carve([TT, E])
        chosen = carve([TT, E])
        top = carve([TT])
        expo = carve([TT, E])
        esum = carve([TT])
        comb = carve([TT, E])
        posm = carve([TT, E])
        count = carve([E])
        flag = carve([2 * E])
        frank = carve([2 * E])
        fsel = carve([2 * E])
        ftmp = carve([2 * E])
        over_e = carve([MAX_OVER])
        over_t = carve([MAX_OVER])
        n_over_f = carve([1])
        item_tab = carve([MAX_ITEMS + 1, 4])
        item_cur = carve([4])
        itmp = carve([TT, E])
        over_int = sb("over_int", [P, MAX_OVER + 1], I32)

        bank = [ctx.enter_context(nc.psum_tensor(f"bank{n}", [P, HALF], F32)) for n in range(8)]

        ident = cst[:, C_ID:C_ID + P]
        tri = cst[:, C_TRI:C_TRI + P]
        ones = cst[:, C_ONES:C_ONES + P]
        ones_t = cst[0:HEADS, C_ONES:C_ONES + T]
        iota = cst[:, C_IOTA:C_IOTA + CAP]
        eps_col = small[:, 1:2]

        landed = [sem(f"landed{n}") for n in range(RAW)]
        fetched = [sem(f"fetched{n}") for n in range(RING)]
        x_in = [sem(f"x_in{t}") for t in range(TT)]
        ident_in, consts_in, par_in, gatew_in, gateb_in, poolw_in, router_in, ln_in, out_done = map(sem, (
            "ident_in", "consts_in", "par_in", "gatew_in", "gateb_in", "poolw_in", "router_in", "ln_in", "out_done"))
        hi_ready, lo_ready = map(sem, ("hi_ready", "lo_ready"))
        unit_done, chunk_done, par_turned, turned, gates_mm, cols_mm, bcast_mm, score_mm, pooly_mm, pv_mm, ht_mm, \
            logit_mm, pos_mm, count_mm, gather_mm, eturn_mm, scat_mm, st_mm, half_mm = map(sem, (
                "unit_done", "chunk_done", "par_turned", "turned", "gates_mm", "cols_mm", "bcast_mm", "score_mm",
                "pooly_mm", "pv_mm", "ht_mm", "logit_mm", "pos_mm", "count_mm", "gather_mm", "eturn_mm", "scat_mm",
                "st_mm", "half_mm"))
        xf_act, xhi_ready, gate_i, gate_e, gate_l, zqk_ready, qk_ready, u_ready, sig_ready, decay_ready, \
            guard_ready, hstd_ready, yhi_ready, std_ready, dsilu, dhi_ready, esilu, ehi_ready, xghi_ready, \
            expo_ready, ysb_ready = map(sem, (
                "xf_act", "xhi_ready", "gate_i", "gate_e", "gate_l", "zqk_ready", "qk_ready", "u_ready",
                "sig_ready", "decay_ready", "guard_ready", "hstd_ready", "yhi_ready", "std_ready", "dsilu",
                "dhi_ready", "esilu", "ehi_ready", "xghi_ready", "expo_ready", "ysb_ready"))
        par_ready, xf_dve, xlo_ready, absf_ready, rows_ready, conv_ready, v_ready, cols_ready, arg_ready, w_ready, \
            ypool_ready, rden_ready, hvar_ready, h_ready, ym_ready, ylo_ready, var_ready, xhat_ready, dh_ready, \
            dlo_ready, logit_ready, chosen_ready, eh_ready, elo_ready, xglo_ready, scat_ready, \
            acc_done, out_ready, steps, flags_ready, pick_ready, pickc_ready, cur_ready = map(sem, (
                "par_ready", "xf_dve", "xlo_ready", "absf_ready", "rows_ready", "conv_ready", "v_ready",
                "cols_ready", "arg_ready", "w_ready", "ypool_ready", "rden_ready", "hvar_ready", "h_ready",
                "ym_ready", "ylo_ready", "var_ready", "xhat_ready", "dh_ready", "dlo_ready", "logit_ready",
                "chosen_ready", "eh_ready", "elo_ready", "xglo_ready", "scat_ready", "acc_done",
                "out_ready", "steps", "flags_ready", "pick_ready", "pickc_ready", "cur_ready"))
        small_ready, gatew_zero, gatew_ready, pool_steps, convp_ready, pool_ready, mask_ready, tokens_ready, \
            table_ready = map(sem, ("small_ready", "gatew_zero", "gatew_ready", "pool_steps", "convp_ready",
                                    "pool_ready", "mask_ready", "tokens_ready", "table_ready"))

        x_d = x.rearrange("b (t p) d -> p (b t) d", p=P)
        out_d = out.rearrange("b (t p) d -> p (b t) d", p=P)

        def par_col(name, layer, k):
            if name in R_LN:
                c = R_LN[name] + DK * layer + k
            elif name == "conv_b":
                c = R_CONVB + 8 * layer + k
            elif name == "pool_scale":
                c = R_POOLS + 4 * layer + k
            elif name == "mlstm_g":
                c = R_MG + 4 * layer + k
            else:
                c = R_CONVW + (layer * TAPS + name[1]) * 8 + k
            return par[:, c:c + 1]

        SUM_BANKS = [(0, 1), (4, 5)]
        TURN_BANKS = [(2, 3), (6, 7)]
        NORM = {1: (1, 0), 2: (2, 0), 3: (1, 1), 4: (2, 1)}

        Y_PARTS = [(slice(None), slice(0, 2)), (slice(None), slice(2, 4))] + \
                  [(slice(None), slice(GROUPS, 8), slice(t * P, (t + 1) * P)) for t in range(TT)]
        SCORE_BANKS = (5, 6, 7, 4)
        PV_BANKS = (7, 6)
        POOL_BANKS = (5, 2)
        GATHER_BANKS = (bank[4], bank[6])
        TAIL_BANKS = (2, 3, 6, 7)

        def rows_of(w, r0, n):
            return w[r0:r0 + n * P, :].rearrange("(k p) n -> p k n", p=P)

        def mixer_source(l, kind, half):
            if kind == "w":
                return rows_of(w_out[l], 2 * P * half, 2)
            c0 = {"p": 0, "q": D_POOL, "k": D_POOL + D_MLSTM, "v": D_POOL + 2 * D_MLSTM,
                  "o": D_POOL + 3 * D_MLSTM}[kind]
            return rows_of(w_in[l], 4 * P * half, 4)[:, :, c0:c0 + FBLK]

        def dense_source(kind, b, half):
            if kind == "d":
                return rows_of(wd_dense[0], b * FBLK + 2 * P * half, 2)
            w = wg_dense if kind == "g" else wu_dense
            if b == DENSE_BLOCKS - 1:
                return rows_of(w[0], 0, DK)[:, :, b * FBLK:]
            return rows_of(w[0], 4 * P * half, 4)[:, :, b * FBLK:(b + 1) * FBLK]

        def expert_source(kind, b, half, e):
            w = {"g": wg_exp, "u": wu_exp, "d": wd_exp}[kind][0, e].rearrange("(k p) n -> p k n", p=P)
            if kind == "d":
                return w[:, 4 * b + 2 * half:4 * b + 2 * half + 2, :]
            return w[:, 4 * half:4 * half + 4, b * FBLK:(b + 1) * FBLK]

        def parts_of(n, width):
            return tuple(w[:, n % SPLIT, :].rearrange("p (k n) -> p k n", n=width) for w in (w_hi, w_lo))

        def chunk_event(l, kind, c):
            if c == (TT if kind == "v" else 4) - 1:
                return unit_done, mixer_unit(l, kind, 1) + 1
            before = {"q": 0, "k": 3, "v": 6, "p": 7, "o": 10}[kind]
            return chunk_done, CHUNKS0[l] + before + c + 1

        def dense_event(c):
            b = c // 4
            if c % 4 == dense_chunks(b) - 1:
                return unit_done, dense_unit("u", b, 1 if b < DENSE_BLOCKS - 1 else 0) + 1
            return chunk_done, DENSE_CHUNKS0 + 3 * b + c % 4 + 1

        CHUNKS_MIXER = 3 + 3 + 1 + 3 + 3 + 3
        CHUNKS_DENSE = 3 * (DENSE_BLOCKS - 1) + (DENSE_LAST - 1) + 3
        CHUNKS0 = [0, CHUNKS_MIXER + CHUNKS_DENSE]
        DENSE_CHUNKS0 = CHUNKS_MIXER

        def sum_event(s, t, n):
            l = (s - 1) // 2
            if (t, n) == (TT - 1, 1):
                return unit_done, DENSE_UNIT0 + DENSE_UNITS if s == 2 else mixer_unit(l, "w", 3) + 1
            return chunk_done, (CHUNKS_MIXER + CHUNKS_DENSE if s == 2 else CHUNKS0[l] + CHUNKS_MIXER) - 3 + 2 * t + n + 1

        def xf_event(s, t, n):
            return (xf_act, xf_dve)[n], 4 * (TT * s + t + 1)

        assert at[0] <= ARENA - UNIT
        spare = [arena[:, ARENA - UNIT:], arena[:, 0:UNIT]]
        assert RING == RAW + len(spare)

        def slot(n):
            if n < MOE_UNIT0:
                return raw[:, n % RAW, :]
            u = (n - MOE_UNIT0) % ITEM_UNITS % RING
            return raw[:, (MOE_UNIT0 + u) % RAW, :] if u < RAW else spare[u - RAW]

        def landing(n, i=0):
            if n < MOE_UNIT0:
                return landed[n % RAW], 16 * (n // RAW + 1)
            j, u = divmod(n - MOE_UNIT0, ITEM_UNITS)
            per_item = len(range(u % RING, ITEM_UNITS, RING))
            return fetched[u % RING], (i + j) * (16 * per_item) + 16 * (u // RING + 1)

        block = ctx.enter_context(nc.Block())

        @block.sync
        def _(sp):
            def slot_free(n, i=0, first=False):
                u = n - MOE_UNIT0
                if u >= RING:
                    sp.wait_ge(lo_ready, i * ITEM_UNITS + (n - RING + 1))
                elif u >= 0 and not first:
                    before = range(u, ITEM_UNITS, RING)[-1] - ITEM_UNITS
                    sp.wait_ge(lo_ready, i * ITEM_UNITS + (MOE_UNIT0 + before + 1))
                elif u == RAW:
                    sp.wait_ge(ylo_ready, 4 * LAYERS)
                elif u == RAW + 1:
                    sp.wait_ge(logit_mm, 1)
                elif n >= RAW:
                    sp.wait_ge(lo_ready, n - RAW + 1)

            def load(n, src, i=0, first=False):
                k, c = src.shape[1], src.shape[2]
                slot_free(n, i, first)
                dst = slot(n).rearrange("p (k n) -> p k n", n=c)[:, 0:k, :]
                sp.dma_start(dst, src).then_inc(landing(n)[0], 16)

            for t in range(TT):
                sp.dma_start(tokens[:, t, :], x_d[:, t, :]).then_inc(x_in[t], 16)
            for l in range(LAYERS):
                sp.dma_start(gate_raw[:, l, :, :],
                             w_in[l, :, GATE_COL:GATE_COL + 2 * HEADS].rearrange("(k p) h -> p k h", p=P)
                             ).then_inc(gatew_in, 16)
            for n, (kind, half) in enumerate(MIXER_KINDS):
                load(mixer_unit(0, kind, half), mixer_source(0, kind, half))
                if n == SPLIT - 1:
                    sp.dma_start(cst[:, C_TRI:], consts[:, C_TRI:]).then_inc(consts_in, 16)
                    for (norm, gb), w in (((1, "g"), ln1_g), ((1, "b"), ln1_b), ((2, "g"), ln2_g), ((2, "b"), ln2_b)):
                        row = R_LN[(norm, gb)]
                        sp.dma_start(par_rows[row:row + 16, :], w.rearrange("l (k p) -> (l k) p", p=P)) \
                            .then_inc(par_in, 16)
                    for row, m, w in ((R_CONVB, 16, conv_b), (R_POOLS, 8, pool_scale), (R_MG, 8, mlstm_g)):
                        sp.dma_start(par_rows[row:row + m, :], w.rearrange("l (k p) -> (l k) p", p=P)) \
                            .then_inc(par_in, 16)
                    sp.dma_start(par_rows2, conv_w.rearrange("l j (k p) -> (l j k) p", p=P)).then_inc(par_in, 16)
            for n, (kind, b, half) in enumerate(DENSE_ORDER):
                load(DENSE_UNIT0 + n, dense_source(kind, b, half))
            for kind, half in MIXER_KINDS:
                load(mixer_unit(1, kind, half), mixer_source(1, kind, half))

            def item_loads(i, e, first=False):
                for u, (kind, b, half) in enumerate(ITEM_ORDER):
                    load(MOE_UNIT0 + u, expert_source(kind, b, half, e), i, first)

            item_loads(0, 0, first=True)
            with sp.Fori(1, E) as i:
                item_loads(i, i)
            sp.wait_ge(table_ready, 1)
            n_over = sp.value_load(over_int[0:1, MAX_OVER:MAX_OVER + 1], min_val=0, max_val=MAX_OVER)
            with sp.If(0 < n_over):
                with sp.Fori(0, MAX_OVER) as j:
                    with sp.If(j < n_over):
                        e = sp.value_load(over_int[0:1, bass.ds(j, 1)], min_val=0, max_val=E - 1)
                        item_loads(j + E, e)
            for n in range(MOE_UNIT0, MOE_UNIT0 + AHEAD):
                slot_free(n, n_over + E)
                sp.dma_start(slot(n)[:, 0:8], w_in[0, 0:P, 0:8]).then_inc(landing(n)[0], 16)
            sp.wait_ge(tokens_ready, TT * 3 + 1)
            sp.dma_start(out_d[:, 0, :], tokens[:, 0, :]).then_inc(out_done, 16)
            for n in range(2):
                c = slice(n * HALF, (n + 1) * HALF)
                sp.wait_ge(out_ready, n + 1)
                sp.dma_start(out_d[:, 1, c], tokens[:, 1, c]).then_inc(out_done, 16)
            sp.wait_ge(out_done, 16 * 3)

        @block.gpsimd
        def _(pool):
            g = nc.gpsimd
            g.memset(small[:, 0:1], 1.0).then_inc(small_ready, 1)
            g.memset(small[:, 1:2], EPS).then_inc(small_ready, 1)
            g.memset(gate_w[:], 0.0).then_inc(gatew_zero, 1)
            for l in range(LAYERS):
                for r, c in ((0, 0), (32, HEADS)):
                    pool.dma_start(gate_b[r:r + HEADS, l:l + 1],
                                   b_gates[l, c:c + HEADS].rearrange("(h a) -> h a", a=1)).then_inc(gateb_in, 16)
            pool.wait_ge(gatew_in, 16 * LAYERS)
            pool.wait_ge(gatew_zero, 1)
            g.tensor_copy(gate_w[:, :, :, 0:HEADS].rearrange("p l k h -> p (l k) h"),
                          gate_raw[:, :, :, 0:HEADS].rearrange("p l k h -> p (l k) h")).then_inc(gatew_ready, 1)
            g.tensor_copy(gate_w[:, :, :, 32:32 + HEADS].rearrange("p l k h -> p (l k) h"),
                          gate_raw[:, :, :, HEADS:].rearrange("p l k h -> p (l k) h")).then_inc(gatew_ready, 1)

            def load_ln(s):
                norm, l = NORM[s]
                for n, w in enumerate(((ln1_g, ln1_b), (ln2_g, ln2_b))[norm - 1]):
                    pool.dma_start(ln_row[:, n, :], w[l:l + 1, :].partition_broadcast(P)
                                   .rearrange("p a d -> p (a d)")).then_inc(ln_in, 16)

            pool.wait_ge(landed[AHEAD], 16)
            load_ln(1)
            pool.dma_start(pool_ws[:], pool_w[0].rearrange("g c d -> c g d")).then_inc(poolw_in, 16)
            pool.dma_start(rout_w[:], w_router[0].rearrange("(k p) e -> p k e", p=P)).then_inc(router_in, 16)
            pool.dma_start(rout_b[:], b_router[0:1, :].partition_broadcast(P)
                           .rearrange("p a e -> p (a e)")).then_inc(router_in, 16)

            st = Steps(pool, pool_steps)

            def pooling(l):
                st.then(g.memset(ptmp[:, :, 0:16], 0.0))
                for gr in range(GROUPS):
                    pool.wait_ge(u_ready, GROUPS * l + gr + 1)
                    st.then(g.memset(ubuf[:, gr, 0:16], 0.0))
                    u = ubuf[:, gr, :]
                    src = u
                    if gr:
                        st.wait()
                    for step in range(gr + 1):
                        sh = 1 << step
                        dst = ptmp[:, step % 2, :]
                        st.then(g.tensor_tensor(dst[:, 16:], src[:, 16:], src[:, 16 - sh:16 + T - sh], ALU.add))
                        src = dst
                    st.add(g.tensor_tensor(src[:, 16:32], src[:, 16:32], cst[:, C_INV + 16 * gr:C_INV + 16 * gr + 16],
                                           ALU.mult))
                    st.then(g.tensor_scalar(src[:, 32:], src[:, 32:], 1.0 / (2 << gr), None, ALU.mult))
                    g.tensor_tensor(u[:, 16:], src[:, 16:], u[:, 16:], ALU.subtract).then_inc(pool_ready, 1)
                    pool.wait_ge(pool_ready, GROUPS * l + gr + 1)

            def convs(l):
                pool.wait_ge(absf_ready, l + 1)
                for n, c in enumerate(POOL_CONVS):
                    pool.wait_ge(zqk_ready, 8 * l + c + 1)
                    if l == 0 and n == 0:
                        pool.wait_ge(par_ready, 2)
                    acc = acc_pool[:, n, :]
                    st.then(g.tensor_scalar(acc, zqk[:, c, 0:T], par_col(("conv_w", 0), l, c), None, ALU.mult))
                    for j in range(1, TAPS):
                        st.then(g.tensor_scalar(prod_pool, zqk[:, c, j:j + T], par_col(("conv_w", j), l, c), None,
                                                ALU.mult))
                        ins = g.tensor_tensor(acc, acc, prod_pool, ALU.add)
                        if j < TAPS - 1:
                            st.then(ins)
                        else:
                            ins.then_inc(convp_ready, 1)
                    pool.wait_ge(convp_ready, 2 * l + n + 1)

            def masks(l):
                pool.wait_ge(decay_ready, HEADS * (l + 1))
                for c in (0, T):
                    blk = decay[:, :, c:c + P]
                    g.affine_select(out=blk, in_=blk, compare_op=ALU.is_ge, fill=0.0, base=0,
                                    pattern=[[0, HEADS], [1, P]], channel_multiplier=-1).then_inc(mask_ready, 1)

            def token_rows(s, tiles=range(TT)):
                pool.wait_ge(ln_in, 32 * s)
                for t in tiles:
                    pool.wait_ge(xhat_ready, TT * (s - 1) + t + 1)
                    st.then(g.tensor_tensor(tokens[:, t, :], work[:, t, :], ln_row[:, 0, :], ALU.mult))
                    g.tensor_tensor(tokens[:, t, :], tokens[:, t, :], ln_row[:, 1, :], ALU.add) \
                        .then_inc(tokens_ready, 1)
                if s < 4:
                    pool.wait_ge(tokens_ready, TT * s)
                    load_ln(s + 1)

            def overflow_items():
                def row_sums(out_, v, n):
                    while n > 2:
                        n //= 2
                        st.then(g.tensor_tensor(v[..., 0:n], v[..., 0:n], v[..., n:2 * n], ALU.add))
                    st.then(g.tensor_tensor(out_, v[..., 0:1], v[..., 1:2], ALU.add))

                pool.wait_ge(flags_ready, 1)
                for j in range(MAX_OVER):
                    st.then(g.tensor_scalar(fsel, frank, float(j + 1), None, ALU.is_equal))
                    st.then(g.tensor_tensor(fsel, fsel, flag, ALU.mult))
                    for col, o in ((C_CE, over_e), (C_CT, over_t)):
                        st.then(g.tensor_tensor(ftmp, fsel, cst[:, col:col + 2 * E], ALU.mult))
                        row_sums(o[:, j:j + 1], ftmp, 2 * E)
                    st.then(g.tensor_scalar(fsel[:, 0:E], cst[:, C_CE:C_CE + E], over_e[:, j:j + 1], None,
                                            ALU.is_equal))
                    for src, c in ((posm, 0), (comb, 2)):
                        for t in range(TT):
                            st.then(g.tensor_tensor(itmp[:, t, :], src[:, t, :], fsel[:, 0:E], ALU.mult))
                        row_sums(item_tab[:, E + j, c:c + 2].unsqueeze(2), itmp, E)
                    st.then(g.tensor_scalar(item_tab[:, E + j, 0:2], item_tab[:, E + j, 0:2], over_t[:, j:j + 1],
                                            None, ALU.subtract))
                st.add(g.memset(item_tab[:, MAX_ITEMS, :], -1.0))
                st.add(g.tensor_copy(over_int[:, 0:MAX_OVER], over_e))
                st.then(g.tensor_copy(over_int[:, MAX_OVER:], n_over_f))
                g.sem_inc(table_ready, 1)

            pool.wait_ge(consts_in, 16)
            for l in range(LAYERS):
                convs(l)
                masks(l)
                pooling(l)
                token_rows(2 * l + 1)
                if l + 1 < LAYERS:
                    pool.wait_ge(pooly_mm, 2)
                    pool.dma_start(pool_ws[:], pool_w[1].rearrange("g c d -> c g d")).then_inc(poolw_in, 16)
                    token_rows(2 * l + 2)
            overflow_items()
            token_rows(4, [0])

        @block.scalar
        def _(act):
            a = nc.scalar
            act.dma_start(ident, consts[:, C_ID:C_ID + P]).then_inc(ident_in, 16)

            at_unit = [0]

            def round_hi(n, i=0):
                act.wait_ge(*landing(n, i))
                if n >= SPLIT:
                    act.wait_ge(unit_done, i * ITEM_UNITS + (n - SPLIT + 1))
                a.copy(w_hi[:, n % SPLIT, :], slot(n)).then_inc(hi_ready, 1)

            def ahead():
                round_hi(at_unit[0])
                at_unit[0] += 1

            def norm_std(s, t):
                act.wait_ge(var_ready, TT * (s - 1) + t + 1)
                a.activation(rstd[:, t, 0:1], mv[:, t, 1:2], ACT.Sqrt, bias=eps_col).then_inc(std_ready, 1)

            def turn(s):
                if s:
                    norm_std(s, 0)
                for t in range(TT):
                    act.wait_ge(turned, 2 * (TT * s + t) + 1)
                    if s == 1 and t == 0:
                        act.wait_ge(par_ready, 2)
                    for k in range(DK // 2):
                        src = bank[TURN_BANKS[t][0]][:, k * P:(k + 1) * P]
                        if s == 0:
                            a.copy(xf[:, t, k, :], src).then_inc(xf_act, 1)
                        else:
                            norm, l = NORM[s]
                            a.activation(xf[:, t, k, :], src, ACT.Identity, bias=par_col((norm, "b"), l, k),
                                         scale=par_col((norm, "g"), l, k)).then_inc(xf_act, 1)
                    if s and t == 0:
                        norm_std(s, 1)
                    if s < 3:
                        x_high(s, t, 0)
                if s < 3:
                    for t in range(TT):
                        x_high(s, t, 1)

            def x_high(s, t, n):
                act.wait_ge(*xf_event(s, t, n))
                a.copy(x_hi[:, 4 * n:4 * n + 4, t * P:(t + 1) * P], xf[:, t, 4 * n:4 * n + 4, :]) \
                    .then_inc(xhi_ready, 1)

            def mixer(l):
                ahead()
                act.wait_ge(absf_ready, l + 1)
                a.activation(r_i, bank[6][0:HEADS, 0:T], ACT.Identity, bias=gate_b[0:HEADS, l:l + 1]) \
                    .then_inc(gate_i, 1)
                a.activation(r_l, r_l, ACT.Exp, scale=-1.0).then_inc(gate_e, 1)
                act.wait_ge(gate_e, l + 1)
                if l == 0:
                    act.wait_ge(small_ready, 2)
                a.activation(r_l, r_l, ACT.Ln, bias=small[0:HEADS, 0:1]).then_inc(gate_l, 1)
                ahead()

                def copies(kind, c0):
                    for c in range(4):
                        act.wait_ge(*chunk_event(l, kind, c))
                        a.copy(zqk[:, c0 + c, PAD:], bank[c][:, 0:T]).then_inc(zqk_ready, 1)

                def silu(c):
                    if c in POOL_CONVS:
                        n = POOL_CONVS.index(c)
                        act.wait_ge(convp_ready, 2 * l + n + 1)
                        acc = acc_pool[:, n, :]
                    else:
                        n = DVE_CONVS.index(c)
                        act.wait_ge(conv_ready, len(DVE_CONVS) * l + n + 1)
                        acc = conv_acc[:, n % 2, :]
                    a.activation(qkT[:, c, :], acc, ACT.Silu, bias=par_col("conv_b", l, c)) \
                        .then_inc(qk_ready, 1)

                copies("q", 0)
                ahead()
                silu(0)
                silu(1)
                ahead()
                silu(2)
                silu(3)
                copies("k", 4)
                ahead()
                silu(4)
                silu(5)
                ahead()
                silu(6)
                silu(7)
                ahead()
                for h in range(HEADS):
                    act.wait_ge(arg_ready, HEADS * l + h + 1)
                    a.activation(decay[:, h, :], decay[:, h, :], ACT.Exp).then_inc(decay_ready, 1)
                act.wait_ge(cols_ready, l + 1)
                a.activation(guard[:].rearrange("p t h -> p (t h)"), cols[:, 1].rearrange("p t h -> p (t h)"),
                             ACT.Exp, scale=-1.0).then_inc(guard_ready, 1)
                ahead()
                act.wait_ge(qk_ready, 8 * (l + 1))
                for c in range(GROUPS):
                    act.wait_ge(*chunk_event(l, "p", c))
                    a.copy(ubuf[:, c, 16:], bank[c][:, 0:T]).then_inc(u_ready, 1)
                ahead()
                ahead()

                def y_round(at_y):
                    a.copy(y_hi[at_y], yT[at_y]).then_inc(yhi_ready, 1)

                act.wait_ge(ypool_ready, 2 * l + 1)
                y_round(Y_PARTS[0])
                for c in range(HEADS):
                    act.wait_ge(*chunk_event(l, "o", c))
                    a.activation(sigT[:, c, :], bank[c][:, 0:T], ACT.Sigmoid).then_inc(sig_ready, 1)
                for t in range(TT):
                    act.wait_ge(hvar_ready, TT * l + t + 1)
                    a.activation(hstd[:, t, :], hmv[:, t, :, 1], ACT.Sqrt, bias=eps_col).then_inc(hstd_ready, 1)
                act.wait_ge(ypool_ready, 2 * l + 2)
                y_round(Y_PARTS[1])
                ahead()
                ahead()
                for t in range(TT):
                    act.wait_ge(ym_ready, HEADS * (TT * l + t + 1))
                    y_round(Y_PARTS[2 + t])
                ahead()

            def dense():
                def silu(c):
                    act.wait_ge(*dense_event(c))
                    if c >= 2:
                        act.wait_ge(dh_ready, c - 1)
                    a.activation(dsg[:, c % 2, :], bank[(2, 3, 6, 7)[c % 4]][:, 0:T], ACT.Silu).then_inc(dsilu, 1)

                def hidden_hi(c):
                    act.wait_ge(dh_ready, c + 1)
                    if c % 4 == 0 and c >= 8:
                        act.wait_ge(unit_done, dense_unit("d", c // 4 - 2, 1) + 1)
                    a.copy(dh_hi[:, c // 4 % 2, c % 4, :], dh[:, c % 2, :]).then_inc(dhi_ready, 1)

                for kind, b, half in DENSE_ORDER[:-1]:
                    ahead()
                    if kind == "u" and half == (1 if b < DENSE_BLOCKS - 1 else 0):
                        c0, n = 4 * b, dense_chunks(b)
                        silu(c0)
                        for c in range(c0 + 1, c0 + n):
                            silu(c)
                            hidden_hi(c - 1)
                        hidden_hi(c0 + n - 1)

            turn(0)
            for _ in range(AHEAD):
                ahead()
            for l in range(LAYERS):
                mixer(l)
                turn(2 * l + 1)
                ahead()
                if l == 0:
                    dense()
                    turn(2)
                    ahead()
            ahead()
            act.wait_ge(logit_ready, 1)
            for t in range(TT):
                a.activation(expo[:, t, :], logit[:, t, :], ACT.Exp, bias=top[:, t:t + 1]).then_inc(expo_ready, 1)

            def gathered_hi(i, n, psum):
                act.wait_ge(gather_mm, 2 * i + n + 1)
                a.copy(xg_hi[:, 4 * n:4 * n + 4, :].rearrange("p k c -> p (k c)"), psum[:, 0:4 * CAP]) \
                    .then_inc(xghi_ready, 1)

            def item(i, first=False):
                for u in range(ITEM_UNITS):
                    if not first or u:
                        round_hi(MOE_UNIT0 + u + AHEAD, i)
                    if u in STEP_SILU:
                        b = STEP_SILU[u]
                        act.wait_ge(unit_done, i * ITEM_UNITS + (MOE_UNIT0 + u + 1))
                        a.activation(esg[0:CAP, b % 2, :], bank[(2, 6)[b % 2]][0:CAP, :], ACT.Silu) \
                            .then_inc(esilu, 1)
                    if u in STEP_TURN:
                        b = STEP_TURN[u]
                        act.wait_ge(eturn_mm, i * EXP_BLOCKS + (b + 1))
                        a.copy(eh_hi[:, b % 2].rearrange("p j c -> p (j c)"), bank[5][:, 0:4 * CAP]) \
                            .then_inc(ehi_ready, 1)
                    if u in STEP_TAKE:
                        if STEP_TAKE[u] == 0:
                            act.wait_ge(unit_done, i * ITEM_UNITS + (MOE_UNIT0 + u + 1))
                        gathered_hi(i + 1, STEP_TAKE[u], GATHER_BANKS[STEP_TAKE[u]])
                for n in range(2):
                    if n == 0:
                        act.wait_ge(half_mm, i + 1)
                    else:
                        act.wait_ge(unit_done, i * ITEM_UNITS + (MOE_UNIT0 + ITEM_UNITS))
                    a.copy(y_sb[0:CAP, n * HALF:(n + 1) * HALF], bank[n][0:CAP, :]).then_inc(ysb_ready, 1)

            gathered_hi(0, 0, bank[4])
            gathered_hi(0, 1, bank[5])
            item(0, first=True)
            with act.Fori(1, E) as i:
                item(i)
            act.wait_ge(table_ready, 1)
            n_over = act.value_load(over_int[0:1, MAX_OVER:MAX_OVER + 1], min_val=0, max_val=MAX_OVER)
            with act.If(0 < n_over):
                with act.Fori(0, MAX_OVER) as j:
                    with act.If(j < n_over):
                        item(j + E)
            for t in range(TT):
                norm_std(4, t)

        @block.vector
        def _(dve):
            v = nc.vector
            st = Steps(dve, steps)

            at_unit = [0]

            def subtract_lo(n, i=0):
                dve.wait_ge(hi_ready, i * ITEM_UNITS + (n + 1))
                v.tensor_tensor(w_lo[:, n % SPLIT, :], slot(n), w_hi[:, n % SPLIT, :].bitcast(F32),
                                ALU.subtract).then_inc(lo_ready, 1)

            def ahead():
                subtract_lo(at_unit[0])
                at_unit[0] += 1

            def turn(s):
                for t in range(TT):
                    dve.wait_ge(turned, 2 * (TT * s + t) + 2)
                    if s == 1 and t == 0:
                        dve.wait_ge(par_ready, 2)
                    for k in range(DK // 2, DK):
                        src = bank[TURN_BANKS[t][1]][:, (k - 4) * P:(k - 3) * P]
                        if s == 0:
                            v.tensor_copy(xf[:, t, k, :], src).then_inc(xf_dve, 1)
                        else:
                            norm, l = NORM[s]
                            v.tensor_scalar(xf[:, t, k, :], src, par_col((norm, "g"), l, k),
                                            par_col((norm, "b"), l, k), ALU.mult, ALU.add).then_inc(xf_dve, 1)
                if s < 3:
                    for n in range(2):
                        for t in range(TT):
                            dve.wait_ge(xhi_ready, 2 * TT * s + TT * n + t + 1)
                            at_x = (slice(None), slice(4 * n, 4 * n + 4), slice(t * P, (t + 1) * P))
                            v.tensor_tensor(x_lo[at_x], xf[:, t, 4 * n:4 * n + 4, :], x_hi[at_x].bitcast(F32),
                                            ALU.subtract).then_inc(xlo_ready, 1)

            def mixer(l):
                ahead()
                dve.wait_ge(gates_mm, l + 1)
                dve.wait_ge(gateb_in, 16 * 2 * LAYERS)
                dve.wait_ge(xlo_ready, 2 * TT * (2 * l + 1))
                st.add(v.memset(zqk[:, :, 0:PAD], 0.0))
                st.then(v.tensor_scalar(r_f, bank[6][32:32 + HEADS, 0:T], gate_b[32:32 + HEADS, l:l + 1], None,
                                        ALU.add))
                v.scalar_tensor_tensor(out=r_l, in0=r_f, scalar=-1.0, in1=r_f, op0=ALU.mult, op1=ALU.max) \
                    .then_inc(absf_ready, 1)
                dve.wait_ge(gate_l, l + 1)
                st.then(v.scalar_tensor_tensor(out=r_f, in0=r_f, scalar=0.0, in1=r_l, op0=ALU.min,
                                               op1=ALU.subtract))
                if l == 0:
                    dve.wait_ge(consts_in, 16)
                st.then(v.tensor_tensor_scan(r_l, ones_t, r_f, 0.0, ALU.mult, ALU.add))
                dve.wait_ge(gate_i, l + 1)
                st.then(v.tensor_tensor(r_i, r_i, r_l, ALU.subtract))
                st.then(v.tensor_tensor_scan(r_m, ones_t, r_i, 0.0, ALU.mult, ALU.max))
                st.add(v.tensor_scalar(r_negm, r_m, -1.0, None, ALU.mult))
                st.wait()
                v.tensor_tensor(r_m, r_m, r_l, ALU.add).then_inc(rows_ready, 1)

                if l == 0:
                    for n, (r, c) in enumerate(((96, 0), (64, 96))):
                        dve.wait_ge(par_turned, n + 1)
                        v.tensor_copy(par[:, c:c + r], bank[(4, 5)[n]][:, 0:r]).then_inc(par_ready, 1)
                    dve.wait_ge(par_ready, 2)
                ahead()

                def conv(c):
                    n = DVE_CONVS.index(c)
                    dve.wait_ge(zqk_ready, 8 * l + c + 1)
                    if n >= 2:
                        dve.wait_ge(qk_ready, 8 * l + DVE_CONVS[n - 2] + 1)
                    acc = conv_acc[:, n % 2, :]
                    st.then(v.tensor_scalar(acc, zqk[:, c, 0:T], par_col(("conv_w", 0), l, c), None, ALU.mult))
                    for j in range(1, TAPS):
                        ins = v.scalar_tensor_tensor(out=acc, in0=zqk[:, c, j:j + T],
                                                     scalar=par_col(("conv_w", j), l, c), in1=acc,
                                                     op0=ALU.mult, op1=ALU.add)
                        if j < TAPS - 1:
                            st.then(ins)
                        else:
                            ins.then_inc(conv_ready, 1)

                conv(0)
                conv(1)
                ahead()
                conv(2)
                ahead()
                conv(4)
                conv(5)
                ahead()
                conv(7)
                ahead()
                for t in range(TT):
                    dve.wait_ge(*chunk_event(l, "v", t))
                    v.tensor_copy(v_sb[:, t, :], bank[4 + t][:, :]).then_inc(v_ready, 1)
                dve.wait_ge(cols_mm, l + 1)
                v.tensor_copy(cols[:].rearrange("p a t h -> p (a t h)"), bank[6][:, 0:4 * HEADS]) \
                    .then_inc(cols_ready, 1)
                dve.wait_ge(cols_ready, l + 1)
                ahead()
                dve.wait_ge(conv_ready, len(DVE_CONVS) * (l + 1))
                dve.wait_ge(convp_ready, 2 * (l + 1))
                for h in range(HEADS):
                    dve.wait_ge(bcast_mm, 2 * l + h // 2 + 1)
                    m = bank[(7, 4)[h // 2]][:, (h % 2) * T:(h % 2 + 1) * T]
                    st.add(v.tensor_scalar(decay[:, h, 0:T], m, cols[:, 0, 0, h:h + 1], 0.0, ALU.add, ALU.min))
                    v.tensor_scalar(decay[:, h, T:T + P], m[:, P:T], cols[:, 0, 1, h:h + 1], 0.0, ALU.add,
                                    ALU.min).then_inc(arg_ready, 1)
                ahead()
                ahead()
                dve.wait_ge(mask_ready, 2 * (l + 1))
                for h in range(HEADS):
                    dve.wait_ge(score_mm, HEADS * l + h + 1)
                    v.scalar_tensor_tensor(out=decay[:, h, :], in0=bank[SCORE_BANKS[h]][:, 0:T + P],
                                           scalar=QK_SCALE, in1=decay[:, h, :], op0=ALU.mult, op1=ALU.mult) \
                        .then_inc(w_ready, 1)
                ahead()
                dve.wait_ge(guard_ready, l + 1)
                dve.wait_ge(pv_mm, TT * l + 1)
                den = bank[4][:, 0:TT * HEADS]
                rd, gd = (w[:].rearrange("p t h -> p (t h)") for w in (rden, guard))
                st.then(v.tensor_tensor(rd, den, gd, ALU.max))
                v.scalar_tensor_tensor(out=rd, in0=den, scalar=-1.0, in1=rd, op0=ALU.mult, op1=ALU.max) \
                    .then_inc(rden_ready, 1)
                dve.wait_ge(rden_ready, l + 1)
                st.then(v.reciprocal(rd, rd))

                def pooled(n):
                    dve.wait_ge(pooly_mm, 2 * l + n + 1)
                    for g in range(2):
                        ins = v.tensor_scalar(yT[:, 2 * n + g, :], bank[POOL_BANKS[n]][:, g * T:(g + 1) * T],
                                              par_col("pool_scale", l, 2 * n + g), None, ALU.mult)
                        if g == 0:
                            st.add(ins)
                        else:
                            ins.then_inc(ypool_ready, 1)

                def y_low(n):
                    dve.wait_ge(yhi_ready, 4 * l + n + 1)
                    at_y = Y_PARTS[n]
                    v.tensor_tensor(y_lo[at_y], yT[at_y], y_hi[at_y].bitcast(F32), ALU.subtract) \
                        .then_inc(ylo_ready, 1)

                def head_stats(t):
                    dve.wait_ge(pv_mm, TT * l + t + 1)
                    for h in range(HEADS):
                        st.add(v.tensor_scalar(h_norm[t][:, h * DH:(h + 1) * DH],
                                               bank[PV_BANKS[t]][:, h * DH:(h + 1) * DH],
                                               rden[:, t, h:h + 1], None, ALU.mult))
                    st.wait()
                    for h in range(HEADS):
                        st.add(v.bn_stats(hstats[:, t, h, :], h_norm[t][:, h * DH:(h + 1) * DH]))
                    st.wait()
                    for h in range(HEADS):
                        ins = v.bn_aggr(hmv[:, t, h, :], hstats[:, t, h, :])
                        if h < HEADS - 1:
                            st.add(ins)
                        else:
                            ins.then_inc(hvar_ready, 1)

                pooled(0)
                head_stats(0)
                y_low(0)
                head_stats(1)
                pooled(1)
                for t in range(TT):
                    dve.wait_ge(hstd_ready, TT * l + t + 1)
                    dve.wait_ge(hvar_ready, TT * l + t + 1)
                    st.then(v.reciprocal(hrstd[:, t, :], hstd[:, t, :]))
                    for h in range(HEADS):
                        v.tensor_scalar(h_norm[t][:, h * DH:(h + 1) * DH], h_norm[t][:, h * DH:(h + 1) * DH],
                                        hmv[:, t, h, 0:1], hrstd[:, t, h:h + 1], ALU.subtract, ALU.mult) \
                            .then_inc(h_ready, 1)
                y_low(1)
                ahead()
                dve.wait_ge(sig_ready, HEADS * (l + 1))
                for t in range(TT):
                    dve.wait_ge(ht_mm, TT * l + t + 1)
                    for h in range(HEADS):
                        v.scalar_tensor_tensor(out=yT[:, GROUPS + h, t * P:(t + 1) * P],
                                               in0=bank[PV_BANKS[t]][:, h * P:(h + 1) * P],
                                               scalar=par_col("mlstm_g", l, h),
                                               in1=sigT[:, h, t * P:(t + 1) * P],
                                               op0=ALU.mult, op1=ALU.mult).then_inc(ym_ready, 1)
                ahead()
                y_low(2)
                y_low(3)
                ahead()

            def residual_half(s, t, n):
                c = slice(n * HALF, (n + 1) * HALF)
                dve.wait_ge(*sum_event(s, t, n))
                st.then(v.scalar_tensor_tensor(out=work[:, t, c], in0=tokens[:, t, c], scalar=ALPHA,
                                               in1=bank[SUM_BANKS[t][n]][:, :], op0=ALU.mult, op1=ALU.add))
                st.add(v.bn_stats(stats[:, t, n, :], work[:, t, c]))

            def normalise(s, t):
                st.wait()
                v.bn_aggr(mv[:, t, :], stats[:, t].rearrange("p a b -> p (a b)")).then_inc(var_ready, 1)
                dve.wait_ge(std_ready, TT * (s - 1) + t + 1)
                dve.wait_ge(var_ready, TT * (s - 1) + t + 1)
                st.then(v.reciprocal(rstd[:, t, 1:2], rstd[:, t, 0:1]))
                v.tensor_scalar(work[:, t, :], work[:, t, :], mv[:, t, 0:1], rstd[:, t, 1:2],
                                ALU.subtract, ALU.mult).then_inc(xhat_ready, 1)

            def dense():
                def mul(c):
                    dve.wait_ge(dsilu, c + 1)
                    if c >= 2:
                        dve.wait_ge(dlo_ready, c - 1)
                    v.tensor_tensor(dh[:, c % 2, :], dsg[:, c % 2, :], bank[(2, 3, 6, 7)[c % 4]][:, T:2 * T],
                                    ALU.mult).then_inc(dh_ready, 1)

                def hidden_lo(c):
                    dve.wait_ge(dhi_ready, c + 1)
                    v.tensor_tensor(dh_lo[:, c // 4 % 2, c % 4, :], dh[:, c % 2, :],
                                    dh_hi[:, c // 4 % 2, c % 4, :].bitcast(F32), ALU.subtract).then_inc(dlo_ready, 1)

                for kind, b, half in DENSE_ORDER[:-1]:
                    ahead()
                    if kind == "u" and half == (1 if b < DENSE_BLOCKS - 1 else 0):
                        c0, n = 4 * b, dense_chunks(b)
                        mul(c0)
                        for c in range(c0 + 1, c0 + n):
                            mul(c)
                            hidden_lo(c - 1)
                        hidden_lo(c0 + n - 1)

            def norm(s):
                if s > 1:
                    dve.wait_ge(tokens_ready, TT * (s - 1))
                for t in range(TT):
                    for n in range(2):
                        residual_half(s, t, n)
                    normalise(s, t)
                turn(s)

            turn(0)
            for _ in range(AHEAD):
                ahead()
            for l in range(LAYERS):
                mixer(l)
                norm(2 * l + 1)
                if l == 0:
                    ahead()
                    dense()
                    norm(2)
                    ahead()

            dve.wait_ge(logit_mm, 1)
            dve.wait_ge(router_in, 32)
            for t in range(TT):
                st.add(v.tensor_tensor(logit[:, t, :], bank[0][:, t * E:(t + 1) * E], rout_b[:], ALU.add))
            st.wait()
            for t in range(TT):
                lj = logit[:, t, :].unsqueeze(1).to_broadcast([P, E, E])
                le = logit[:, t, :].unsqueeze(2).to_broadcast([P, E, E])
                st.add(v.tensor_tensor(gt[:, t], lj, le, ALU.is_gt))
                st.add(v.tensor_tensor(eq[:, t], lj, le, ALU.is_equal))
            st.wait()
            lt = cst[:, C_LT:C_LT + E * E].rearrange("p (e j) -> p e j", e=E)
            for t in range(TT):
                st.add(v.tensor_tensor(eq[:, t], eq[:, t], lt, ALU.mult))
            st.wait()
            st.then(v.tensor_tensor(gt.rearrange("p t e j -> p (t e j)"), gt.rearrange("p t e j -> p (t e j)"),
                                    eq.rearrange("p t e j -> p (t e j)"), ALU.add))
            st.then(v.tensor_reduce(rank.rearrange("p t e -> p (t e)"), gt.rearrange("p t e j -> p (t e) j"),
                                    AX_X, ALU.add))
            v.tensor_scalar(chosen.rearrange("p t e -> p (t e)"), rank.rearrange("p t e -> p (t e)"),
                            TOP_K - 0.5, None, ALU.is_lt).then_inc(chosen_ready, 1)
            dve.wait_ge(chosen_ready, 1)
            st.then(v.tensor_reduce(top, logit, AX_X, ALU.max))
            v.tensor_scalar(top, top, -1.0, None, ALU.mult).then_inc(logit_ready, 1)
            dve.wait_ge(pos_mm, 1)
            st.then(v.scalar_tensor_tensor(out=posm.rearrange("p t e -> p (t e)"), in0=bank[0][:, 2 * E:4 * E],
                                           scalar=1.0, in1=chosen.rearrange("p t e -> p (t e)"),
                                           op0=ALU.add, op1=ALU.mult))
            st.then(v.tensor_scalar(posm, posm, -1.0, None, ALU.add))

            def pick_tiles(slot_of, combine_of):
                for t in range(TT):
                    if combine_of is None:
                        v.tensor_scalar(pick[:, t, :], iota, slot_of(t), None, ALU.is_equal).then_inc(pick_ready, 1)
                    else:
                        v.tensor_scalar(pickc[:, t, :], iota, slot_of(t), combine_of(t), ALU.is_equal, ALU.mult) \
                            .then_inc(pickc_ready, 1)

            pick_tiles(lambda t: posm[:, t, 0:1], None)
            dve.wait_ge(expo_ready, 2)
            st.then(v.tensor_tensor(comb, expo, chosen, ALU.mult))
            st.then(v.tensor_reduce(esum, comb, AX_X, ALU.add))
            st.then(v.reciprocal(esum, esum))
            for t in range(TT):
                st.add(v.tensor_scalar(comb[:, t, :], comb[:, t, :], esum[:, t:t + 1], None, ALU.mult))
            st.wait()

            def item_tables():
                pick_tiles(lambda t: posm[:, t, 0:1], lambda t: comb[:, t, 0:1])
                for t in range(TT):
                    st.add(v.tensor_copy(item_tab[:, 0:E, t], posm[:, t, :]))
                    st.add(v.tensor_copy(item_tab[:, 0:E, 2 + t], comb[:, t, :]))
                dve.wait_ge(count_mm, 1)
                st.then(v.tensor_copy(count, bank[0][:, 4 * E:5 * E]))
                st.add(v.tensor_scalar(flag[:, 0:E], count, CAP + 0.5, None, ALU.is_gt))
                st.then(v.tensor_scalar(flag[:, E:], count, 2 * CAP + 0.5, None, ALU.is_gt))
                st.add(v.tensor_reduce(n_over_f, flag, AX_X, ALU.add))
                st.wait()
                v.tensor_tensor_scan(frank, cst[:, C_ONES:C_ONES + 2 * E], flag, 0.0, ALU.mult, ALU.add) \
                    .then_inc(flags_ready, 1)

            def start_sums():
                dve.wait_ge(tokens_ready, TT * 3)
                st.then(v.tensor_scalar(work[:, :, :], tokens[:, :, :], ALPHA, None, ALU.mult))

            def build_pick(i):
                dve.wait_ge(table_ready, 1)
                v.tensor_copy(item_cur.unsqueeze(1), item_tab[:, bass.ds(i, 1), :]).then_inc(cur_ready, 1)
                dve.wait_ge(cur_ready, i)
                pick_tiles(lambda t: item_cur[:, t:t + 1], None)
                pick_tiles(lambda t: item_cur[:, t:t + 1], lambda t: item_cur[:, 2 + t:3 + t])

            def gathered_lo(i, n, psum):
                dve.wait_ge(xghi_ready, 2 * i + n + 1)
                at_x = (slice(None), slice(4 * n, 4 * n + 4))
                v.tensor_tensor(xg_lo[at_x].rearrange("p k c -> p (k c)"), psum[:, 0:4 * CAP],
                                xg_hi[at_x].rearrange("p k c -> p (k c)").bitcast(F32),
                                ALU.subtract).then_inc(xglo_ready, 1)

            def add_scattered(i, q, psum=bank[4]):
                t, n = divmod(q, 2)
                dve.wait_ge(scat_mm, 4 * i + q + 1)
                w = work[:, t, n * HALF:(n + 1) * HALF]
                v.tensor_tensor(w, w, psum[:, :], ALU.add).then_inc(acc_done, 1)

            def item(i, first=False):
                for u in range(ITEM_UNITS):
                    if not first or u:
                        subtract_lo(MOE_UNIT0 + u + AHEAD, i)
                    if first and u == STEP_TABLES:
                        item_tables()
                    if first and u == STEP_SUMS:
                        start_sums()
                    if u in STEP_MUL:
                        b = STEP_MUL[u]
                        dve.wait_ge(esilu, i * EXP_BLOCKS + (b + 1))
                        dve.wait_ge(unit_done, i * ITEM_UNITS + (MOE_UNIT0 + u + 1))
                        v.tensor_tensor(eh[0:CAP, b % 2, :], esg[0:CAP, b % 2, :], bank[(3, 7)[b % 2]][0:CAP, :],
                                        ALU.mult).then_inc(eh_ready, 1)
                    if u in STEP_TURN:
                        b = STEP_TURN[u]
                        dve.wait_ge(ehi_ready, i * EXP_BLOCKS + (b + 1))
                        v.tensor_tensor(eh_lo[:, b % 2].rearrange("p j c -> p (j c)"), bank[5][:, 0:4 * CAP],
                                        eh_hi[:, b % 2].rearrange("p j c -> p (j c)").bitcast(F32),
                                        ALU.subtract).then_inc(elo_ready, 1)
                    if u in STEP_SCATTER and not first:
                        add_scattered(i - 1, STEP_SCATTER[u])
                    if u == STEP_SLOTS:
                        dve.wait_ge(st_mm, i + 1)
                        v.tensor_copy(scat[0:CAP, :], bank[4][0:CAP, 0:T]).then_inc(scat_ready, 1)
                    if u == STEP_PICK:
                        build_pick(i + 1)
                    if u in STEP_TAKE:
                        gathered_lo(i + 1, STEP_TAKE[u], GATHER_BANKS[STEP_TAKE[u]])

            ahead()
            gathered_lo(0, 0, bank[4])
            ahead()
            gathered_lo(0, 1, bank[5])
            item(0, first=True)
            with dve.Fori(1, E) as i:
                item(i)
            dve.wait_ge(table_ready, 1)
            n_over = dve.value_load(over_int[0:1, MAX_OVER:MAX_OVER + 1], min_val=0, max_val=MAX_OVER)
            with dve.If(0 < n_over):
                with dve.Fori(0, MAX_OVER) as j:
                    with dve.If(j < n_over):
                        item(j + E)
            for t in range(TT):
                for n in range(2):
                    q = 2 * t + n
                    add_scattered(n_over + (E - 1), q, bank[TAIL_BANKS[q]])
                    dve.wait_ge(acc_done, 4 * (n_over + (E - 1)) + (q + 1))
                    st.add(v.bn_stats(stats[:, t, n, :], work[:, t, n * HALF:(n + 1) * HALF]))
                normalise(4, t)
            dve.wait_ge(ln_in, 32 * 4)
            dve.wait_ge(xhat_ready, TT * 4)
            for n in range(2):
                c = slice(n * HALF, (n + 1) * HALF)
                st.then(v.tensor_tensor(work[:, 1, c], work[:, 1, c], ln_row[:, 0, c], ALU.mult))
                v.tensor_tensor(tokens[:, 1, c], work[:, 1, c], ln_row[:, 1, c], ALU.add).then_inc(out_ready, 1)

        @block.tensor
        def _(pe):
            mm = nc.tensor.matmul
            tr = nc.tensor.transpose

            def arrived(n, i=0):
                pe.wait_ge(lo_ready, i * ITEM_UNITS + (n + 1))

            def product(psum, left, right, first, last):
                mm(psum, left[0], right[0], start=first, stop=False)
                mm(psum, left[0], right[1], start=False, stop=False)
                return mm(psum, left[1], right[0], start=False, stop=last)

            def logits(t, ks):
                for k in ks:
                    pe.wait_ge(*xf_event(3, t, k // 4))
                    last = mm(bank[0][:, t * E:(t + 1) * E], xf[:, t, k, :], rout_w[:, k, :],
                              start=k == 0, stop=k == DK - 1)
                return last

            def turn(s, tiles=range(TT)):
                for t in tiles:
                    if s == 0:
                        pe.wait_ge(x_in[t], 16)
                    else:
                        pe.wait_ge(xhat_ready, TT * (s - 1) + t + 1)
                    src = tokens if s == 0 else work
                    for k in range(DK):
                        last = tr(bank[TURN_BANKS[t][k // 4]][:, (k % 4) * P:(k % 4 + 1) * P],
                                  src[:, t, k * P:(k + 1) * P], ident)
                        if k % 4 == 3:
                            last.then_inc(turned, 1)

            def x_parts(k, c=slice(None)):
                return x_hi[:, k, c], x_lo[:, k, c]

            def first_product(psum, hi, lo, s):
                pe.wait_ge(xhi_ready, 2 * TT * s + TT)
                for k in range(4):
                    mm(psum, hi[:, k, :], x_hi[:, k, :], start=k == 0, stop=False)
                    mm(psum, lo[:, k, :], x_hi[:, k, :], start=False, stop=False)
                pe.wait_ge(xlo_ready, 2 * TT * s + TT)
                for k in range(4):
                    mm(psum, hi[:, k, :], x_lo[:, k, :], start=False, stop=False)

            def mixer(l):
                def chunks(kind, half, free=None):
                    arrived(mixer_unit(l, kind, half))
                    hi, lo = parts_of(mixer_unit(l, kind, half), FBLK)
                    for c in range(4):
                        if half == 0 and free is not None:
                            pe.wait_ge(*free(c))
                        if kind == "q" and half == 0 and c == 0:
                            first_product(bank[c][:, 0:T], hi[:, :, 0:P], lo[:, :, 0:P], 2 * l)
                            continue
                        for kk in range(4):
                            w = (slice(None), kk, slice(c * P, (c + 1) * P))
                            last = product(bank[c][:, 0:T], (hi[w], lo[w]), x_parts(4 * half + kk),
                                           half == 0 and kk == 0, half == 1 and kk == 3)
                        if c == 3:
                            last.then_inc(unit_done, 1)
                        elif half == 1:
                            last.then_inc(chunk_done, 1)

                def gates():
                    if l == 0:
                        pe.wait_ge(gatew_ready, 2)
                    for n in range(2):
                        pe.wait_ge(*xf_event(2 * l, TT - 1, n))
                    for t in range(TT):
                        for k in range(DK):
                            last = mm(bank[6][0:32 + HEADS, t * P:(t + 1) * P], gate_w[:, l, k, :], xf[:, t, k, :],
                                      start=k == 0, stop=k == DK - 1)
                    last.then_inc(gates_mm, 1)

                if l == 0:
                    gates()
                chunks("q", 0)
                if l:
                    gates()
                else:
                    pe.wait_ge(par_in, 16 * 8)
                    tr(bank[4][:, 0:96], par_rows, ident[0:96, 0:96]).then_inc(par_turned, 1)
                    tr(bank[5][:, 0:64], par_rows2, ident[0:64, 0:64]).then_inc(par_turned, 1)
                pe.wait_ge(xlo_ready, 2 * TT * (2 * l + 1))
                chunks("q", 1)
                chunks("k", 0, lambda c: (zqk_ready, 8 * l + c + 1))
                chunks("k", 1)
                if l == 0:
                    pe.wait_ge(par_ready, 2)
                for half in range(2):
                    n = mixer_unit(l, "v", half)
                    arrived(n)
                    w = parts_of(n, FBLK)
                    for t in range(TT):
                        for kk in range(4):
                            last = product(bank[4 + t][:, :], x_parts(4 * half + kk, slice(t * P, (t + 1) * P)),
                                           (w[0][:, kk, :], w[1][:, kk, :]), half == 0 and kk == 0,
                                           half == 1 and kk == 3)
                        if t == TT - 1:
                            last.then_inc(unit_done, 1)
                        elif half == 1:
                            last.then_inc(chunk_done, 1)
                pe.wait_ge(rows_ready, l + 1)
                for n, r in enumerate((r_i, r_m)):
                    for t in range(TT):
                        c = (n * TT + t) * HEADS
                        last = tr(bank[6][:, c:c + HEADS], r[:, t * P:(t + 1) * P], ident[0:HEADS, 0:HEADS])
                last.then_inc(cols_mm, 1)
                for h in range(HEADS):
                    if h == 2:
                        pe.wait_ge(v_ready, TT * l + 1)
                    last = mm(bank[(7, 4)[h // 2]][:, (h % 2) * T:(h % 2 + 1) * T],
                              cst[0:HEADS, C_SEL + h * P:C_SEL + (h + 1) * P], r_negm, start=True, stop=True)
                    if h % 2:
                        last.then_inc(bcast_mm, 1)
                chunks("p", 0, lambda c: (zqk_ready, 8 * l + 4 + c + 1))
                chunks("p", 1)
                pe.wait_ge(qk_ready, 8 * (l + 1))
                pe.wait_ge(v_ready, TT * (l + 1))
                pe.wait_ge(cols_ready, l + 1)
                pe.wait_ge(arg_ready, HEADS * (l + 1))
                for h, n in enumerate(SCORE_BANKS):
                    mm(bank[n][:, 0:T], qkT[:, HEADS + h, 0:P], qkT[:, h, :], start=True, stop=True)
                    mm(bank[n][:, T:T + P], qkT[:, HEADS + h, P:T], qkT[:, h, P:T], start=True, stop=True) \
                        .then_inc(score_mm, 1)
                chunks("o", 0, lambda c: (u_ready, GROUPS * l + c + 1))
                pe.wait_ge(w_ready, HEADS * (l + 1))
                wts = [[(decay[:, h, 0:P], 0)] for h in range(HEADS)], \
                      [[(decay[:, h, P:T], 0), (decay[:, h, T:T + P], 1)] for h in range(HEADS)]
                for t in range(TT):
                    for h in range(HEADS):
                        for w, s in wts[t][h]:
                            mm(bank[4][:, t * HEADS + h:t * HEADS + h + 1], w, ones[:, 0:1],
                               start=s == 0, stop=s == t)
                for t in range(TT):
                    for h in range(HEADS):
                        for w, s in wts[t][h]:
                            last = mm(bank[PV_BANKS[t]][:, h * DH:(h + 1) * DH], w, v_sb[:, s, h * DH:(h + 1) * DH],
                                      start=s == 0, stop=s == t)
                    last.then_inc(pv_mm, 1)
                pe.wait_ge(poolw_in, 16 * (l + 1))

                def pool_maps(n):
                    for g in range(2):
                        pe.wait_ge(pool_ready, GROUPS * l + 2 * n + g + 1)
                        last = mm(bank[POOL_BANKS[n]][:, g * T:(g + 1) * T], pool_ws[:, 2 * n + g, :],
                                  ubuf[:, 2 * n + g, 16:], start=True, stop=True)
                    last.then_inc(pooly_mm, 1)

                pool_maps(0)
                chunks("o", 1)
                pe.wait_ge(sig_ready, HEADS * (l + 1))
                pool_maps(1)

                def project(units, t):
                    for half in range(2):
                        for q in units:
                            w = parts_of(mixer_unit(l, "w", q), D)
                            for kk in range(2):
                                y = (slice(None), 2 * q + kk, slice(t * P, (t + 1) * P))
                                r = (slice(None), kk, slice(half * HALF, (half + 1) * HALF))
                                last = product(bank[SUM_BANKS[t][half]][:, :], (y_hi[y], y_lo[y]),
                                               (w[0][r], w[1][r]), q == 0 and kk == 0, q == 3 and kk == 1)
                            if (t, half) == (TT - 1, 1):
                                last.then_inc(unit_done, 1)
                            elif q == 3:
                                last.then_inc(chunk_done, 1)

                pe.wait_ge(ylo_ready, 4 * l + 1)
                pe.wait_ge(rden_ready, l + 1)
                arrived(mixer_unit(l, "w", 0))
                project([0], 0)
                pe.wait_ge(ypool_ready, 2 * l + 1)
                project([0], 1)
                for t in range(TT):
                    pe.wait_ge(h_ready, HEADS * (TT * l + t + 1))
                    for h in range(HEADS):
                        last = tr(bank[PV_BANKS[t]][:, h * P:(h + 1) * P], h_norm[t][:, h * DH:(h + 1) * DH], ident)
                    last.then_inc(ht_mm, 1)
                pe.wait_ge(ylo_ready, 4 * l + 2)
                arrived(mixer_unit(l, "w", 1))
                project([1], 0)
                project([1], 1)
                arrived(mixer_unit(l, "w", 3))
                for t in range(TT):
                    pe.wait_ge(ylo_ready, 4 * l + 3 + t)
                    project([2, 3], t)

            def dense():
                def gate_up(b):
                    n = dense_chunks(b)
                    whole = b == DENSE_BLOCKS - 1
                    for kind in "gu":
                        cols_ = slice(0, T) if kind == "g" else slice(T, 2 * T)
                        for half in range(1 if whole else 2):
                            unit = dense_unit(kind, b, half)
                            arrived(unit)
                            hi, lo = parts_of(unit, n * P)
                            if unit == dense_unit("g", 0, 1):
                                pe.wait_ge(xlo_ready, 2 * TT * 2)
                            ks = range(DK) if whole else range(4 * half, 4 * half + 4)
                            for j in range(n):
                                c = 4 * b + j
                                if kind == "g" and half == 0 and c >= 4:
                                    pe.wait_ge(dh_ready, c - 3)
                                if unit == DENSE_UNIT0 and j == 0:
                                    first_product(bank[2][:, cols_], hi[:, :, 0:P], lo[:, :, 0:P], 1)
                                    continue
                                for kk, k in enumerate(ks):
                                    w = (slice(None), kk, slice(j * P, (j + 1) * P))
                                    last = product(bank[(2, 3, 6, 7)[c % 4]][:, cols_], (hi[w], lo[w]), x_parts(k),
                                                   k == 0, k == DK - 1)
                                if j == n - 1:
                                    last.then_inc(unit_done, 1)
                                elif kind == "u" and (whole or half == 1):
                                    last.then_inc(chunk_done, 1)

                def down(pieces):
                    b = pieces[-1][0]
                    pe.wait_ge(dlo_ready, 4 * b + dense_chunks(b))
                    arrived(dense_unit("d", *pieces[-1]))
                    for t in range(TT):
                        for n in range(2):
                            for b, half in pieces:
                                w = parts_of(dense_unit("d", b, half), D)
                                for jj in range(2):
                                    j = 2 * half + jj
                                    y = (slice(None), b % 2, j, slice(t * P, (t + 1) * P))
                                    r = (slice(None), jj, slice(n * HALF, (n + 1) * HALF))
                                    last = product(bank[SUM_BANKS[t][n]][:, :], (dh_hi[y], dh_lo[y]),
                                                   (w[0][r], w[1][r]), b == 0 and j == 0,
                                                   b == DENSE_BLOCKS - 1 and jj == 1)
                                if (t, n) == (TT - 1, 1):
                                    last.then_inc(unit_done, 1)
                                elif b == DENSE_BLOCKS - 1:
                                    last.then_inc(chunk_done, 1)

                for b in range(DENSE_BLOCKS):
                    gate_up(b)
                    if b:
                        down([(b - 1, 0)])
                        if b < DENSE_BLOCKS - 1:
                            down([(b - 1, 1)])
                down([(DENSE_BLOCKS - 2, 1), (DENSE_BLOCKS - 1, 0)])

            pe.wait_ge(ident_in, 16)
            turn(0)
            mixer(0)
            turn(1)
            dense()
            turn(2)
            mixer(1)
            pe.wait_ge(router_in, 32)
            turn(3, [0])
            logits(0, range(0, 4))
            turn(3, [1])
            logits(0, range(4, DK))
            logits(1, range(DK)).then_inc(logit_mm, 1)
            pe.wait_ge(chosen_ready, 1)
            mm(bank[0][:, 2 * E:3 * E], tri, chosen[:, 0, :], start=True, stop=True)
            mm(bank[0][:, 3 * E:4 * E], ones, chosen[:, 0, :], start=True, stop=False)
            mm(bank[0][:, 3 * E:4 * E], tri, chosen[:, 1, :], start=False, stop=True).then_inc(pos_mm, 1)

            def gather(i, n, psum):
                if n == 0:
                    pe.wait_ge(pick_ready, 2 * i + 2)
                for k in range(4 * n, 4 * n + 4):
                    for t in range(TT):
                        last = mm(psum[:, (k % 4) * CAP:(k % 4 + 1) * CAP],
                                  tokens[:, t, k * P:(k + 1) * P], pick[:, t, :], start=t == 0, stop=t == TT - 1)
                last.then_inc(gather_mm, 1)

            def scatter(i, q, psum=bank[4]):
                t, n = divmod(q, 2)
                if q == 0:
                    pe.wait_ge(ysb_ready, 2 * i + 2)
                    pe.wait_ge(scat_ready, i + 1)
                elif psum is bank[4]:
                    pe.wait_ge(acc_done, 4 * i + q)
                mm(psum[:, :], scat[0:CAP, t * P:(t + 1) * P], y_sb[0:CAP, n * HALF:(n + 1) * HALF],
                   start=True, stop=True).then_inc(scat_mm, 1)

            def item(i, first=False):
                for u, (kind, b, half) in enumerate(ITEM_ORDER):
                    n = MOE_UNIT0 + u
                    if u < 2:
                        pe.wait_ge(xglo_ready, 2 * i + u + 1)
                    arrived(n, i)
                    w = parts_of(n, D if kind == "d" else FBLK)
                    if kind == "d":
                        if half == 0:
                            pe.wait_ge(elo_ready, i * EXP_BLOCKS + (b + 1))
                        if b == 0 and half == 0 and not first:
                            pe.wait_ge(ysb_ready, 2 * i)
                        if first and b == 0 and half == 0:
                            pe.wait_ge(flags_ready, 1)
                        for hw in range(2):
                            for jj in range(2):
                                j = 2 * half + jj
                                r = (slice(None), jj, slice(hw * HALF, (hw + 1) * HALF))
                                last = product(bank[hw][0:CAP, :], (eh_hi[:, b % 2, j, :], eh_lo[:, b % 2, j, :]),
                                               (w[0][r], w[1][r]), b == 0 and j == 0,
                                               b == EXP_BLOCKS - 1 and j == 3)
                            if u == ITEM_UNITS - 1 and hw == 0:
                                last.then_inc(half_mm, 1)
                    else:
                        psum = bank[((2, 3), (6, 7))[b % 2][kind == "u"]][0:CAP, :]
                        for kk in range(4):
                            k = 4 * half + kk
                            last = product(psum, (xg_hi[:, k, :], xg_lo[:, k, :]), (w[0][:, kk, :], w[1][:, kk, :]),
                                           k == 0, k == DK - 1)
                    last.then_inc(unit_done, 1)
                    if first and u == 1:
                        mm(bank[0][:, 4 * E:5 * E], ones, chosen[:, 0, :], start=True, stop=False)
                        mm(bank[0][:, 4 * E:5 * E], ones, chosen[:, 1, :], start=False, stop=True) \
                            .then_inc(count_mm, 1)
                    if u in STEP_TURN:
                        tb = STEP_TURN[u]
                        pe.wait_ge(eh_ready, i * EXP_BLOCKS + (tb + 1))
                        for j in range(4):
                            last = tr(bank[5][:, j * CAP:(j + 1) * CAP], eh[0:CAP, tb % 2, j * P:(j + 1) * P],
                                      ident[0:CAP, 0:CAP])
                        last.then_inc(eturn_mm, 1)
                    if u in STEP_SCATTER and not first:
                        scatter(i - 1, STEP_SCATTER[u])
                    if u == STEP_SLOTS:
                        if not first:
                            pe.wait_ge(acc_done, 4 * i)
                        pe.wait_ge(pickc_ready, 2 * i + 2)
                        for t in range(TT):
                            last = tr(bank[4][0:CAP, t * P:(t + 1) * P], pickc[:, t, :], ident)
                        last.then_inc(st_mm, 1)
                    if u in STEP_GATHER:
                        if STEP_GATHER[u] == 0:
                            pe.wait_ge(scat_ready, i + 1)
                        gather(i + 1, STEP_GATHER[u], GATHER_BANKS[STEP_GATHER[u]])

            pe.wait_ge(tokens_ready, TT * 3)
            gather(0, 0, bank[4])
            gather(0, 1, bank[5])
            item(0, first=True)
            with pe.Fori(1, E) as i:
                item(i)
            pe.wait_ge(table_ready, 1)
            n_over = pe.value_load(over_int[0:1, MAX_OVER:MAX_OVER + 1], min_val=0, max_val=MAX_OVER)
            with pe.If(0 < n_over):
                with pe.Fori(0, MAX_OVER) as j:
                    with pe.If(j < n_over):
                        item(j + E)
            last_item = n_over + (E - 1)
            pe.wait_ge(xglo_ready, 2 * last_item + 4)
            for q in range(4):
                scatter(last_item, q, bank[TAIL_BANKS[q]])


def constant_table():
    c = np.zeros((P, C_END), np.float32)
    c[:, C_ID:C_ID + P] = np.eye(P)
    c[:, C_TRI:C_TRI + P] = np.triu(np.ones((P, P)), 1)
    c[:, C_ONES:C_ONES + T] = 1.0
    c[:, C_IOTA:C_IOTA + P] = np.arange(P)
    c[:, C_LT:C_LT + E * E] = np.tril(np.ones((E, E)), -1).reshape(-1)
    for g in range(GROUPS):
        c[:, C_INV + 16 * g:C_INV + 16 * g + 16] = 1.0 / np.minimum(np.arange(16) + 1, 2 << g)
    c[:, C_CE:C_CE + 2 * E] = np.tile(np.arange(E), 2)
    c[:, C_CT:C_CT + 2 * E] = np.repeat([CAP, 2 * CAP], E)
    for h in range(HEADS):
        c[h, C_SEL + h * P:C_SEL + (h + 1) * P] = 1.0
    return c


_INS = ["x", "w_in", "b_gates", "conv_w", "conv_b", "pool_w", "pool_scale", "mlstm_g", "w_out", "ln1_g", "ln1_b",
        "ln2_g", "ln2_b", "wg_dense", "wu_dense", "wd_dense", "w_router", "b_router", "wg_exp", "wu_exp", "wd_exp"]


def kernel(**inputs):
    import concourse.bacc as bacc
    from concourse.bass_utils import run_bass_kernel_spmd

    nc = bacc.Bacc("TRN2", target_bir_lowering=False, num_devices=1)
    arrays, args = {}, []
    for name in _INS:
        a = np.ascontiguousarray(inputs[name])
        arrays[f"in_{name}"] = a
        args.append(nc.dram_tensor(f"in_{name}", a.shape, mybir.dt.from_np(a.dtype), kind="ExternalInput").ap())
    c = constant_table()
    arrays["consts"] = c
    args.append(nc.dram_tensor("consts", c.shape, F32, kind="ExternalInput").ap())
    out = nc.dram_tensor("out", (1, T, D), F32, kind="ExternalOutput").ap()
    build(nc, *args, out)
    r = run_bass_kernel_spmd(nc, [arrays], core_ids=[0])
    return r.results[0]["out"]
```
